# Optimizing a Trainium2 kernel written in Bass

```python
import jax, jax.numpy as jnp
from jax import lax
import numpy as np
import jax
import jax.numpy as jnp

D_MODEL = 1024
BATCH = 1
SEQ = 512
DEPTH = 2

MLA_HEADS = 8
MLA_NOPE = 64
MLA_ROPE = 32
MLA_V = 64
MLA_Q_RANK = 768
MLA_KV_RANK = 256
DSA_HEADS = 4
DSA_DIM = 64
IDX_HEADS = 8
IDX_DIM = 32
DSA_TOPK_MAX = 256
RET_HEADS = 4
RET_DK = 64
RET_DV = 64
RET_CHUNK = 128
D_FF = 4 * D_MODEL
ROPE_THETA = 10000.0
EPS = 1e-6
Q_BLOCK = 128

MIX_WIDTH = MLA_HEADS * MLA_V + DSA_HEADS * DSA_DIM + RET_HEADS * RET_DV
MLA_COLS = (MLA_Q_RANK, MLA_KV_RANK, MLA_ROPE)
DSA_COLS = (DSA_HEADS * DSA_DIM, DSA_DIM, DSA_DIM, IDX_HEADS * IDX_DIM, IDX_DIM, IDX_HEADS)
RET_COLS = (RET_HEADS * RET_DK, RET_HEADS * RET_DK, RET_HEADS * RET_DV, RET_HEADS * RET_DV)
SPLITS = MLA_COLS + DSA_COLS + RET_COLS
IN_WIDTH = sum(SPLITS)


def rmsnorm(x, g):
    xf = x.astype(jnp.float32)
    y = xf * lax.rsqrt(jnp.mean(xf * xf, axis=-1, keepdims=True) + EPS)
    return (y * g.astype(jnp.float32)).astype(x.dtype)

def rope_tables(seq, dim):
    pos = jnp.arange(seq, dtype=jnp.float32)
    inv = ROPE_THETA ** (-jnp.arange(0, dim, 2, dtype=jnp.float32) / dim)
    ang = pos[:, None] * inv[None, :]
    return jnp.cos(ang), jnp.sin(ang)

def apply_rope(x, cos, sin):
    d2 = x.shape[-1] // 2
    x1, x2 = x[..., :d2], x[..., d2:]
    c = cos[:, None, :].astype(x.dtype)
    s = sin[:, None, :].astype(x.dtype)
    return jnp.concatenate([x1 * c - x2 * s, x1 * s + x2 * c], axis=-1)

def to_blocks(t):
    b, s = t.shape[0], t.shape[1]
    return t.reshape((b, s // Q_BLOCK, Q_BLOCK) + t.shape[2:]).swapaxes(0, 1)

def from_blocks(t):
    t = t.swapaxes(0, 1)
    return t.reshape(t.shape[0], t.shape[1] * t.shape[2], -1)

def mla_attention(q_nope, q_rope, k_nope, k_rope, v):
    S = q_nope.shape[1]
    nb = S // Q_BLOCK
    scale = (MLA_NOPE + MLA_ROPE) ** -0.5
    key_pos = jnp.arange(S)
    neg = jnp.finfo(jnp.float32).min

    def block(args):
        qn, qr, start = args
        s = jnp.einsum('bqhd,bkhd->bhqk', qn, k_nope) + jnp.einsum('bqhd,bkd->bhqk', qr, k_rope)
        s = s.astype(jnp.float32) * scale
        qpos = start + jnp.arange(Q_BLOCK)
        causal = key_pos[None, :] <= qpos[:, None]
        p = jax.nn.softmax(jnp.where(causal, s, neg), axis=-1).astype(v.dtype)
        return jnp.einsum('bhqk,bkhd->bqhd', p, v)

    starts = jnp.arange(nb, dtype=jnp.int32) * Q_BLOCK
    out = lax.map(block, (to_blocks(q_nope), to_blocks(q_rope), starts))
    return from_blocks(out)

def dsa_attention(q, k, v, q_idx, k_idx, w_idx, topk):
    S = q.shape[1]
    nb = S // Q_BLOCK
    scale = DSA_DIM ** -0.5
    key_pos = jnp.arange(S)
    neg = jnp.finfo(jnp.float32).min
    gather = jax.vmap(lambda table, idx: table[idx])

    def block(args):
        qb, qib, wb, start = args
        qpos = start + jnp.arange(Q_BLOCK)
        causal = key_pos[None, :] <= qpos[:, None]
        rel = jax.nn.relu(jnp.einsum('bqhd,bkd->bqhk', qib, k_idx))
        score = jnp.einsum('bqh,bqhk->bqk', wb, rel).astype(jnp.float32)
        score = jnp.where(causal[None], score, -jnp.inf)
        _, sel = lax.top_k(score, topk)
        valid = sel <= qpos[None, :, None]
        k_sel = gather(k, sel)
        v_sel = gather(v, sel)
        s = jnp.einsum('bqhd,bqjd->bhqj', qb, k_sel).astype(jnp.float32) * scale
        p = jax.nn.softmax(jnp.where(valid[:, None], s, neg), axis=-1).astype(v.dtype)
        return jnp.einsum('bhqj,bqjd->bqhd', p, v_sel)

    starts = jnp.arange(nb, dtype=jnp.int32) * Q_BLOCK
    out = lax.map(block, (to_blocks(q), to_blocks(q_idx), to_blocks(w_idx), starts))
    return from_blocks(out)

def retention(q, k, v, log_gamma):
    B, S, H, dk = q.shape
    dv = v.shape[-1]
    C = RET_CHUNK
    n = S // C
    qc = q.astype(jnp.float32).reshape(B, n, C, H, dk)
    kc = k.astype(jnp.float32).reshape(B, n, C, H, dk)
    vc = v.astype(jnp.float32).reshape(B, n, C, H, dv)
    pos = jnp.arange(C, dtype=jnp.float32)
    rel = pos[:, None] - pos[None, :]
    decay = jnp.where(rel[None] >= 0, jnp.exp(jnp.maximum(rel, 0.0)[None] * log_gamma[:, None, None]), 0.0)
    inner = jnp.einsum('bnqhd,bnchd->bnhqc', qc, kc) * decay[None, None]
    inner_out = jnp.einsum('bnhqc,bnche->bnqhe', inner, vc)
    zeta = jnp.exp((C - 1.0 - pos)[None, :] * log_gamma[:, None])
    chunk_state = jnp.einsum('bnchd,hc,bnche->bnhde', kc, zeta, vc)
    chunk_decay = jnp.exp(C * log_gamma)[None, :, None, None]

    def step(R, s_i):
        return R * chunk_decay + s_i, R

    R0 = jnp.zeros((B, H, dk, dv), jnp.float32)
    _, R_prev = lax.scan(step, R0, chunk_state.swapaxes(0, 1))
    R_prev = R_prev.swapaxes(0, 1)
    xi = jnp.exp((pos + 1.0)[None, :] * log_gamma[:, None])
    cross = jnp.einsum('bnqhd,bnhde,hq->bnqhe', qc, R_prev, xi)
    return (inner_out + cross).reshape(B, S, H, dv)

def head_groupnorm(x, g):
    mu = jnp.mean(x, axis=-1, keepdims=True)
    xc = x - mu
    var = jnp.mean(xc * xc, axis=-1, keepdims=True)
    return xc * lax.rsqrt(var + EPS) * g

def first_inputs(seed: int = 0) -> dict:
    key = jax.random.key(seed)
    ks = jax.random.split(key, 16)

    def nrm(k, shape, scale):
        return jax.random.normal(k, shape, jnp.float32) * scale

    def gain(k, shape):
        return 1.0 + 0.05 * jax.random.normal(k, shape, jnp.float32)

    return {
        'x': nrm(ks[0], (BATCH, SEQ, D_MODEL), 1.0),
        'g_mix': gain(ks[1], (DEPTH, D_MODEL)),
        'w_in': nrm(ks[2], (DEPTH, D_MODEL, IN_WIDTH), D_MODEL ** -0.5),
        'g_q': gain(ks[3], (DEPTH, MLA_Q_RANK)),
        'w_uq': nrm(ks[4], (DEPTH, MLA_Q_RANK, MLA_HEADS * (MLA_NOPE + MLA_ROPE)), MLA_Q_RANK ** -0.5),
        'g_kv': gain(ks[5], (DEPTH, MLA_KV_RANK)),
        'w_ukv': nrm(ks[6], (DEPTH, MLA_KV_RANK, MLA_HEADS * (MLA_NOPE + MLA_V)), MLA_KV_RANK ** -0.5),
        'g_ret': gain(ks[7], (DEPTH, RET_HEADS * RET_DV)),
        'w_out': nrm(ks[8], (DEPTH, MIX_WIDTH, D_MODEL), MIX_WIDTH ** -0.5),
        'g_mlp': gain(ks[9], (DEPTH, D_MODEL)),
        'w_ff1': nrm(ks[10], (DEPTH, D_MODEL, D_FF), D_MODEL ** -0.5),
        'w_ff2': nrm(ks[11], (DEPTH, D_FF, D_MODEL), D_FF ** -0.5),
        'g_final': gain(ks[12], (D_MODEL,)),
    }

def first_block(x, g_mix, w_in, g_q, w_uq, g_kv, w_ukv, g_ret, w_out, g_mlp, w_ff1, w_ff2, g_final):
    B, S, _ = x.shape
    topk = min(DSA_TOPK_MAX, S // 4)
    cos_r, sin_r = rope_tables(S, MLA_ROPE)
    cos_a, sin_a = rope_tables(S, DSA_DIM)
    cos_i, sin_i = rope_tables(S, IDX_DIM)
    cos_t, sin_t = rope_tables(S, RET_DK)
    log_gamma = jnp.log1p(-jnp.exp2(-5.0 - jnp.arange(RET_HEADS, dtype=jnp.float32)))
    split_at = np.cumsum(SPLITS)[:-1].tolist()
    idx_scale = (IDX_HEADS ** -0.5) * (IDX_DIM ** -0.5)

    for l in range(DEPTH):
        h = rmsnorm(x, g_mix[l])
        (cq, ckv, kr, aq, ak, av, qi, ki, wi, rq, rk, rv, rg) = jnp.split(h @ w_in[l], split_at, axis=-1)

        q = (rmsnorm(cq, g_q[l]) @ w_uq[l]).reshape(B, S, MLA_HEADS, MLA_NOPE + MLA_ROPE)
        q_nope = q[..., :MLA_NOPE]
        q_rope = apply_rope(q[..., MLA_NOPE:], cos_r, sin_r)
        kv = (rmsnorm(ckv, g_kv[l]) @ w_ukv[l]).reshape(B, S, MLA_HEADS, MLA_NOPE + MLA_V)
        k_nope, v_mla = kv[..., :MLA_NOPE], kv[..., MLA_NOPE:]
        k_rope = apply_rope(kr[:, :, None, :], cos_r, sin_r)[:, :, 0]
        o_a = mla_attention(q_nope, q_rope, k_nope, k_rope, v_mla)

        q_b = apply_rope(aq.reshape(B, S, DSA_HEADS, DSA_DIM), cos_a, sin_a)
        k_b = apply_rope(ak[:, :, None, :], cos_a, sin_a)[:, :, 0]
        q_i = apply_rope(qi.reshape(B, S, IDX_HEADS, IDX_DIM), cos_i, sin_i)
        k_i = apply_rope(ki[:, :, None, :], cos_i, sin_i)[:, :, 0]
        o_b = dsa_attention(q_b, k_b, av, q_i, k_i, wi * idx_scale, topk)

        q_c = apply_rope(rq.reshape(B, S, RET_HEADS, RET_DK), cos_t, sin_t)
        k_c = apply_rope(rk.reshape(B, S, RET_HEADS, RET_DK), cos_t, sin_t) * (RET_DK ** -0.5)
        ret = retention(q_c, k_c, rv.reshape(B, S, RET_HEADS, RET_DV), log_gamma)
        ret = head_groupnorm(ret, g_ret[l].reshape(RET_HEADS, RET_DV).astype(jnp.float32))
        o_c = (jax.nn.silu(rg.astype(jnp.float32)) * ret.reshape(B, S, RET_HEADS * RET_DV)).astype(x.dtype)

        x = x + jnp.concatenate([o_a, o_b, o_c], axis=-1) @ w_out[l]

        hf = rmsnorm(x, g_mlp[l])
        x = x + jnp.square(jax.nn.relu(hf @ w_ff1[l])) @ w_ff2[l]

    return rmsnorm(x, g_final)


HEAD_DIM = 64
N_GDN = 6
N_NSA = 6
N_NSA_KV = 2
NSA_REP = N_NSA // N_NSA_KV
N_SB = 4
D_GDN = N_GDN * HEAD_DIM
D_NSA = N_NSA * HEAD_DIM
D_NSA_KV = N_NSA_KV * HEAD_DIM
D_SB = N_SB * HEAD_DIM
D_MIX = D_GDN + D_NSA + D_SB
GDN_CONV = 4
GDN_CHUNK = 64
CMP_LEN = 32
CMP_STRIDE = 16
CMP_HIDDEN = 128
SEL_BLOCK = 64
SEL_TOPK = 16
WINDOW = 512
D_FF_2 = 2816
FFN_CONV = 3
D_PLE = 256
NEG = -1e30
FORCE_SCORE = 1e4
SPLIT_SIZES = (D_GDN, D_GDN, D_GDN, D_GDN, N_GDN, N_GDN,
               D_NSA, D_NSA_KV, D_NSA_KV, D_NSA_KV, D_NSA_KV, D_NSA_KV, D_NSA_KV, 3 * N_NSA,
               D_SB, D_SB, D_SB)
SPLIT_POINTS = tuple(int(c) for c in np.cumsum(SPLIT_SIZES)[:-1])
N_IN = int(sum(SPLIT_SIZES))


def rmsnorm_2(x, w):
    xf = x.astype(jnp.float32)
    y = xf * lax.rsqrt(jnp.mean(xf * xf, axis=-1, keepdims=True) + EPS)
    return (y * w.astype(jnp.float32)).astype(x.dtype)

def head_rmsnorm(x, w):
    b, t, c = x.shape
    return rmsnorm_2(x.reshape(b, t, c // HEAD_DIM, HEAD_DIM), w).reshape(b, t, c)

def l2norm(x):
    return x * lax.rsqrt(jnp.sum(x * x, axis=-1, keepdims=True) + EPS)

def causal_dwconv(x, w):
    k, c = w.shape
    return lax.conv_general_dilated(x, w[:, None, :].astype(x.dtype), window_strides=(1,),
                                    padding=[(k - 1, 0)], dimension_numbers=('NWC', 'WIO', 'NWC'),
                                    feature_group_count=c)

def rope(x, pos):
    half = x.shape[-1] // 2
    inv = ROPE_THETA ** (-jnp.arange(half, dtype=jnp.float32) / half)
    ang = pos.astype(jnp.float32)[..., None] * inv
    cos = jnp.cos(ang)[:, :, None, :]
    sin = jnp.sin(ang)[:, :, None, :]
    xf = x.astype(jnp.float32)
    x1, x2 = xf[..., :half], xf[..., half:]
    return jnp.concatenate([x1 * cos - x2 * sin, x2 * cos + x1 * sin], axis=-1).astype(x.dtype)

def masked_softmax(s, mask):
    s = jnp.where(mask, s, NEG)
    e = jnp.where(mask, jnp.exp(s - jnp.max(s, axis=-1, keepdims=True)), 0.0)
    return e / jnp.maximum(jnp.sum(e, axis=-1, keepdims=True), 1e-30)

def gated_deltanet(q, k, v, z, a, b_logit, conv_w, a_log, dt_bias, norm_w):
    bsz, t, _ = q.shape
    H, D, C = N_GDN, HEAD_DIM, GDN_CHUNK
    n = t // C
    f32 = jnp.float32
    qkv = jax.nn.silu(causal_dwconv(jnp.concatenate([q, k, v], axis=-1), conv_w))
    q, k, v = jnp.split(qkv, 3, axis=-1)
    to_chunks = lambda u_: u_.astype(f32).reshape(bsz, n, C, H, D).transpose(0, 3, 1, 2, 4)
    q = l2norm(to_chunks(q)) * D ** -0.5
    k = l2norm(to_chunks(k))
    v = to_chunks(v)
    beta = jax.nn.sigmoid(b_logit.astype(f32)).reshape(bsz, n, C, H).transpose(0, 3, 1, 2)
    g = -jnp.exp(a_log.astype(f32)) * jax.nn.softplus(a.astype(f32) + dt_bias.astype(f32))
    g = jnp.cumsum(g.reshape(bsz, n, C, H).transpose(0, 3, 1, 2), axis=-1)
    idx = jnp.arange(C)
    incl = idx[:, None] >= idx[None, :]
    strict = idx[:, None] > idx[None, :]
    decay = jnp.exp(jnp.where(incl, g[..., :, None] - g[..., None, :], -jnp.inf))
    k_beta = k * beta[..., None]
    lower = jnp.where(strict, jnp.einsum('bhncd,bhnsd->bhncs', k_beta, k) * decay, 0.0)
    rhs = jnp.concatenate([v * beta[..., None], k_beta * jnp.exp(g)[..., None]], axis=-1)
    sol = lax.linalg.triangular_solve(lower, rhs, left_side=True, lower=True, unit_diagonal=True)
    u, w = jnp.split(sol, 2, axis=-1)
    attn = jnp.einsum('bhncd,bhnsd->bhncs', q, k) * decay

    def step(state, xs):
        q_i, k_i, u_i, w_i, g_i, a_i = xs
        v_new = u_i - jnp.einsum('bhcd,bhde->bhce', w_i, state)
        o_i = (jnp.einsum('bhcd,bhde->bhce', q_i * jnp.exp(g_i)[..., None], state)
               + jnp.einsum('bhcs,bhse->bhce', a_i, v_new))
        g_last = g_i[..., -1:]
        state = (state * jnp.exp(g_last)[..., None]
                 + jnp.einsum('bhcd,bhce->bhde', k_i * jnp.exp(g_last - g_i)[..., None], v_new))
        return state, o_i

    xs = tuple(jnp.moveaxis(t_, 2, 0) for t_ in (q, k, u, w, g, attn))
    _, o = lax.scan(step, jnp.zeros((bsz, H, D, D), f32), xs)
    o = o.transpose(1, 0, 3, 2, 4).reshape(bsz, t, H, D)
    o = rmsnorm_2(o, norm_w) * jax.nn.silu(z.astype(f32).reshape(bsz, t, H, D))
    return o.reshape(bsz, t, D_GDN).astype(z.dtype)

def compress(kv, pe, w1, w2):
    b, t, g, d = kv.shape
    n_cmp = (t - CMP_LEN) // CMP_STRIDE + 1
    idx = jnp.arange(n_cmp)[:, None] * CMP_STRIDE + jnp.arange(CMP_LEN)[None, :]
    blocks = kv[:, idx] + pe[None, None, :, None, :]
    blocks = blocks.transpose(0, 1, 3, 2, 4).reshape(b, n_cmp, g, CMP_LEN * d)
    return jax.nn.silu(blocks @ w1) @ w2

def native_sparse_attention(q, k_cmp, v_cmp, k_slc, v_slc, k_win, v_win, gates, positions,
                            pe_k, pe_v, ck_w1, ck_w2, cv_w1, cv_w2):
    b, t, _ = q.shape
    G, R, D = N_NSA_KV, NSA_REP, HEAD_DIM
    scale = D ** -0.5
    f32 = jnp.float32
    q = rope(q.reshape(b, t, N_NSA, D), positions).reshape(b, t, G, R, D)
    kv = lambda z_: z_.reshape(b, t, G, D)
    kc = compress(rope(kv(k_cmp), positions), pe_k, ck_w1, ck_w2)
    vc = compress(kv(v_cmp), pe_v, cv_w1, cv_w2)
    n_cmp = kc.shape[1]
    n_sel = t // SEL_BLOCK
    top_k = min(SEL_TOPK, n_sel)
    ks_blk = rope(kv(k_slc), positions).reshape(b, n_sel, SEL_BLOCK, G, D).transpose(0, 3, 1, 2, 4)
    vs_blk = kv(v_slc).reshape(b, n_sel, SEL_BLOCK, G, D).transpose(0, 3, 1, 2, 4)
    pad = ((0, 0), (WINDOW, 0), (0, 0), (0, 0))
    kw_pad = jnp.pad(rope(kv(k_win), positions), pad)
    vw_pad = jnp.pad(kv(v_win), pad)
    c0 = jnp.arange(n_cmp) * CMP_STRIDE
    s0 = jnp.arange(n_sel) * SEL_BLOCK
    overlap = jnp.clip(jnp.minimum(c0[:, None] + CMP_LEN, s0[None, :] + SEL_BLOCK)
                       - jnp.maximum(c0[:, None], s0[None, :]), 0).astype(f32) / CMP_LEN
    cmp_end = c0 + CMP_LEN - 1
    b_idx = jnp.arange(b)[:, None, None, None]
    g_idx = jnp.arange(G)[None, :, None, None]
    blk = jnp.arange(n_sel)

    def block(args):
        qb, gb, q0 = args
        tq = q0 + jnp.arange(Q_BLOCK)
        s_c = jnp.einsum('bqgrd,bigd->bgrqi', qb, kc).astype(f32) * scale
        p_c = masked_softmax(s_c, cmp_end[None, :] <= tq[:, None])
        o_c = jnp.einsum('bgrqi,bigd->bqgrd', p_c.astype(vc.dtype), vc)
        imp = jnp.einsum('bgrqi,ij->bgqj', p_c, overlap)
        cur = tq // SEL_BLOCK
        forced = (blk[None, :] == 0) | (blk[None, :] == cur[:, None]) | (blk[None, :] == cur[:, None] - 1)
        visible = blk[None, :] * SEL_BLOCK <= tq[:, None]
        score = jnp.where(forced, FORCE_SCORE, jnp.where(visible, imp, -1.0))
        _, sel = lax.top_k(score, top_k)
        k_sel = ks_blk[b_idx, g_idx, sel].reshape(b, G, Q_BLOCK, top_k * SEL_BLOCK, D)
        v_sel = vs_blk[b_idx, g_idx, sel].reshape(b, G, Q_BLOCK, top_k * SEL_BLOCK, D)
        key_pos = (sel[..., None] * SEL_BLOCK + jnp.arange(SEL_BLOCK)).reshape(b, G, 1, Q_BLOCK, top_k * SEL_BLOCK)
        s_s = jnp.einsum('bqgrd,bgqnd->bgrqn', qb, k_sel).astype(f32) * scale
        p_s = masked_softmax(s_s, key_pos <= tq[:, None])
        o_s = jnp.einsum('bgrqn,bgqnd->bqgrd', p_s.astype(v_sel.dtype), v_sel)
        kw = lax.dynamic_slice_in_dim(kw_pad, q0, WINDOW + Q_BLOCK, axis=1)
        vw = lax.dynamic_slice_in_dim(vw_pad, q0, WINDOW + Q_BLOCK, axis=1)
        pos_w = q0 - WINDOW + jnp.arange(WINDOW + Q_BLOCK)
        diff = tq[:, None] - pos_w[None, :]
        m_w = (diff >= 0) & (diff < WINDOW) & (pos_w >= 0)[None, :]
        s_w = jnp.einsum('bqgrd,bngd->bgrqn', qb, kw).astype(f32) * scale
        p_w = masked_softmax(s_w, m_w)
        o_w = jnp.einsum('bgrqn,bngd->bqgrd', p_w.astype(vw.dtype), vw)
        gt = jax.nn.sigmoid(gb.astype(f32))[..., None]
        return (gt[:, :, 0] * o_c + gt[:, :, 1] * o_s + gt[:, :, 2] * o_w).astype(qb.dtype)

    nb = t // Q_BLOCK
    q_blocks = q.reshape(b, nb, Q_BLOCK, G, R, D).transpose(1, 0, 2, 3, 4, 5)
    g_blocks = gates.reshape(b, nb, Q_BLOCK, 3, G, R).transpose(1, 0, 2, 3, 4, 5)
    out = lax.map(block, (q_blocks, g_blocks, jnp.arange(nb) * Q_BLOCK))
    return out.transpose(1, 0, 2, 3, 4, 5).reshape(b, t, D_NSA)

def stick_breaking_attention(q, k, v):
    b, t, _ = q.shape
    H, D = N_SB, HEAD_DIM
    scale = D ** -0.5
    k = k.reshape(b, t, H, D)
    v = v.reshape(b, t, H, D)
    nb = t // Q_BLOCK
    q_blocks = q.reshape(b, nb, Q_BLOCK, H, D).transpose(1, 0, 2, 3, 4)
    key_pos = jnp.arange(t)

    def block(args):
        qb, q0 = args
        tq = q0 + jnp.arange(Q_BLOCK)
        strict = key_pos[None, :] < tq[:, None]
        z = jnp.einsum('bqhd,bkhd->bhqk', qb, k).astype(jnp.float32) * scale
        log_1m = jnp.where(strict, jax.nn.log_sigmoid(-z), 0.0)
        log_stick = lax.cumsum(log_1m, axis=3, reverse=True) - log_1m
        a = jnp.where(strict, jnp.exp(jax.nn.log_sigmoid(z) + log_stick), 0.0)
        return jnp.einsum('bhqk,bkhd->bqhd', a.astype(v.dtype), v)

    out = lax.map(block, (q_blocks, jnp.arange(nb) * Q_BLOCK))
    return out.transpose(1, 0, 2, 3, 4).reshape(b, t, D_SB)

def conv_ffn(x, w_up, conv_w, w_down):
    u = causal_dwconv(x @ w_up, conv_w)
    gate, up = jnp.split(u, 2, axis=-1)
    return (jax.nn.silu(gate) * up) @ w_down

def second_inputs(seed: int = 0) -> dict:
    key = jax.random.key(seed)
    keys = iter(jax.random.split(key, 40))
    f32 = jnp.float32

    def normal(shape, scale):
        return jax.random.normal(next(keys), shape, f32) * scale

    def gain(shape):
        return 1.0 + 0.01 * jax.random.normal(next(keys), shape, f32)

    x = normal((BATCH, SEQ, D_MODEL), 1.0)
    p = normal((DEPTH, BATCH, SEQ, D_PLE), 1.0)
    positions = (jax.random.randint(next(keys), (BATCH, 1), 0, 1024, jnp.int32)
                 + jnp.arange(SEQ, dtype=jnp.int32)[None, :])
    a_log = jnp.log(jax.random.uniform(next(keys), (DEPTH, N_GDN), f32, 1.0, 16.0))
    dt = jnp.exp(jax.random.uniform(next(keys), (DEPTH, N_GDN), f32, -6.907755, -2.302585))
    dt_bias = dt + jnp.log(-jnp.expm1(-dt))
    return {
        'x': x,
        'p': p,
        'positions': positions,
        'ln_mix': gain((DEPTH, D_MODEL)),
        'w_in': normal((DEPTH, D_MODEL, N_IN), D_MODEL ** -0.5),
        'gdn_conv': normal((DEPTH, GDN_CONV, 3 * D_GDN), GDN_CONV ** -0.5),
        'gdn_a_log': a_log,
        'gdn_dt_bias': dt_bias,
        'gdn_norm': gain((DEPTH, HEAD_DIM)),
        'nsa_pe_k': normal((DEPTH, CMP_LEN, HEAD_DIM), 0.1),
        'nsa_pe_v': normal((DEPTH, CMP_LEN, HEAD_DIM), 0.1),
        'nsa_cmp_k_w1': normal((DEPTH, CMP_LEN * HEAD_DIM, CMP_HIDDEN), (CMP_LEN * HEAD_DIM) ** -0.5),
        'nsa_cmp_k_w2': normal((DEPTH, CMP_HIDDEN, HEAD_DIM), CMP_HIDDEN ** -0.5),
        'nsa_cmp_v_w1': normal((DEPTH, CMP_LEN * HEAD_DIM, CMP_HIDDEN), (CMP_LEN * HEAD_DIM) ** -0.5),
        'nsa_cmp_v_w2': normal((DEPTH, CMP_HIDDEN, HEAD_DIM), CMP_HIDDEN ** -0.5),
        'nsa_norm': gain((DEPTH, HEAD_DIM)),
        'sb_norm': gain((DEPTH, HEAD_DIM)),
        'w_out': normal((DEPTH, D_MIX, D_MODEL), D_MIX ** -0.5),
        'ln_ffn': gain((DEPTH, D_MODEL)),
        'w_up': normal((DEPTH, D_MODEL, 2 * D_FF_2), D_MODEL ** -0.5),
        'ffn_conv': normal((DEPTH, FFN_CONV, 2 * D_FF_2), FFN_CONV ** -0.5),
        'w_down': normal((DEPTH, D_FF_2, D_MODEL), D_FF_2 ** -0.5),
        'ln_ple': gain((DEPTH, D_MODEL)),
        'w_ple_gate': normal((DEPTH, D_MODEL, D_MODEL), D_MODEL ** -0.5),
        'w_ple': normal((DEPTH, D_PLE, D_MODEL), D_PLE ** -0.5),
        'ple_norm': gain((DEPTH, D_MODEL)),
        'ln_final': gain((D_MODEL,)),
    }

def second_block(x, p, positions, ln_mix, w_in, gdn_conv, gdn_a_log, gdn_dt_bias, gdn_norm,
              nsa_pe_k, nsa_pe_v, nsa_cmp_k_w1, nsa_cmp_k_w2, nsa_cmp_v_w1, nsa_cmp_v_w2,
              nsa_norm, sb_norm, w_out, ln_ffn, w_up, ffn_conv, w_down,
              ln_ple, w_ple_gate, w_ple, ple_norm, ln_final):
    h = x
    for i in range(DEPTH):
        hn = rmsnorm_2(h, ln_mix[i])
        (g_q, g_k, g_v, g_z, g_a, g_b,
         n_q, n_kc, n_vc, n_ks, n_vs, n_kw, n_vw, n_gate,
         s_q, s_k, s_v) = jnp.split(hn @ w_in[i], SPLIT_POINTS, axis=-1)
        o_gdn = gated_deltanet(g_q, g_k, g_v, g_z, g_a, g_b, gdn_conv[i], gdn_a_log[i],
                               gdn_dt_bias[i], gdn_norm[i])
        o_nsa = native_sparse_attention(n_q, n_kc, n_vc, n_ks, n_vs, n_kw, n_vw, n_gate, positions,
                                        nsa_pe_k[i], nsa_pe_v[i], nsa_cmp_k_w1[i], nsa_cmp_k_w2[i],
                                        nsa_cmp_v_w1[i], nsa_cmp_v_w2[i])
        o_sb = stick_breaking_attention(s_q, s_k, s_v)
        mix = jnp.concatenate([o_gdn, head_rmsnorm(o_nsa, nsa_norm[i]), head_rmsnorm(o_sb, sb_norm[i])], axis=-1)
        h = h + mix @ w_out[i]
        h = h + conv_ffn(rmsnorm_2(h, ln_ffn[i]), w_up[i], ffn_conv[i], w_down[i])
        gate = jax.nn.sigmoid(rmsnorm_2(h, ln_ple[i]) @ w_ple_gate[i])
        h = h + gate * rmsnorm_2(p[i] @ w_ple[i], ple_norm[i])
    return rmsnorm_2(h, ln_final)


def setup_inputs(seed=0):
    out = dict(first_inputs(seed))
    for name, value in second_inputs(seed + 1).items():
        if name != "x":
            out[name + "_2"] = value
    return out


def reference(
    x, g_mix, w_in, g_q, w_uq, g_kv, w_ukv, g_ret, w_out, g_mlp, w_ff1, w_ff2, g_final, p_2,
    positions_2, ln_mix_2, w_in_2, gdn_conv_2, gdn_a_log_2, gdn_dt_bias_2, gdn_norm_2,
    nsa_pe_k_2, nsa_pe_v_2, nsa_cmp_k_w1_2, nsa_cmp_k_w2_2, nsa_cmp_v_w1_2, nsa_cmp_v_w2_2,
    nsa_norm_2, sb_norm_2, w_out_2, ln_ffn_2, w_up_2, ffn_conv_2, w_down_2, ln_ple_2,
    w_ple_gate_2, w_ple_2, ple_norm_2, ln_final_2,
):
    x = first_block(
        x, g_mix, w_in, g_q, w_uq, g_kv, w_ukv, g_ret, w_out, g_mlp, w_ff1, w_ff2, g_final,
    )
    return second_block(
        x, p_2, positions_2, ln_mix_2, w_in_2, gdn_conv_2, gdn_a_log_2, gdn_dt_bias_2,
        gdn_norm_2, nsa_pe_k_2, nsa_pe_v_2, nsa_cmp_k_w1_2, nsa_cmp_k_w2_2, nsa_cmp_v_w1_2,
        nsa_cmp_v_w2_2, nsa_norm_2, sb_norm_2, w_out_2, ln_ffn_2, w_up_2, ffn_conv_2, w_down_2,
        ln_ple_2, w_ple_gate_2, w_ple_2, ple_norm_2, ln_final_2,
    )


_drawn_inputs = setup_inputs


def setup_inputs(seed=0):
    import zlib

    import numpy as np

    out = dict(_drawn_inputs(seed))
    spreads = {}
    factors = {'g_q': 6.91,
     'ln_mix_2': 4.99,
     'gdn_norm_2': 25.567,
     'nsa_pe_k_2': 8.0,
     'nsa_norm_2': 64.0,
     'sb_norm_2': 64.0,
     'ln_ffn_2': 7.472,
     'ln_ple_2': 64.0,
     'ple_norm_2': 185.747,
     'ln_final_2': 169.628,
     'nsa_pe_v_2': 8.0}
    for name, (base, spread) in spreads.items():
        noise = np.random.default_rng([zlib.crc32(name.encode()), seed]).standard_normal(out[name].shape)
        drawn = base * np.exp(spread * noise) if base else spread * noise
        out[name] = jnp.asarray(drawn.astype(out[name].dtype))
    for name, factor in factors.items():
        out[name] = (out[name] * factor).astype(out[name].dtype)
    return out
```

```python
import math
from contextlib import ExitStack, contextmanager

import numpy as np
import concourse.bass as bass
from concourse import mybir
from concourse.alu_op_type import AluOpType as ALU

F32 = mybir.dt.float32
I32 = mybir.dt.int32
ACT = mybir.ActivationFunctionType
AX = mybir.AxisListType

P = 128
SEQ = 512
TT = SEQ // P
DM = 1024
DEPTH = 2
EPS = 1e-6
MASKED = -1e30
TAKEN = -3e38
BANK = 512

MLA_H, MLA_NOPE, MLA_ROPE, MLA_V = 8, 64, 32, 64
MLA_QK = MLA_NOPE + MLA_ROPE
Q_RANK, KV_RANK = 768, 256
DSA_H, DSA_D, IDX_H, IDX_D = 4, 64, 8, 32
TOPK = min(256, SEQ // 4)
RET_H, RET_D = 4, 64
D_FF = 4 * DM
A_CQ = 0
A_CKV = A_CQ + Q_RANK
A_KR = A_CKV + KV_RANK
A_AQ = A_KR + MLA_ROPE
A_AK = A_AQ + DSA_H * DSA_D
A_AV = A_AK + DSA_D
A_QI = A_AV + DSA_D
A_KI = A_QI + IDX_H * IDX_D
A_WI = A_KI + IDX_D
A_RQ = A_WI + IDX_H
A_RK = A_RQ + RET_H * RET_D
A_RV = A_RK + RET_H * RET_D
A_RG = A_RV + RET_H * RET_D
A_IN = A_RG + RET_H * RET_D

HD = 64
GDN_H, NSA_H, NSA_G, SB_H = 6, 6, 2, 4
NSA_R = NSA_H // NSA_G
GDN_QKV = 3 * GDN_H * HD
GDN_CONV = 4
CMP_LEN, CMP_STRIDE, CMP_HIDDEN = 32, 16, 128
N_CMP = (SEQ - CMP_LEN) // CMP_STRIDE + 1
D_FF2, FFN_CONV, D_PLE = 2816, 3, 256
B_NQ = 0
B_KC = B_NQ + NSA_H * HD
B_VC = B_KC + NSA_G * HD
B_KS = B_VC + NSA_G * HD
B_VS = B_KS + NSA_G * HD
B_KW = B_VS + NSA_G * HD
B_VW = B_KW + NSA_G * HD
B_GATE = B_VW + NSA_G * HD
B_SQ = B_GATE + 3 * NSA_H
B_SK = B_SQ + SB_H * HD
B_SV = B_SK + SB_H * HD
B_ATT = B_SV + SB_H * HD
B_Z = 0
B_A = B_Z + GDN_H * HD
B_B = B_A + GDN_H
B_ZAB = B_B + GDN_H

RING = 3
CHUNK = 8 * 512


def chunks_of(rows, cols, width=512, deep=8):
    tiles = rows // P
    return [(k, min(deep, tiles - k), n, min(width, cols - n))
            for n in range(0, cols, width) for k in range(0, tiles, deep)]


A_WEIGHTS = {
    "w_in": chunks_of(DM, A_IN), "w_uq": chunks_of(Q_RANK, MLA_H * MLA_QK),
    "w_ukv": chunks_of(KV_RANK, MLA_H * (MLA_NOPE + MLA_V)), "w_out": chunks_of(DM, DM),
    "w_ff1": chunks_of(DM, D_FF), "w_ff2": chunks_of(D_FF, DM),
}
B_WEIGHTS = {
    "w_in_att": chunks_of(DM, B_ATT),
    "cmp_k_w1": chunks_of(CMP_LEN * HD, CMP_HIDDEN, deep=16),
    "cmp_v_w1": chunks_of(CMP_LEN * HD, CMP_HIDDEN, deep=16),
    "w_in_conv": chunks_of(DM, GDN_QKV), "w_in_zab": chunks_of(DM, B_ZAB),
    "w_out": chunks_of(DM, DM), "w_up": chunks_of(DM, 2 * D_FF2), "w_down": chunks_of(D_FF2, DM),
    "w_ple_gate": chunks_of(DM, DM), "w_ple": chunks_of(D_PLE, DM),
}


class Steps:

    def __init__(self, engine, sem):
        self.engine, self.sem, self.count = engine, sem, 0

    def __call__(self, instruction):
        self.count += 1
        instruction.then_inc(self.sem, 1)
        self.engine.wait_ge(self.sem, self.count)


class Core:

    def __init__(self, nc, ctx):
        self.nc, self.ctx, self.old = nc, ctx, []
        self.n_stage = 0
        self.ps = ctx.enter_context(nc.psum_tensor("ps", [P, 8, BANK], F32))
        self.x = self.sb("x", [P, TT, DM])
        self.hT = self.sb("hT", [P, 8, SEQ])
        self.ring = self.sb("ring", [P, RING, CHUNK])
        self.slot_full = [ctx.enter_context(nc.semaphore(f"slot{i}_full")) for i in range(RING)]
        self.chunk_used = ctx.enter_context(nc.semaphore("chunk_used"))
        self.queue, self.loaded, self.used = [], 0, 0

    def sb(self, name, shape, dt=F32):
        return self.ctx.enter_context(self.nc.sbuf_tensor(name, shape, dt))

    @contextmanager
    def stage(self, name, *signals):
        nc = self.nc
        self.n_stage += 1
        sems = [nc.alloc_semaphore(name=f"{name}{self.n_stage}_{s}") for s in signals]
        with nc.Block() as block:
            yield (block, *sems)
        for s in sems:
            nc.sync.sem_clear(s)
        for s in self.old:
            nc.release_semaphore(s)
        self.old = sems

    def banks(self, t):
        return self.ps[:, t, :]

    def start_layer(self, weights, drams, prefix, l):
        self.queue = [(drams[prefix + n], c) for n, cs in weights.items() for c in cs]
        self.offsets, at, last = [], 0, None
        for d, (k, kt, n, w) in self.queue:
            at = at if d is last else 0
            self.offsets.append(at)
            at, last = at + kt * w, d
        self.loaded = self.used = 0
        self.l = l

    def load_up_to(self, sp, end):
        for i in range(self.loaded, min(end, len(self.queue))):
            if i >= RING:
                sp.wait_ge(self.chunk_used, i - RING + 1)
            d, (_, kt, _, w) = self.queue[i]
            o = self.offsets[i]
            src = d[bass.ds(self.l, 1), :, o:o + kt * w].rearrange("a p n -> p (a n)")
            sp.dma_start(self.ring[:, i % RING, 0:kt * w], src).then_inc(self.slot_full[i % RING], 16)
        self.loaded = max(self.loaded, min(end, len(self.queue)))

    def arrived(self, pe):
        i = self.used
        self.used += 1
        pe.wait_ge(self.slot_full[i % RING], 16 * (i // RING + 1))
        _, (_, kt, _, w) = self.queue[i]
        return self.ring[:, i % RING, 0:kt * w].rearrange("p (k n) -> p k n", n=w)

    def end_layer(self):
        nc = self.nc
        assert self.used == self.loaded == len(self.queue)
        nc.all_engine_barrier()
        for s in self.slot_full + [self.chunk_used]:
            nc.sync.sem_clear(s)
        nc.all_engine_barrier()


def norm_transpose(c, name, src, groups, gain, half, load=0):
    nc = c.nc
    G = len(groups)
    with ExitStack() as ctx:
        sb = lambda n, s: ctx.enter_context(nc.sbuf_tensor(name + n, s, F32))
        xn, junk = sb("xn", [P, TT, DM]), sb("junk", [P, DM])
        ssq, rstd = sb("ssq", [P, TT, G]), sb("rstd", [P, TT, G])
        with c.stage(name, "squares", "mean", "rstd", "rows", "turned", "kept") as (
                block, squares, mean, rstd_ready, rows, turned, kept):
            if load:
                @block.sync
                def _(sp):
                    c.load_up_to(sp, load)

            @block.scalar
            def _(act):
                n = 0
                for t in range(TT):
                    for g, (a, w) in enumerate(groups):
                        if n:
                            act.wait_ge(squares, n)
                        nc.scalar.activation(junk[:, a:a + w], src[:, t, a:a + w], ACT.Square,
                                             accum_out=ssq[:, t, g:g + 1]).then_inc(squares, 1)
                        n += 1
                for k in range(1, 8, 2):
                    act.wait_ge(turned, k + 1)
                    nc.scalar.activation(c.hT[:, k, :], c.banks(k), ACT.Copy,
                                         scale=gain[:, k:k + 1]).then_inc(kept, 1)

            @block.gpsimd
            def _(pool):
                for t in range(TT):
                    pool.wait_ge(squares, G * (t + 1))
                    for g, (a, w) in enumerate(groups):
                        nc.gpsimd.tensor_scalar(ssq[:, t, g:g + 1], ssq[:, t, g:g + 1], 1.0 / w, EPS,
                                                ALU.mult, ALU.add).then_inc(mean, 1)
                    pool.wait_ge(mean, G * (t + 1))
                    nc.gpsimd.tensor_tensor(rstd[:, t, :], ssq[:, t, :], half[:, 0:G],
                                            ALU.pow).then_inc(rstd_ready, 1)

            @block.vector
            def _(dve):
                for t in range(TT):
                    dve.wait_ge(rstd_ready, t + 1)
                    for g, (a, w) in enumerate(groups):
                        nc.vector.tensor_scalar(xn[:, t, a:a + w], src[:, t, a:a + w],
                                                rstd[:, t, g:g + 1], None, ALU.mult).then_inc(rows, 1)
                for k in range(0, 8, 2):
                    dve.wait_ge(turned, k + 1)
                    nc.vector.tensor_scalar(c.hT[:, k, :], c.banks(k), gain[:, k:k + 1], None,
                                            ALU.mult).then_inc(kept, 1)

            @block.tensor
            def _(pe):
                for t in range(TT):
                    pe.wait_ge(rows, G * (t + 1))
                    for k in range(8):
                        ins = nc.tensor.transpose(c.ps[:, k, t * P:(t + 1) * P],
                                                  xn[:, t, k * P:(k + 1) * P], c.ident)
                        if t == TT - 1:
                            ins.then_inc(turned, 1)


def gemm_tokens(c, name, aT, k_tiles, n_chunks, out, add=None, also_dve=True):
    nc = c.nc
    first = c.used
    plan = [q[1] for q in c.queue[first:]]
    cols, at = [], 0
    for n in range(n_chunks):
        parts, done = [], 0
        while done < k_tiles:
            parts.append(plan[at])
            done += plan[at][1]
            at += 1
        cols.append(parts)
    end = first + at
    by_act = lambda t: add is None and (t % 2 == 0 or not also_dve)
    per_n = {True: sum(by_act(t) for t in range(TT)), False: sum(not by_act(t) for t in range(TT))}
    with c.stage(name, "filled", "act_kept", "dve_kept") as (block, filled, act_kept, dve_kept):
        @block.sync
        def _(sp):
            c.load_up_to(sp, end + RING)

        @block.tensor
        def _(pe):
            for n, parts in enumerate(cols):
                if n >= 2:
                    if per_n[True]:
                        pe.wait_ge(act_kept, per_n[True] * (n - 1))
                    if per_n[False]:
                        pe.wait_ge(dve_kept, per_n[False] * (n - 1))
                for (k0, kt, n0, w) in parts:
                    wt = c.arrived(pe)
                    for t in range(TT):
                        for k in range(kt):
                            ins = nc.tensor.matmul(c.ps[:, (n % 2) * TT + t, 0:w],
                                                   aT[:, k0 + k, t * P:(t + 1) * P], wt[:, k, :],
                                                   start=(k0 + k == 0), stop=(k0 + k == k_tiles - 1))
                        if t == TT - 1:
                            ins.then_inc(c.chunk_used, 1)
                        if k0 + kt == k_tiles:
                            if t < TT - 1:
                                ins.then_inc(filled, 1)

        def keep(engine, scalar):
            for n, parts in enumerate(cols):
                _, _, n0, w = parts[0]
                for t in range(TT):
                    if by_act(t) != scalar:
                        continue
                    if t == TT - 1:
                        engine.wait_ge(c.chunk_used, first + sum(len(p) for p in cols[:n + 1]))
                    else:
                        engine.wait_ge(filled, (TT - 1) * n + t + 1)
                    bank = c.ps[:, (n % 2) * TT + t, 0:w]
                    if scalar:
                        nc.scalar.copy(out(t, n0, w), bank).then_inc(act_kept, 1)
                    elif add is None:
                        nc.vector.tensor_copy(out(t, n0, w), bank).then_inc(dve_kept, 1)
                    else:
                        nc.vector.tensor_tensor(out(t, n0, w), bank, add(t, n0, w),
                                                ALU.add).then_inc(dve_kept, 1)

        if per_n[True]:
            @block.scalar
            def _(act):
                keep(act, True)

        if per_n[False]:
            @block.vector
            def _(dve):
                keep(dve, False)


def transpose_tiles(c, name, jobs):
    nc = c.nc

    def bank(i, dst):
        b = c.ps[0:dst.shape[0], i % 8, :]
        return b if len(dst.shape) == 2 else b.rearrange("p (t n) -> p t n", t=TT)

    with c.stage(name, "turned", "act_kept", "dve_kept") as (block, turned, act_kept, dve_kept):
        @block.tensor
        def _(pe):
            for i, (src, m, dst, scale) in enumerate(jobs):
                if i >= 8:
                    if i % 2:
                        pe.wait_ge(dve_kept, (i - 8) // 2 + 1)
                    else:
                        pe.wait_ge(act_kept, (i - 8) // 2 + 1)
                for t in range(TT):
                    ins = nc.tensor.transpose(c.ps[0:m, i % 8, t * P:(t + 1) * P], src(t), c.ident)
                ins.then_inc(turned, 1)

        @block.scalar
        def _(act):
            for i, (src, m, dst, scale) in enumerate(jobs):
                if i % 2 == 0:
                    act.wait_ge(turned, i + 1)
                    nc.scalar.activation(dst, bank(i, dst), ACT.Copy,
                                         scale=scale).then_inc(act_kept, 1)

        @block.vector
        def _(dve):
            for i, (src, m, dst, scale) in enumerate(jobs):
                if i % 2:
                    dve.wait_ge(turned, i + 1)
                    nc.vector.tensor_scalar(dst, bank(i, dst), scale, None,
                                            ALU.mult).then_inc(dve_kept, 1)


def relu_squared_gemm(c, name, uT):
    nc = c.nc
    first = c.used
    plan = c.queue[first:first + D_FF // 512]
    F = D_FF // P
    with ExitStack() as ctx:
        r = ctx.enter_context(nc.sbuf_tensor(name + "r", [P, 4, SEQ], F32))
        with c.stage(name, "filled", "relu_done", "squared") as (block, filled, relu_done, squared):
            @block.sync
            def _(sp):
                c.load_up_to(sp, first + len(plan) + RING)

            @block.tensor
            def _(pe):
                f = 0
                for _ in plan:
                    wt = c.arrived(pe)
                    for b in range(4):
                        if f >= 8:
                            pe.wait_ge(relu_done, f - 7)
                            pe.wait_ge(squared, f - 7)
                        for k in range(8):
                            ins = nc.tensor.matmul(c.banks(f % 8), wt[:, k, b * P:(b + 1) * P],
                                                   c.hT[:, k, :], start=(k == 0), stop=(k == 7))
                        f += 1
                        ins.then_inc(c.chunk_used if b == 3 else filled, 1)

            def wait_filled(engine, f):
                if f % 4 == 3:
                    engine.wait_ge(c.chunk_used, first + f // 4 + 1)
                else:
                    engine.wait_ge(filled, 3 * (f // 4) + f % 4 + 1)

            @block.scalar
            def _(act):
                for f in range(F):
                    wait_filled(act, f)
                    if f >= 4:
                        act.wait_ge(squared, f - 3)
                    nc.scalar.activation(r[:, f % 4, :], c.banks(f % 8), ACT.Relu).then_inc(relu_done, 1)

            @block.vector
            def _(dve):
                for f in range(F):
                    dve.wait_ge(relu_done, f + 1)
                    nc.vector.tensor_tensor(uT[:, f, :], c.banks(f % 8), r[:, f % 4, :],
                                            ALU.mult).then_inc(squared, 1)


def rope(eng, step, x, cos, sin, tmp, heads, half):
    shape = [P, TT, heads, half]
    x1, x2 = x[:, :, :, 0:half], x[:, :, :, half:2 * half]
    cb = cos.unsqueeze(2).broadcast_to(shape)
    sb = sin.unsqueeze(2).broadcast_to(shape)
    n = TT * heads * half
    t1 = tmp[:, 0:n].rearrange("p (t h d) -> p t h d", t=TT, h=heads)
    t2 = tmp[:, n:2 * n].rearrange("p (t h d) -> p t h d", t=TT, h=heads)
    eng.tensor_tensor(t1, x1, sb, ALU.mult)
    step(eng.tensor_tensor(t2, x2, sb, ALU.mult))
    eng.tensor_tensor(x1, x1, cb, ALU.mult)
    step(eng.tensor_tensor(x2, x2, cb, ALU.mult))
    eng.tensor_tensor(x1, x1, t2, ALU.subtract)
    step(eng.tensor_tensor(x2, x2, t1, ALU.add))


def softmax_attention(c, name, units):
    nc = c.nc
    U = len(units)
    with ExitStack() as ctx:
        sb = lambda n, s: ctx.enter_context(nc.sbuf_tensor(name + n, s, F32))
        p, pT = sb("p", [P, 2, SEQ]), sb("pT", [P, 2, SEQ])
        negmax, rsum, rinv = sb("negmax", [P, 8]), sb("rsum", [P, 8]), sb("rinv", [P, 8])
        tmp = sb("o", [P, 2, HD])
        with c.stage(name, "scores", "maxed", "probs", "turned", "probsT", "outs", "kept", "step") as (
                block, scores, maxed, probs, turned, probsT, outs, kept, step_sem):
            @block.tensor
            def _(pe):
                for i in range(U + 3):
                    if i < U:
                        qT, kT = units[i][0], units[i][1]
                        if i >= 4:
                            pe.wait_ge(probs, i - 3)
                        nc.tensor.matmul(c.ps[:, i % 4, 0:kT.shape[1]], qT, kT,
                                         start=True, stop=True).then_inc(scores, 1)
                    u = i - 2
                    if 0 <= u < U:
                        nk = units[u][1].shape[1]
                        pe.wait_ge(probs, u + 1)
                        if u >= 2:
                            pe.wait_ge(probsT, u - 1)
                        for j in range(nk // P):
                            ins = nc.tensor.transpose(c.ps[:, 4 + u % 2, j * P:(j + 1) * P],
                                                      p[:, u % 2, j * P:(j + 1) * P], c.ident)
                        ins.then_inc(turned, 1)
                    u = i - 3
                    if 0 <= u < U:
                        nb = units[u][1].shape[1] // P
                        pe.wait_ge(probsT, u + 1)
                        if u >= 2:
                            pe.wait_ge(kept, u - 1)
                        for j in range(nb):
                            v = units[u][2](j)
                            ins = nc.tensor.matmul(c.ps[:, 6 + u % 2, 0:v.shape[1]],
                                                   pT[:, u % 2, j * P:(j + 1) * P], v,
                                                   start=(j == 0), stop=(j == nb - 1))
                        ins.then_inc(outs, 1)

            @block.vector
            def _(dve):
                step = Steps(dve, step_sem)
                for i in range(U + 4):
                    if i < U:
                        mask, nk = units[i][3], units[i][1].shape[1]
                        dve.wait_ge(scores, i + 1)
                        nm = mask.shape[1]
                        s = c.ps[:, i % 4, nk - nm:nk]
                        step(nc.vector.tensor_tensor(s, s, mask, ALU.add))
                        nc.vector.tensor_reduce(negmax[:, i % 8:i % 8 + 1], c.ps[:, i % 4, 0:nk],
                                                AX.X, ALU.max, negate=True).then_inc(maxed, 1)
                    u = i - 4
                    if 0 <= u < U:
                        out, gate, add = units[u][4:7]
                        ri = rinv[:, u % 8:u % 8 + 1]
                        dve.wait_ge(outs, u + 1)
                        step(nc.vector.reciprocal(ri, rsum[:, u % 8:u % 8 + 1]))
                        o = c.ps[:, 6 + u % 2, 0:out.shape[1]]
                        if gate is None:
                            nc.vector.tensor_scalar(out, o, ri, None, ALU.mult).then_inc(kept, 1)
                        elif add:
                            step(nc.vector.tensor_scalar(tmp[:, u % 2, :], o, ri, gate, ALU.mult, ALU.mult))
                            nc.vector.tensor_tensor(out, out, tmp[:, u % 2, :], ALU.add).then_inc(kept, 1)
                        else:
                            nc.vector.tensor_scalar(out, o, ri, gate, ALU.mult, ALU.mult).then_inc(kept, 1)

            @block.scalar
            def _(act):
                for i in range(U + 3):
                    if i < U:
                        nk = units[i][1].shape[1]
                        act.wait_ge(maxed, i + 1)
                        if i >= 2:
                            act.wait_ge(turned, i - 1)
                        nc.scalar.activation(p[:, i % 2, 0:nk], c.ps[:, i % 4, 0:nk], ACT.Exp,
                                             bias=negmax[:, i % 8:i % 8 + 1],
                                             accum_out=rsum[:, i % 8:i % 8 + 1]).then_inc(probs, 1)
                    u = i - 1
                    if 0 <= u < U:
                        nk = units[u][1].shape[1]
                        act.wait_ge(turned, u + 1)
                        if u >= 2:
                            act.wait_ge(outs, u - 1)
                        nc.scalar.copy(pT[:, u % 2, 0:nk], c.ps[:, 4 + u % 2, 0:nk]).then_inc(probsT, 1)


def index_scores(c, name, qiT, kiT, weights, score):
    nc = c.nc
    units = [(t, h) for t in range(1, TT) for h in range(IDX_H)]
    with ExitStack() as ctx:
        rel = ctx.enter_context(nc.sbuf_tensor(name + "rel", [P, 3, SEQ], F32))
        with c.stage(name, "dots", "rectified", "summed") as (block, dots, rectified, summed):
            @block.tensor
            def _(pe):
                for u, (t, h) in enumerate(units):
                    b = 32 * (h % 4)
                    if u >= 8:
                        pe.wait_ge(rectified, u - 7)
                    nc.tensor.matmul(c.ps[:, u % 8, 0:(t + 1) * P],
                                     qiT[b:b + 32, h // 4, t * P:(t + 1) * P],
                                     kiT[b:b + 32, 0:(t + 1) * P], start=True, stop=True,
                                     ).then_inc(dots, 1)

            @block.scalar
            def _(act):
                for u, (t, h) in enumerate(units):
                    act.wait_ge(dots, u + 1)
                    if u >= 3:
                        act.wait_ge(summed, u - 2)
                    nc.scalar.activation(rel[:, u % 3, 0:(t + 1) * P], c.ps[:, u % 8, 0:(t + 1) * P],
                                         ACT.Relu).then_inc(rectified, 1)

            @block.vector
            def _(dve):
                for u, (t, h) in enumerate(units):
                    nk = (t + 1) * P
                    w = weights[:, t, h:h + 1]
                    dve.wait_ge(rectified, u + 1)
                    if h == 0:
                        nc.vector.tensor_scalar(score[:, t - 1, 0:nk], rel[:, u % 3, 0:nk], w, None,
                                                ALU.mult).then_inc(summed, 1)
                    else:
                        dve.wait_ge(summed, u)
                        nc.vector.scalar_tensor_tensor(out=score[:, t - 1, 0:nk], in0=rel[:, u % 3, 0:nk],
                                                       scalar=w, in1=score[:, t - 1, 0:nk],
                                                       op0=ALU.mult, op1=ALU.add).then_inc(summed, 1)
                dve.wait_ge(summed, len(units))
                for t in range(1, TT):
                    d = score[:, t - 1, t * P:(t + 1) * P]
                    nc.vector.tensor_tensor(d, d, c.causal, ALU.add).then_inc(summed, 1)
                dve.wait_ge(summed, len(units) + TT - 1)


def top_k_mask(nc, dve, step, score, best):
    for r in range(TOPK // 8):
        for t in range(1, TT):
            ins = nc.vector.max(best[:, t - 1, :], score[:, t - 1, 0:(t + 1) * P])
            if t == TT - 1:
                step(ins)
        for t in range(1, TT):
            s = score[:, t - 1, 0:(t + 1) * P]
            ins = nc.vector.match_replace(s, best[:, t - 1, :], s, TAKEN)
            if t == TT - 1:
                step(ins)
    for t in range(1, TT):
        s = score[:, t - 1, 0:(t + 1) * P]
        ins = nc.vector.tensor_scalar(s, s, TAKEN, MASKED, ALU.not_equal, ALU.mult)
    step(ins)


def retention(c, name, qT, kT, v, decay, out):
    nc = c.nc
    with ExitStack() as ctx:
        inner = ctx.enter_context(nc.sbuf_tensor(name + "inner", [P, 2, TT, SEQ], F32))
        with c.stage(name, "dots", "inners", "outs", "kept") as (block, dots, inners, outs, kept):
            @block.tensor
            def _(pe):
                for i in range(RET_H + 1):
                    if i < RET_H:
                        b, pair = HD * (i % 2), i // 2
                        for j in range(TT):
                            if i >= 1:
                                pe.wait_ge(inners, TT * (i - 1) + j + 1)
                            nc.tensor.matmul(c.ps[:, j, 0:SEQ - j * P],
                                             kT[b:b + HD, pair, j * P:(j + 1) * P],
                                             qT[b:b + HD, pair, j * P:SEQ],
                                             start=True, stop=True).then_inc(dots, 1)
                    h = i - 1
                    if h >= 0:
                        pe.wait_ge(inners, TT * (h + 1))
                        if h >= 2:
                            pe.wait_ge(kept, h - 1)
                        for t in range(TT):
                            for j in range(t + 1):
                                ins = nc.tensor.matmul(
                                    c.ps[:, 4 + h % 2, t * HD:(t + 1) * HD],
                                    inner[:, h % 2, j, (t - j) * P:(t - j + 1) * P],
                                    v[:, j, h * HD:(h + 1) * HD], start=(j == 0), stop=(j == t))
                        ins.then_inc(outs, 1)

            @block.vector
            def _(dve):
                for h in range(RET_H):
                    if h >= 2:
                        dve.wait_ge(outs, h - 1)
                    for j in range(TT):
                        dve.wait_ge(dots, TT * h + j + 1)
                        nc.vector.tensor_tensor(inner[:, h % 2, j, 0:SEQ - j * P],
                                                c.ps[:, j, 0:SEQ - j * P],
                                                decay[:, h, 0:SEQ - j * P], ALU.mult).then_inc(inners, 1)

            @block.scalar
            def _(act):
                for h in range(RET_H):
                    act.wait_ge(outs, h + 1)
                    nc.scalar.copy(out[:, :, h, :], c.ps[:, 4 + h % 2, 0:TT * HD].rearrange(
                        "p (t d) -> p t d", t=TT)).then_inc(kept, 1)


def head_norm(c, name, src, heads, gain, dst, half, center=False, gate=None, scratch=None):
    nc = c.nc
    shape = [P, TT, heads, HD]
    with ExitStack() as ctx:
        sb = lambda n, s: ctx.enter_context(nc.sbuf_tensor(name + n, s, F32))
        y, sq = scratch or (sb("y", shape)[:], sb("sq", shape)[:])
        mean, ssq = sb("mean", [P, TT, heads]), sb("ssq", [P, TT, heads])[:]
        with c.stage(name, "summed", "power", "rstd", "step", "gated") as (
                block, summed, power, rstd, step_sem, gated):
            @block.gpsimd
            def _(pool):
                pool.wait_ge(summed, 1)
                nc.gpsimd.tensor_scalar(ssq, ssq, 1.0 / HD, EPS, ALU.mult, ALU.add).then_inc(power, 1)
                pool.wait_ge(power, 1)
                nc.gpsimd.tensor_tensor(
                    ssq, ssq, half[:, 0:1].unsqueeze(2).broadcast_to([P, TT, heads]),
                    ALU.pow).then_inc(rstd, 1)

            if gate is not None:
                @block.scalar
                def _(act):
                    nc.scalar.activation(gate, gate, ACT.Silu).then_inc(gated, 1)

            @block.vector
            def _(dve):
                step = Steps(dve, step_sem)
                z = src
                if center:
                    step(nc.vector.tensor_reduce(mean[:], src, AX.X, ALU.add))
                    step(nc.vector.tensor_scalar(mean[:], mean[:], -1.0 / HD, None, ALU.mult))
                    step(nc.vector.tensor_tensor(y, src, mean[:].unsqueeze(3).broadcast_to(shape), ALU.add))
                    z = y
                step(nc.vector.tensor_tensor(sq, z, z, ALU.mult))
                nc.vector.tensor_reduce(ssq, sq, AX.X, ALU.add).then_inc(summed, 1)
                dve.wait_ge(summed, 1)
                for t in range(TT):
                    ins = nc.vector.tensor_tensor(sq[:, t], z[:, t], gain.broadcast_to([P, heads, HD]), ALU.mult)
                step(ins)
                if gate is not None:
                    dve.wait_ge(gated, 1)
                    step(nc.vector.tensor_tensor(sq, sq, gate, ALU.mult))
                dve.wait_ge(rstd, 1)
                nc.vector.tensor_tensor(dst, sq, ssq.unsqueeze(3).broadcast_to(shape), ALU.mult)


def rotation_tables(c, name, pos_i, inv, cos, sin):
    nc = c.nc
    two_pi = 2 * math.pi

    def short(v, bits):
        e = math.floor(math.log2(v)) + 1 - bits
        return math.floor(v / 2.0 ** e) * 2.0 ** e
    c1 = short(two_pi, 8)
    c2 = short(two_pi - c1, 8)
    c3 = short(two_pi - c1 - c2, 8)
    c4 = two_pi - c1 - c2 - c3
    MAGIC, LIM = 1.5 * 2 ** 23, 3.1415925
    n = TT * HD // 2
    with ExitStack() as ctx:
        sb = lambda m, s: ctx.enter_context(nc.sbuf_tensor(name + m, s, F32))
        pos, ang, k, wrap = sb("pos", [P, TT]), sb("ang", [P, TT, HD // 2]), sb("k", [P, TT, HD // 2]), sb("wrap", [P, TT, HD // 2])
        with c.stage(name, "step", "angles") as (block, step_sem, angles):
            @block.vector
            def _(dve):
                step = Steps(dve, step_sem)
                step(nc.vector.tensor_copy(pos[:], pos_i))
                shape = [P, TT, HD // 2]
                step(nc.vector.tensor_tensor(ang[:], pos[:].unsqueeze(2).broadcast_to(shape),
                                             inv.unsqueeze(1).broadcast_to(shape), ALU.mult))
                step(nc.vector.tensor_scalar(k[:], ang[:], 1 / two_pi, None, ALU.mult))
                step(nc.vector.tensor_scalar(k[:], k[:], MAGIC, None, ALU.add))
                step(nc.vector.tensor_scalar(k[:], k[:], MAGIC, None, ALU.subtract))
                for part in (c1, c2, c3, c4):
                    step(nc.vector.scalar_tensor_tensor(out=ang[:], in0=k[:], scalar=-part, in1=ang[:],
                                                        op0=ALU.mult, op1=ALU.add))
                step(nc.vector.tensor_scalar(sin, ang[:], LIM, -LIM, ALU.min, ALU.max))
                step(nc.vector.tensor_scalar(cos, ang[:], math.pi / 2, None, ALU.add))
                step(nc.vector.tensor_scalar(wrap[:], cos, math.pi, -two_pi, ALU.is_gt, ALU.mult))
                step(nc.vector.tensor_tensor(cos, cos, wrap[:], ALU.add))
                nc.vector.tensor_scalar(cos, cos, LIM, -LIM, ALU.min, ALU.max).then_inc(angles, 1)

            @block.scalar
            def _(act):
                act.wait_ge(angles, 1)
                nc.scalar.activation(sin, sin, ACT.Sin)
                nc.scalar.activation(cos, cos, ACT.Sin)


def conv_gemm(c, name, blocks, taps, weight, by_block, acc):
    nc = c.nc
    first = c.used
    plan, at, sizes = c.queue[first:], 0, []
    while sum(sizes) < blocks:
        sizes.append(plan[at][1][3] // P)
        at += 1
    last = [sum(sizes[:i + 1]) - 1 for i in range(len(sizes))]
    if True:
        with c.stage(name, "filled", "convolved", "silus", "step") as (
                block, filled, convolved, silus, step_sem):
            @block.sync
            def _(sp):
                c.load_up_to(sp, first + len(sizes) + RING)

            @block.tensor
            def _(pe):
                f = 0
                for size in sizes:
                    wt = c.arrived(pe)
                    for b in range(size):
                        if f >= 8:
                            pe.wait_ge(convolved, f - 7)
                        for k in range(8):
                            ins = nc.tensor.matmul(c.banks(f % 8), wt[:, k, b * P:(b + 1) * P],
                                                   c.hT[:, k, :], start=(k == 0), stop=(k == 7))
                        ins.then_inc(c.chunk_used if b == size - 1 else filled, 1)
                        f += 1

            @block.vector
            def _(dve):
                step = Steps(dve, step_sem)
                n_silu = 0
                for f in range(blocks):
                    if f in last:
                        dve.wait_ge(c.chunk_used, first + last.index(f) + 1)
                    else:
                        dve.wait_ge(filled, f + 1 - sum(x < f for x in last))
                    kind, dst = by_block(f)
                    w, a = weight(f), acc[:, f % 4, :]
                    if f >= 4:
                        n_before = sum(by_block(i)[0] == "silu" for i in range(f - 3))
                        if n_before:
                            dve.wait_ge(silus, n_before)
                    step(nc.vector.tensor_scalar(a, c.banks(f % 8), w[:, taps - 1:taps], None, ALU.mult))
                    for i in range(1, taps):
                        ins = nc.vector.scalar_tensor_tensor(
                            out=a[:, i:], in0=c.banks(f % 8)[:, 0:SEQ - i], scalar=w[:, taps - 1 - i:taps - i],
                            in1=a[:, i:], op0=ALU.mult, op1=ALU.add)
                        if i < taps - 1:
                            step(ins)
                    ins.then_inc(convolved, 1)
                    if kind == "times":
                        dve.wait_ge(convolved, f + 1)
                        step(nc.vector.tensor_tensor(dst, dst, a, ALU.mult))

            @block.scalar
            def _(act):
                for f in range(blocks):
                    kind, dst = by_block(f)
                    if kind == "silu":
                        act.wait_ge(convolved, f + 1)
                        nc.scalar.activation(dst, acc[:, f % 4, :], ACT.Silu).then_inc(silus, 1)


def rows_norm(c, name, src, gain, half, out, gate=None, add=None):
    nc = c.nc
    with ExitStack() as ctx:
        sb = lambda n, s: ctx.enter_context(nc.sbuf_tensor(name + n, s, F32))
        junk, y = sb("junk", [P, DM]), sb("y", [P, 2, DM])
        ssq, rstd = sb("ssq", [P, TT]), sb("rstd", [P, TT])
        with c.stage(name, "squares", "mean", "rstd", "step") as (block, squares, mean, rstd_ready, step_sem):
            @block.scalar
            def _(act):
                for t in range(TT):
                    if t:
                        act.wait_ge(squares, t)
                    nc.scalar.activation(junk[:], src[:, t, :], ACT.Square,
                                         accum_out=ssq[:, t:t + 1]).then_inc(squares, 1)

            @block.gpsimd
            def _(pool):
                for t in range(TT):
                    pool.wait_ge(squares, t + 1)
                    nc.gpsimd.tensor_scalar(ssq[:, t:t + 1], ssq[:, t:t + 1], 1.0 / DM, EPS,
                                            ALU.mult, ALU.add).then_inc(mean, 1)
                    pool.wait_ge(mean, t + 1)
                    nc.gpsimd.tensor_tensor(rstd[:, t:t + 1], ssq[:, t:t + 1], half[:, 0:1],
                                            ALU.pow).then_inc(rstd_ready, 1)

            @block.vector
            def _(dve):
                step = Steps(dve, step_sem)
                for t in range(TT):
                    dve.wait_ge(rstd_ready, t + 1)
                    dst = out[:, t, :] if gate is None and add is None else y[:, t % 2, :]
                    ins = nc.vector.scalar_tensor_tensor(out=dst, in0=src[:, t, :], scalar=rstd[:, t:t + 1],
                                                         in1=gain, op0=ALU.mult, op1=ALU.mult)
                    if gate is not None:
                        step(ins)
                        ins = nc.vector.tensor_tensor(dst, dst, gate[:, t, :], ALU.mult)
                    if add is not None:
                        step(ins)
                        step(nc.vector.tensor_tensor(out[:, t, :], dst, add[:, t, :], ALU.add))
                    elif gate is None:
                        step(ins)


def delta_inputs(c, name, qkv, proj, rows, half, g, sq):
    nc = c.nc
    H, W = GDN_H, GDN_H * HD
    shape = [P, TT, H, HD]
    wide = lambda s: s.unsqueeze(3).broadcast_to(shape)
    q4, k4, v4 = (qkv[:, :, i * W:(i + 1) * W].rearrange("p t (h d) -> p t h d", d=HD) for i in range(3))
    with ExitStack() as ctx:
        sb = lambda n, s: ctx.enter_context(nc.sbuf_tensor(name + n, s, F32))
        norm = sb("norm", [P, TT, 2 * H])
        a, e, ea = sb("a", [P, TT, H]), sb("e", [P, TT, H]), sb("ea", [P, H])
        with c.stage(name, "step", "squared", "summed", "power", "rstd", "logits", "gates", "softs", "logged",
                     "beta", "decays", "sums", "shifted", "exps", "act_step") as (
                block, step_sem, squared, summed, power, rstd, logits, gates, softs, logged, beta, decays,
                sums, shifted, exps, act_step):
            @block.scalar
            def _(act):
                nc.scalar.activation(sq, qkv[:, :, 0:2 * W].rearrange("p t (h d) -> p t h d", d=HD),
                                     ACT.Square).then_inc(squared, 1)
                nc.scalar.activation(ea[:], rows["a_log"], ACT.Exp).then_inc(gates, 1)
                act.wait_ge(logits, 1)
                nc.scalar.activation(e[:], a[:], ACT.Abs).then_inc(act_step, 1)
                act.wait_ge(act_step, 1)
                nc.scalar.activation(e[:], e[:], ACT.Exp, scale=-1.0).then_inc(act_step, 1)
                act.wait_ge(act_step, 2)
                nc.scalar.activation(e[:], e[:], ACT.Ln, bias=1.0).then_inc(softs, 1)
                nc.scalar.activation(g["beta"], proj[:, :, B_B:B_B + H], ACT.Exp, scale=-1.0).then_inc(beta, 1)
                act.wait_ge(shifted, 1)
                nc.scalar.activation(g["eg"], g["gcum"], ACT.Exp).then_inc(exps, 1)
                nc.scalar.activation(g["el"], g["el"], ACT.Exp).then_inc(exps, 1)
                nc.scalar.activation(g["etot"], g["etot"], ACT.Exp).then_inc(exps, 1)

            @block.gpsimd
            def _(pool):
                pool.wait_ge(summed, 1)
                nc.gpsimd.tensor_scalar(norm[:], norm[:], EPS, None, ALU.add).then_inc(power, 1)
                pool.wait_ge(power, 1)
                nc.gpsimd.tensor_tensor(norm[:], norm[:],
                                        half[:, 0:1].unsqueeze(2).broadcast_to([P, TT, 2 * H]),
                                        ALU.pow).then_inc(rstd, 1)

            @block.tensor
            def _(pe):
                pe.wait_ge(decays, 1)
                for t in range(TT):
                    nc.tensor.matmul(c.ps[:, 0, t * H:(t + 1) * H], c.cst("upto"), a[:, t, :], start=True, stop=True)
                for t in range(TT):
                    ins = nc.tensor.matmul(c.ps[:, 1, t * H:(t + 1) * H], c.cst("ones"), a[:, t, :],
                                           start=True, stop=True)
                ins.then_inc(sums, 1)

            @block.vector
            def _(dve):
                step = Steps(dve, step_sem)
                rowsH = lambda r: r.unsqueeze(1).broadcast_to([P, TT, H])
                nc.vector.tensor_tensor(a[:], proj[:, :, B_A:B_A + H], rowsH(rows["dt_bias"]),
                                        ALU.add).then_inc(logits, 1)
                dve.wait_ge(squared, 1)
                nc.vector.tensor_reduce(norm[:], sq, AX.X, ALU.add).then_inc(summed, 1)
                dve.wait_ge(softs, 1)
                step(nc.vector.scalar_tensor_tensor(out=a[:], in0=a[:], scalar=0.0, in1=e[:],
                                                    op0=ALU.max, op1=ALU.add))
                dve.wait_ge(gates, 1)
                step(nc.vector.tensor_tensor(a[:], a[:], rowsH(ea[:]), ALU.mult))
                nc.vector.tensor_scalar(a[:], a[:], -1.0, None, ALU.mult).then_inc(decays, 1)
                dve.wait_ge(beta, 1)
                step(nc.vector.tensor_scalar(g["beta"], g["beta"], 1.0, None, ALU.add))
                step(nc.vector.reciprocal(g["beta"], g["beta"]))
                dve.wait_ge(sums, 1)
                view = lambda b: c.ps[:, b, 0:TT * H].rearrange("p (t h) -> p t h", t=TT)
                step(nc.vector.tensor_copy(g["gcum"], view(0)))
                nc.vector.tensor_scalar(g["minus_g"], view(0), -1.0, None, ALU.mult)
                step(nc.vector.tensor_copy(g["etot"], view(1)))
                nc.vector.tensor_tensor(g["el"], view(1), g["gcum"], ALU.subtract).then_inc(shifted, 1)
                dve.wait_ge(rstd, 1)
                step(nc.vector.tensor_scalar(norm[:, :, 0:H], norm[:, :, 0:H], HD ** -0.5, None, ALU.mult))
                nc.vector.tensor_tensor(q4, q4, wide(norm[:, :, 0:H]), ALU.mult)
                step(nc.vector.tensor_tensor(k4, k4, wide(norm[:, :, H:]), ALU.mult))
                as4 = lambda n: g[n].rearrange("p t (h d) -> p t h d", d=HD)
                nc.vector.tensor_tensor(as4("kb"), k4, wide(g["beta"]), ALU.mult)
                step(nc.vector.tensor_tensor(v4, v4, wide(g["beta"]), ALU.mult))
                dve.wait_ge(exps, 3)
                nc.vector.tensor_tensor(as4("qe"), q4, wide(g["eg"]), ALU.mult)
                nc.vector.tensor_tensor(as4("kbe"), as4("kb"), wide(g["eg"]), ALU.mult)
                nc.vector.tensor_tensor(as4("kel"), k4, wide(g["el"]), ALU.mult)


def delta_products(c, name, g, kT, kbT, qT, LT, attnT, dec):
    nc = c.nc
    H = GDN_H
    if True:
        with c.stage(name, "rows", "masked", "decays", "dots", "kept", "step") as (
                block, rows, masked, decays, dots, kept, step_sem):
            @block.tensor
            def _(pe):
                for h in range(H):
                    b, pair = HD * (h % 2), h // 2
                    if h >= 2:
                        pe.wait_ge(kept, h - 1)
                    for t in range(TT):
                        ins = nc.tensor.matmul(c.ps[:, h % 2, t * P:(t + 1) * P],
                                               g["gcum"][:, t, h:h + 1].broadcast_to([P, P]), c.ident,
                                               start=True, stop=True)
                    ins.then_inc(rows, 1)
                    for bank, rhs in ((2, kbT), (4, qT)):
                        for t in range(TT):
                            s = slice(t * P, (t + 1) * P)
                            ins = nc.tensor.matmul(c.ps[:, bank + h % 2, s], kT[b:b + HD, pair, s],
                                                   rhs[b:b + HD, pair, s], start=True, stop=True)
                    ins.then_inc(dots, 1)

            @block.scalar
            def _(act):
                for h in range(H):
                    act.wait_ge(masked, h + 1)
                    if h >= 2:
                        act.wait_ge(kept, h - 1)
                    for t in range(TT):
                        s = slice(t * P, (t + 1) * P)
                        ins = nc.scalar.activation(dec[:, h % 2, s], c.ps[:, h % 2, s], ACT.Exp,
                                                   bias=g["minus_g"][:, t, h:h + 1])
                    ins.then_inc(decays, 1)

            @block.vector
            def _(dve):
                step = Steps(dve, step_sem)
                four = lambda m: m.unsqueeze(1).broadcast_to([P, TT, P])
                by4 = lambda a: a.rearrange("p (t n) -> p t n", t=TT)
                for h in range(H):
                    dve.wait_ge(rows, h + 1)
                    r = by4(c.banks(h % 2))
                    nc.vector.tensor_tensor(r, r, four(c.cst("inclT")), ALU.add).then_inc(masked, 1)
                    dve.wait_ge(decays, h + 1)
                    dve.wait_ge(dots, h + 1)
                    d = dec[:, h % 2, :]
                    step(nc.vector.tensor_tensor(attnT[:, h, :], c.banks(4 + h % 2), d, ALU.mult))
                    step(nc.vector.tensor_tensor(LT[:, h, :], c.banks(2 + h % 2), d, ALU.mult))
                    L = by4(LT[:, h, :])
                    nc.vector.tensor_tensor(L, L, four(c.cst("strict01")), ALU.mult).then_inc(kept, 1)


def unit_lower_inverse(c, name, LT, X, XT, Y, M):
    nc = c.nc
    H = GDN_H
    sizes = [1, 2, 4, 8, 16, 32, 64]
    units = [(s, h) for s in sizes for h in range(H)]
    sl = [slice(t * P, (t + 1) * P) for t in range(TT)]
    if True:
        with c.stage(name, "started", "Ys", "Y_kept", "Zs", "masked", "grown") as (
                block, started, Ys, Y_kept, Zs, masked, grown):
            @block.tensor
            def _(pe):
                for i in range(len(units) + 1):
                    if i < len(units):
                        s, h = units[i]
                        if i < H:
                            pe.wait_ge(started, 1)
                        else:
                            pe.wait_ge(grown, i - H + 1)
                        if i >= 2:
                            pe.wait_ge(Y_kept, i - 1)
                        for t in range(TT):
                            ins = nc.tensor.matmul(c.ps[:, i % 2, sl[t]], LT[:, h, sl[t]], X[:, h, sl[t]],
                                                   start=True, stop=True)
                        ins.then_inc(Ys, 1)
                    u = i - 1
                    if u >= 0:
                        s, h = units[u]
                        pe.wait_ge(Y_kept, u + 1)
                        if u >= 2:
                            pe.wait_ge(masked, u - 1)
                        for t in range(TT):
                            ins = nc.tensor.matmul(c.ps[:, 2 + u % 2, sl[t]], Y[:, u % 2, sl[t]],
                                                   XT[:, h, sl[t]], start=True, stop=True)
                        if s != sizes[-1]:
                            for t in range(TT):
                                ins = nc.tensor.matmul(c.ps[:, 4 + u % 2, sl[t]], XT[:, h, sl[t]],
                                                       Y[:, u % 2, sl[t]], start=True, stop=True)
                        ins.then_inc(Zs, 1)

            @block.scalar
            def _(act):
                for i in range(len(units)):
                    act.wait_ge(Ys, i + 1)
                    if i >= 2:
                        act.wait_ge(Zs, i - 1)
                    nc.scalar.copy(Y[:, i % 2, :], c.banks(i % 2)).then_inc(Y_kept, 1)

            @block.vector
            def _(dve):
                four = lambda m: m.unsqueeze(1).broadcast_to([P, TT, P])
                by4 = lambda a: a.rearrange("p (t n) -> p t n", t=TT)
                for h in range(H):
                    nc.vector.tensor_copy(by4(X[:, h, :]), four(c.ident))
                    ins = nc.vector.tensor_copy(by4(XT[:, h, :]), four(c.ident))
                ins.then_inc(started, 1)
                for i, (s, h) in enumerate(units):
                    dve.wait_ge(Zs, i + 1)
                    if i >= 2:
                        dve.wait_ge(grown, i - 1)
                    ins = nc.vector.tensor_tensor(by4(M[:, i % 2, 0, :]), by4(c.banks(2 + i % 2)),
                                                  four(c.cst(f"high{s}")), ALU.mult)
                    if s != sizes[-1]:
                        ins = nc.vector.tensor_tensor(by4(M[:, i % 2, 1, :]), by4(c.banks(4 + i % 2)),
                                                      four(c.cst(f"low{s}")), ALU.mult)
                    ins.then_inc(masked, 1)

            @block.gpsimd
            def _(pool):
                for i, (s, h) in enumerate(units):
                    pool.wait_ge(masked, i + 1)
                    if i == 0:
                        pool.wait_ge(started, 1)
                    ins = nc.gpsimd.tensor_tensor(XT[:, h, :], XT[:, h, :], M[:, i % 2, 0, :], ALU.add)
                    if s != sizes[-1]:
                        ins = nc.gpsimd.tensor_tensor(X[:, h, :], X[:, h, :], M[:, i % 2, 1, :], ALU.add)
                    ins.then_inc(grown, 1)


def delta_scan(c, name, g, XT, attnT, qeT, vb, minus_wT, S, vn, out):
    nc = c.nc
    H = GDN_H
    half_of = lambda h: (HD * (h % 2), h // 2)
    heads_of = lambda bank: c.ps[:, bank, 0:H // 2 * HD].rearrange("p (a d) -> p a d", d=HD)
    with ExitStack() as ctx:
        sb = lambda n, s: ctx.enter_context(nc.sbuf_tensor(name + n, s, F32))
        et = sb("et", [P, TT, H // 2])
        with c.stage(name, "ws", "ws_kept", "news", "news_kept", "outs", "outs_kept", "grown", "states", "step") as (
                block, ws, ws_kept, news, news_kept, outs, outs_kept, grown, states, step_sem):
            @block.tensor
            def _(pe):
                for pair in range(H // 2):
                    for h in (2 * pair, 2 * pair + 1):
                        b = HD * (h % 2)
                        for t in range(TT):
                            s = slice(t * P, (t + 1) * P)
                            ins = nc.tensor.matmul(c.ps[b:b + HD, pair, s], g["kbe"][:, t, h * HD:(h + 1) * HD],
                                                   XT[:, h, s], start=True, stop=True)
                    ins.then_inc(ws, 1)
                pe.wait_ge(ws_kept, H // 2)
                for t in range(TT):
                    s = slice(t * P, (t + 1) * P)
                    if t:
                        pe.wait_ge(states, t)
                    for h in range(H):
                        b, pair = half_of(h)
                        col, own = slice(h * HD, (h + 1) * HD), slice(pair * HD, (pair + 1) * HD)
                        new = c.ps[:, (3, 6)[h % 2], own]
                        ins = nc.tensor.matmul(new, XT[:, h, s], vb[:, t, col],
                                               start=True, stop=(t == 0))
                        if t:
                            ins = nc.tensor.matmul(new, minus_wT[b:b + HD, pair, s],
                                                   S[b:b + HD, pair, :], start=False, stop=True)
                    ins.then_inc(news, 1)
                    if t:
                        pe.wait_ge(outs_kept, t)
                    pe.wait_ge(news_kept, t + 1)
                    for h in range(H):
                        b, pair = half_of(h)
                        if t < TT - 1:
                            ins = nc.tensor.matmul(c.ps[b:b + HD, 5, pair * HD:(pair + 1) * HD],
                                                   g["kel"][:, t, h * HD:(h + 1) * HD], vn[:, t % 2, h, :],
                                                   start=True, stop=True)
                    if t < TT - 1:
                        ins.then_inc(grown, 1)
                    for h in range(H):
                        b, pair = half_of(h)
                        o = c.ps[:, (4, 7)[h % 2], pair * HD:(pair + 1) * HD]
                        ins = nc.tensor.matmul(o, attnT[:, h, s], vn[:, t % 2, h, :],
                                               start=True, stop=(t == 0))
                        if t:
                            ins = nc.tensor.matmul(o, qeT[b:b + HD, pair, s],
                                                   S[b:b + HD, pair, :], start=False, stop=True)
                    ins.then_inc(outs, 1)

            @block.scalar
            def _(act):
                for pair in range(H // 2):
                    act.wait_ge(ws, pair + 1)
                    nc.scalar.mul(minus_wT[:, pair, :], c.banks(pair), -1.0).then_inc(ws_kept, 1)
                for t in range(TT):
                    act.wait_ge(outs, t + 1)
                    for b in range(2):
                        ins = nc.scalar.copy(out[:, t, b:H:2, :], heads_of((4, 7)[b]))
                    ins.then_inc(outs_kept, 1)

            @block.vector
            def _(dve):
                step = Steps(dve, step_sem)
                by_pair = g["etot"].rearrange("p t (a b) -> p t a b", b=2)
                for b in range(2):
                    r = slice(b * HD, (b + 1) * HD)
                    ins = nc.vector.tensor_copy(et[r], by_pair[r, :, :, b])
                step(ins)
                for t in range(TT):
                    dve.wait_ge(news, t + 1)
                    for b in range(2):
                        ins = nc.vector.tensor_copy(vn[:, t % 2, b:H:2, :], heads_of((3, 6)[b]))
                    ins.then_inc(news_kept, 1)
                    if t < TT - 1:
                        dve.wait_ge(grown, t + 1)
                        if t:
                            dve.wait_ge(outs, t + 1)
                        for pair in range(H // 2):
                            new = c.ps[:, 5, pair * HD:(pair + 1) * HD]
                            if t == 0:
                                ins = nc.vector.tensor_copy(S[:, pair, :], new)
                            else:
                                ins = nc.vector.scalar_tensor_tensor(
                                    out=S[:, pair, :], in0=S[:, pair, :], scalar=et[:, t, pair:pair + 1],
                                    in1=new, op0=ALU.mult, op1=ALU.add)
                        ins.then_inc(states, 1)
                        dve.wait_ge(states, t + 1)


def compressed_attention(c, name, qT, blocks, pe_tiles, w2, gates, out, kcT, vcmp, kv2T):
    nc = c.nc
    H, G, N = NSA_H, NSA_G, N_CMP
    first = c.used
    seen, neg = c.cst("cmp_seen"), c.cst("cmp_neg")
    with ExitStack() as ctx:
        sb = lambda n, s: ctx.enter_context(nc.sbuf_tensor(name + n, s, F32))
        hid = sb("hid", [P, 2, G * N])
        s, st = sb("s", [P, H, TT, N]), sb("st", [P, H, TT])
        pT = sb("pT", [N, H, SEQ])
        with c.stage(name, "summed", "hidden", "silus", "small", "small_kept", "scores", "step", "centred", "exps",
                     "masked", "turned", "turned_kept", "outs") as (
                block, summed, hidden, silus, small, small_kept, scores, step_sem, centred, exps, masked,
                turned, turned_kept, outs):
            @block.sync
            def _(sp):
                c.load_up_to(sp, first + 2 + RING)

            @block.tensor
            def _(pe):
                for i in range(2):
                    wt = c.arrived(pe)
                    pe.wait_ge(summed, i + 1)
                    for m in range(CMP_LEN // 2):
                        ins = nc.tensor.matmul(c.ps[:, i, 0:G * N], wt[:, m, :], blocks[:, i, m, :],
                                               start=(m == 0), stop=(m == CMP_LEN // 2 - 1))
                    ins.then_inc(c.chunk_used, 1)
                pe.wait_ge(silus, 2)
                for b in (0, HD):
                    nc.tensor.matmul(c.ps[b:b + HD, 2, 0:G * N], w2[:, 0:HD], hid[:, 0, :], start=True, stop=True)
                for gr in range(G):
                    ins = nc.tensor.matmul(c.ps[0:N, 3, gr * HD:(gr + 1) * HD], hid[:, 1, gr * N:(gr + 1) * N],
                                           w2[:, HD:2 * HD], start=True, stop=True)
                ins.then_inc(small, 1)
                pe.wait_ge(small_kept, 1)
                for h in range(H):
                    b, gr = HD * (h % 2), h // NSA_R
                    for t in range(TT):
                        ins = nc.tensor.matmul(c.ps[:, h, t * N:(t + 1) * N],
                                               qT[b:b + HD, h // 2, t * P:(t + 1) * P],
                                               kcT[b:b + HD, gr * N:(gr + 1) * N], start=True, stop=True)
                ins.then_inc(scores, 1)
                pe.wait_ge(masked, 1)
                for h in range(H):
                    for t in range(TT):
                        ins = nc.tensor.transpose(c.ps[0:N, h, t * P:(t + 1) * P], s[:, h, t, :], c.ident)
                    ins.then_inc(turned, 1)
                for h in range(H):
                    pe.wait_ge(turned_kept, h + 1)
                    for t in range(TT):
                        ins = nc.tensor.matmul(c.ps[:, h, t * HD:(t + 1) * HD], pT[:, h, t * P:(t + 1) * P],
                                               vcmp[0:N, h // NSA_R, :], start=True, stop=True)
                    ins.then_inc(outs, 1)

            @block.scalar
            def _(act):
                for i in range(2):
                    act.wait_ge(c.chunk_used, first + i + 1)
                    nc.scalar.activation(hid[:, i, :], c.ps[:, i, 0:G * N], ACT.Silu).then_inc(silus, 1)
                act.wait_ge(centred, 1)
                nc.scalar.activation(s[:], s[:], ACT.Exp).then_inc(exps, 1)
                for h in range(H):
                    act.wait_ge(turned, h + 1)
                    nc.scalar.copy(pT[:, h, :], c.ps[0:N, h, :]).then_inc(turned_kept, 1)

            @block.vector
            def _(dve):
                step = Steps(dve, step_sem)
                for i in range(2):
                    for gr in range(G):
                        by16 = kv2T[:, i, gr, :].rearrange("p (i r) -> p r i", r=16)
                        for b in range(2):
                            r = slice(b * HD, (b + 1) * HD)
                            for o in range(2):
                                ins = nc.vector.tensor_tensor(
                                    blocks[r, i, 8 * o:8 * o + 8, gr * N:(gr + 1) * N],
                                    by16[r, b:16:2, o:o + N],
                                    pe_tiles[r, 16 * i + 8 * o:16 * i + 8 * o + 8].unsqueeze(2
                                             ).broadcast_to([HD, 8, N]), ALU.add)
                    ins.then_inc(summed, 1)
                dve.wait_ge(small, 1)
                nc.vector.tensor_copy(kcT, c.ps[:, 2, 0:G * N])
                nc.vector.tensor_copy(vcmp[0:N], c.ps[0:N, 3, 0:G * HD].rearrange("p (g d) -> p g d", g=G)
                                      ).then_inc(small_kept, 1)
                dve.wait_ge(scores, 1)
                flat = s[:].rearrange("p h t n -> p h (t n)")
                step(nc.vector.tensor_tensor(flat, c.ps[:, 0:H, 0:TT * N],
                                             neg.unsqueeze(1).broadcast_to([P, H, TT * N]), ALU.add))
                step(nc.vector.tensor_reduce(st[:], s[:], AX.X, ALU.max))
                nc.vector.tensor_tensor(s[:], s[:], st[:].unsqueeze(3).broadcast_to([P, H, TT, N]),
                                        ALU.subtract).then_inc(centred, 1)
                dve.wait_ge(exps, 1)
                nc.vector.tensor_tensor(flat, flat, seen.unsqueeze(1).broadcast_to([P, H, TT * N]),
                                        ALU.mult).then_inc(masked, 1)
                dve.wait_ge(masked, 1)
                step(nc.vector.tensor_reduce(st[:], s[:], AX.X, ALU.add))
                step(nc.vector.tensor_scalar(st[:], st[:], 1e-30, None, ALU.max))
                step(nc.vector.reciprocal(st[:], st[:]))
                step(nc.vector.tensor_tensor(st[:], st[:], gates[:, :, 0:H].rearrange("p t h -> p h t"), ALU.mult))
                for h in range(H):
                    dve.wait_ge(outs, h + 1)
                    nc.vector.tensor_tensor(out[:, :, h, :], c.ps[:, h, 0:TT * HD].rearrange("p (t d) -> p t d", t=TT),
                                            st[:, h, :].unsqueeze(2).broadcast_to([P, TT, HD]), ALU.mult)


def stick_breaking(c, name, qT, kT, v, out):
    nc = c.nc
    units = [(h, j) for h in range(SB_H) for j in reversed(range(TT))]
    U = len(units)
    with ExitStack() as ctx:
        sb = lambda n, s: ctx.enter_context(nc.sbuf_tensor(name + n, s, F32))
        e = sb("e", [P, 2, SEQ])
        sp_, A = sb("sp", [P, 2, TT, SEQ]), sb("A", [P, 2, 2, SEQ])
        aT = sb("aT", [P, 2, TT, SEQ])
        with c.stage(name, "dots", "masked", "act_step", "logs", "softs", "suffix", "sums", "hidden", "weights",
                     "outs", "kept") as (block, dots, masked, act_step, logs, softs, suffix, sums, hidden,
                                         weights, outs, kept):
            @block.tensor
            def _(pe):
                for i in range(U + 8):
                    if i < U:
                        h, j = units[i]
                        b, pair = HD * (h % 2), h // 2
                        if i >= 3:
                            pe.wait_ge(softs, i - 2)
                        nc.tensor.matmul(c.ps[:, i % 3, 0:SEQ - j * P], kT[b:b + HD, pair, j * P:(j + 1) * P],
                                         qT[b:b + HD, pair, j * P:], start=True, stop=True).then_inc(dots, 1)
                    u = i - 2
                    if 0 <= u < U:
                        h, j = units[u]
                        b, pair = HD * (h % 2), h // 2
                        bank = c.ps[:, 3 + u % 3, 0:SEQ - j * P]
                        if u >= 3:
                            pe.wait_ge(weights, u - 2)
                        pe.wait_ge(softs, u + 1)
                        nc.tensor.matmul(bank, kT[b:b + HD, pair, j * P:(j + 1) * P], qT[b:b + HD, pair, j * P:],
                                         start=True, stop=False)
                        ins = nc.tensor.matmul(bank, c.cst("minus_from"), sp_[:, h % 2, j, 0:SEQ - j * P],
                                               start=False, stop=(j == TT - 1))
                        if j < TT - 1:
                            if j == TT - 2:
                                later = sp_[:, h % 2, TT - 1, 0:P]
                            else:
                                pe.wait_ge(suffix, 2 * h + (TT - 2 - j))
                                later = A[:, h % 2, j, 0:SEQ - (j + 1) * P]
                            ins = nc.tensor.matmul(bank[:, P:], c.cst("minus_ones"), later, start=False, stop=True)
                        ins.then_inc(sums, 1)
                    u = i - 5
                    if 0 <= u < U and units[u][1] == 0:
                        h = units[u][0]
                        pe.wait_ge(weights, u + 1)
                        if h >= 2:
                            pe.wait_ge(kept, h - 1)
                        for t in range(TT):
                            for j in range(t + 1):
                                ins = nc.tensor.matmul(c.ps[:, 6 + h % 2, t * HD:(t + 1) * HD],
                                                       aT[:, h % 2, j, (t - j) * P:(t - j + 1) * P],
                                                       v[:, j, h * HD:(h + 1) * HD], start=(j == 0), stop=(j == t))
                        ins.then_inc(outs, 1)

            @block.scalar
            def _(act):
                n = 0
                for i in range(U + 3):
                    if i < U:
                        h, j = units[i]
                        w = SEQ - j * P
                        z, ei = c.ps[:, i % 3, 0:w], e[:, i % 2, 0:w]
                        act.wait_ge(masked, i + 1)
                        if i >= 2:
                            act.wait_ge(softs, i - 1)
                        nc.scalar.activation(ei, z, ACT.Abs).then_inc(act_step, 1)
                        act.wait_ge(act_step, 2 * i + 1)
                        nc.scalar.activation(ei, ei, ACT.Exp, scale=-1.0).then_inc(act_step, 1)
                        act.wait_ge(act_step, 2 * i + 2)
                        nc.scalar.activation(ei, ei, ACT.Ln, bias=1.0).then_inc(logs, 1)
                    u = i - 2
                    if 0 <= u < U:
                        h, j = units[u]
                        w = SEQ - j * P
                        act.wait_ge(hidden, u + 1)
                        if h >= 2:
                            act.wait_ge(outs, h - 1)
                        nc.scalar.activation(aT[:, h % 2, j, 0:w], c.ps[:, 3 + u % 3, 0:w], ACT.Exp).then_inc(weights, 1)

            @block.vector
            def _(dve):
                for i in range(U + 3):
                    if i < U:
                        dve.wait_ge(dots, i + 1)
                        d = c.ps[:, i % 3, 0:P]
                        nc.vector.tensor_tensor(d, d, c.cst("strictT"), ALU.add).then_inc(masked, 1)
                    u = i - 1
                    if 0 <= u < U:
                        h, j = units[u]
                        w = SEQ - j * P
                        dve.wait_ge(logs, u + 1)
                        if h >= 2:
                            dve.wait_ge(weights, TT * (h - 1))
                        nc.vector.scalar_tensor_tensor(out=sp_[:, h % 2, j, 0:w], in0=c.ps[:, u % 3, 0:w],
                                                       scalar=0.0, in1=e[:, u % 2, 0:w], op0=ALU.max,
                                                       op1=ALU.add).then_inc(softs, 1)
                    u = i - 2
                    if 0 <= u < U:
                        dve.wait_ge(sums, u + 1)
                        d = c.ps[:, 3 + u % 3, 0:P]
                        nc.vector.tensor_tensor(d, d, c.cst("strictT"), ALU.add).then_inc(hidden, 1)
                    if 0 <= i - 3 < U and units[i - 3][1] == 1 and units[i - 3][0] >= 1:
                        h = units[i - 3][0] - 1
                        dve.wait_ge(outs, h + 1)
                        nc.vector.tensor_copy(out[:, :, h, :], c.ps[:, 6 + h % 2, 0:TT * HD].rearrange(
                            "p (t d) -> p t d", t=TT)).then_inc(kept, 1)
                h = SB_H - 1
                dve.wait_ge(outs, h + 1)
                nc.vector.tensor_copy(out[:, :, h, :], c.ps[:, 6 + h % 2, 0:TT * HD].rearrange(
                    "p (t d) -> p t d", t=TT)).then_inc(kept, 1)

            @block.gpsimd
            def _(pool):
                n = 0
                for h in range(SB_H):
                    if h >= 2:
                        pool.wait_ge(sums, TT * (h - 1))
                    pool.wait_ge(softs, TT * h + 2)
                    nc.gpsimd.tensor_copy(A[:, h % 2, 1, 0:P], sp_[:, h % 2, 2, 0:P])
                    nc.gpsimd.tensor_tensor(A[:, h % 2, 1, P:2 * P], sp_[:, h % 2, 2, P:2 * P],
                                            sp_[:, h % 2, 3, 0:P], ALU.add).then_inc(suffix, 1)
                    pool.wait_ge(softs, TT * h + 3)
                    pool.wait_ge(suffix, 2 * h + 1)
                    nc.gpsimd.tensor_copy(A[:, h % 2, 0, 0:P], sp_[:, h % 2, 1, 0:P])
                    nc.gpsimd.tensor_tensor(A[:, h % 2, 0, P:3 * P], sp_[:, h % 2, 1, P:3 * P],
                                            A[:, h % 2, 1, 0:2 * P], ALU.add).then_inc(suffix, 1)


def shape_constants():
    lane = np.arange(P)
    cols = {"ident": np.eye(P), "causal": np.where(lane[None, :] <= lane[:, None], 0.0, MASKED),
            "half": np.full((P, 64), -0.5)}
    common = list(cols)
    pos = np.arange(SEQ, dtype=np.float32)
    for dim in (32, 64):
        inv = (np.float32(10000.0) ** (-np.arange(0, dim, 2, dtype=np.float32) / dim)).astype(np.float32)
        ang = (pos[:, None] * inv[None, :]).astype(np.float32).astype(np.float64)
        for f, fn in (("cos", np.cos), ("sin", np.sin)):
            cols[f"{f}{dim}"] = fn(ang).reshape(TT, P, dim // 2).transpose(1, 0, 2).reshape(P, -1)
    gamma = np.log1p(-np.exp2(-5.0 - np.arange(RET_H)))
    rel = np.arange(SEQ)[None, None, :] - lane[:, None, None]
    decay = np.where(rel >= 0, np.exp(np.maximum(rel, 0) * gamma[None, :, None]), 0.0)
    cols["decay"] = decay.reshape(P, -1)
    first = list(cols)
    cols["strictT"] = np.where(lane[:, None] < lane[None, :], 0.0, MASKED)
    cols["inclT"] = np.where(lane[:, None] <= lane[None, :], 0.0, MASKED)
    cols["strict01"] = (lane[:, None] < lane[None, :]) * 1.0
    cols["upto"] = (lane[:, None] <= lane[None, :]) * 1.0
    cols["minus_from"] = (lane[:, None] >= lane[None, :]) * -1.0
    cols["ones"] = np.ones((P, P))
    cols["minus_ones"] = -np.ones((P, P))
    for s in (1, 2, 4, 8, 16, 32, 64):
        same = (lane[:, None] // (2 * s)) == (lane[None, :] // (2 * s))
        low = same & ((lane[:, None] // s) % 2 == 1) & ((lane[None, :] // s) % 2 == 0)
        cols[f"low{s}"] = -1.0 * low
        cols[f"high{s}"] = -1.0 * low.T
    t = np.arange(SEQ).reshape(TT, P).T[:, :, None]
    seen = np.arange(N_CMP)[None, None, :] * CMP_STRIDE + CMP_LEN - 1 <= t
    cols["cmp_seen"] = (seen * 1.0).reshape(P, -1)
    cols["cmp_neg"] = np.where(seen, 0.0, MASKED).reshape(P, -1)
    inv = (np.float32(10000.0) ** (-np.arange(HD // 2, dtype=np.float32) / (HD // 2))).astype(np.float32)
    cols["inv"] = np.broadcast_to(inv, (P, HD // 2))
    second = common + [k for k in cols if k not in first]

    def pack(names):
        where, at = {}, 0
        for k in names:
            where[k] = (at, at + cols[k].shape[1])
            at += cols[k].shape[1]
        return np.concatenate([cols[k] for k in names], axis=1).astype(np.float32), where
    return pack(first), pack(second)


def first_block(c, d, cst, layers=DEPTH):
    nc = c.nc
    x, hT = c.x, c.hT
    cos32 = cst("cos32").rearrange("p (t d) -> p t d", t=TT)
    sin32 = cst("sin32").rearrange("p (t d) -> p t d", t=TT)
    cos64 = cst("cos64").rearrange("p (t d) -> p t d", t=TT)
    sin64 = cst("sin64").rearrange("p (t d) -> p t d", t=TT)
    decay = cst("decay").rearrange("p (h u) -> p h u", h=RET_H)
    half = cst("half")
    with nc.Fori(0, layers) as l, ExitStack() as ctx:
        sb = lambda n, s: ctx.enter_context(nc.sbuf_tensor("a_" + n, s, F32))
        c.start_layer(A_WEIGHTS, d, "a_", l)
        gains = sb("gains", [P, 24])
        g_ret = sb("g_ret", [P, RET_H * RET_D])
        with c.stage("a_gains", "arrived") as (block, arrived):
            @block.sync
            def _(sp):
                layer = lambda n: d[n][bass.ds(l, 1)].rearrange("a p n -> p (a n)")
                sp.dma_start(gains[:], layer("a_gains")).then_inc(arrived, 16)
                sp.dma_start(g_ret[:], d["g_ret"][bass.ds(l, 1), :].broadcast_to([P, RET_H * RET_D])
                             ).then_inc(arrived, 16)
                c.load_up_to(sp, RING)
                sp.wait_ge(arrived, 32)

        norm_transpose(c, "mixnorm", x, [(0, DM)], gains[:, 0:8], half)
        with ExitStack() as ctx2:
            sb2 = lambda n, s: ctx2.enter_context(nc.sbuf_tensor("a_" + n, s, F32))
            mix = sb2("mix", [P, TT, DM])
            proj = sb2("proj", [P, TT, A_IN])
            gemm_tokens(c, "win", hT, 8, 6, lambda t, n, w: proj[:, t, n:n + w])
            norm_transpose(c, "ranknorm", proj, [(A_CQ, Q_RANK), (A_CKV, KV_RANK)], gains[:, 8:16], half)
            heads = lambda a, n, dim: proj[:, :, a:a + n * dim].rearrange("p t (h d) -> p t h d", d=dim)
            with ExitStack() as ctx3:
                sb3 = lambda n, s: ctx3.enter_context(nc.sbuf_tensor("a_" + n, s, F32))
                q = sb3("q", [P, TT, MLA_H * MLA_QK])
                kcat = sb3("kcat", [P, TT, MLA_H, MLA_QK])
                kT = sb3("kT", [P, MLA_H, SEQ])
                gemm_tokens(c, "uq", hT, Q_RANK // P, 2, lambda t, n, w: q[:, t, n:n + w])
                kv = proj[:, :, 0:DM]
                gemm_tokens(c, "ukv", hT[:, Q_RANK // P:], KV_RANK // P, 2,
                            lambda t, n, w: kv[:, t, n:n + w])
                q4 = q[:].rearrange("p t (h d) -> p t h d", d=MLA_QK)
                kv4 = kv.rearrange("p t (h d) -> p t h d", d=MLA_NOPE + MLA_V)
                flat = kT[:].rearrange("p h s -> p (h s)")
                rt1, rt2 = flat[:, 0:4 * SEQ], flat[:, 4 * SEQ:8 * SEQ + 0]
                if True:
                    with c.stage("mla_rope", "step", "pool_step") as (block, step_sem, pool_step):
                        @block.vector
                        def _(dve):
                            step = Steps(dve, step_sem)
                            kr = heads(A_KR, 1, MLA_ROPE)
                            rope(nc.vector, step, kr, cos32, sin32, rt1, 1, 16)
                            for t in range(TT):
                                nc.vector.tensor_copy(kcat[:, t, :, MLA_NOPE:], kr[:, t].broadcast_to([P, MLA_H, MLA_ROPE]))
                            rope(nc.vector, step, q4[:, :, :, MLA_NOPE:], cos32, sin32, rt1, MLA_H, 16)

                        @block.scalar
                        def _(act):
                            for t in range(TT):
                                nc.scalar.copy(kcat[:, t, :, 0:MLA_NOPE], kv4[:, t, :, 0:MLA_NOPE])

                        @block.gpsimd
                        def _(pool):
                            step = Steps(pool, pool_step)
                            for a, n, dim, cs, sn in ((A_AQ, DSA_H + 1, DSA_D, cos64, sin64),
                                                      (A_QI, IDX_H + 1, IDX_D, cos32, sin32)):
                                rope(nc.gpsimd, step, heads(a, n, dim), cs, sn, rt2, n, dim // 2)
                mla_scale = MLA_QK ** -0.5
                jobs = [(lambda t, h=h: kcat[:, t, h, :], MLA_QK, kT[0:MLA_QK, h, :], 1.0) for h in range(MLA_H)]
                jobs += [(lambda t, h=h: q4[:, t, h, :], MLA_QK, hT[0:MLA_QK, h, :], mla_scale) for h in range(MLA_H)]
                transpose_tiles(c, "mlaT", jobs)
                softmax_attention(c, "mla", [
                    (hT[0:MLA_QK, h, t * P:(t + 1) * P], kT[0:MLA_QK, h, 0:(t + 1) * P],
                     lambda j, h=h: kv4[:, j, h, MLA_NOPE:], c.causal,
                     mix[:, t, h * MLA_V:(h + 1) * MLA_V], None, False)
                    for h in range(MLA_H) for t in range(TT)])
            with ExitStack() as ctx3:
                sb3 = lambda n, s: ctx3.enter_context(nc.sbuf_tensor("a_" + n, s, F32))
                kdup, kidup = sb3("kdup", [P, TT, 2 * DSA_D]), sb3("kidup", [P, TT, 4 * IDX_D])
                qbT, kbT = sb3("qbT", [P, 2, SEQ]), sb3("kbT", [P, SEQ])
                qiT, kiT = sb3("qiT", [P, 2, SEQ]), sb3("kiT", [P, SEQ])
                rqT, rkT = sb3("rqT", [P, 2, SEQ]), sb3("rkT", [P, 2, SEQ])
                score, best = sb3("score", [P, TT - 1, SEQ]), sb3("best", [P, TT - 1, 8])
                rt = sb3("rt", [P, 2048])
                with c.stage("ret_rope", "step") as (block, step_sem):
                    @block.vector
                    def _(dve):
                        step = Steps(dve, step_sem)
                        for a in (A_RQ, A_RK):
                            rope(nc.vector, step, heads(a, RET_H, RET_D), cos64, sin64, rt, RET_H, 32)

                    @block.scalar
                    def _(act):
                        for i in range(2):
                            nc.scalar.copy(kdup[:, :, i * DSA_D:(i + 1) * DSA_D], proj[:, :, A_AK:A_AK + DSA_D])
                        for i in range(4):
                            nc.scalar.copy(kidup[:, :, i * IDX_D:(i + 1) * IDX_D], proj[:, :, A_KI:A_KI + IDX_D])
                        nc.scalar.mul(proj[:, :, A_WI:A_WI + IDX_H], proj[:, :, A_WI:A_WI + IDX_H],
                                      IDX_H ** -0.5 * IDX_D ** -0.5)
                tile_of = lambda a: (lambda t: proj[:, t, a:a + P])
                jobs = [(tile_of(A_AQ + i * P), P, qbT[:, i, :], DSA_D ** -0.5) for i in range(2)]
                jobs += [(tile_of(A_QI + i * P), P, qiT[:, i, :], 1.0) for i in range(2)]
                jobs += [(tile_of(A_RQ + i * P), P, rqT[:, i, :], RET_D ** -0.5) for i in range(2)]
                jobs += [(tile_of(A_RK + i * P), P, rkT[:, i, :], 1.0) for i in range(2)]
                jobs += [(lambda t: kdup[:, t, :], P, kbT[:], 1.0), (lambda t: kidup[:, t, :], P, kiT[:], 1.0)]
                transpose_tiles(c, "mixT", jobs)
                index_scores(c, "idx", qiT, kiT, proj[:, :, A_WI:A_WI + IDX_H], score)
                with c.stage("topk", "step") as (block, step_sem):
                    @block.vector
                    def _(dve):
                        top_k_mask(nc, dve, Steps(dve, step_sem), score, best)
                o_b = MLA_H * MLA_V
                units = []
                for h in range(DSA_H):
                    b = DSA_D * (h % 2)
                    for t in range(TT):
                        mask = c.causal if t == 0 else score[:, t - 1, 0:(t + 1) * P]
                        units.append((qbT[b:b + DSA_D, h // 2, t * P:(t + 1) * P],
                                      kbT[b:b + DSA_D, 0:(t + 1) * P],
                                      lambda j: proj[:, j, A_AV:A_AV + DSA_D], mask,
                                      mix[:, t, o_b + h * DSA_D:o_b + (h + 1) * DSA_D], None, False))
                softmax_attention(c, "dsa", units)
                o_c = o_b + DSA_H * DSA_D
                out4 = mix[:, :, o_c:o_c + RET_H * RET_D].rearrange("p t (h d) -> p t h d", d=RET_D)
                retention(c, "ret", rqT, rkT, proj[:, :, A_RV:A_RV + RET_H * RET_D], decay, out4)
                head_norm(c, "retnorm", out4, RET_H, g_ret[:].rearrange("p (h d) -> p h d", d=RET_D), out4,
                          half, center=True, gate=heads(A_RG, RET_H, RET_D))
            transpose_tiles(c, "mixcat", [(lambda t, k=k: mix[:, t, k * P:(k + 1) * P], P, hT[:, k, :], 1.0)
                                          for k in range(8)])
        resid = lambda t, n, w: x[:, t, n:n + w]
        gemm_tokens(c, "wout", hT, 8, 2, resid, add=resid)
        norm_transpose(c, "mlpnorm", x, [(0, DM)], gains[:, 16:24], half)
        with nc.sbuf_tensor("a_uT", [P, D_FF // P, SEQ], F32) as uT:
            relu_squared_gemm(c, "ff1", uT)
            gemm_tokens(c, "ff2", uT, D_FF // P, 2, resid, add=resid)
        c.end_layer()


def spans(sizes):
    at, where = 0, {}
    for n, w in sizes:
        where[n] = (at, at + w)
        at += w
    return where, at


B_COLS, B_NCOLS = spans([("ln_mix", 8), ("ln_ffn", 8), ("ln_ple", 8), ("gdn_conv", 9 * GDN_CONV),
                         ("ffn_conv", 2 * D_FF2 // P * FFN_CONV), ("pe", 2 * CMP_LEN // 2), ("w2", 2 * HD)])
B_ROWS, B_NROWS = spans([("a_log", GDN_H), ("dt_bias", GDN_H), ("gdn_norm", HD), ("nsa_norm", HD),
                         ("sb_norm", HD), ("ple_norm", DM)])


def second_block(c, d, cst, pos_i, layers=DEPTH):
    nc = c.nc
    x, hT = c.x, c.hT
    c.cst = cst
    half = cst("half")
    with ExitStack() as ctx0:
        cosb = ctx0.enter_context(nc.sbuf_tensor("b_cos", [P, TT, HD // 2], F32))
        sinb = ctx0.enter_context(nc.sbuf_tensor("b_sin", [P, TT, HD // 2], F32))
        cos, sin = cosb[:], sinb[:]
        rotation_tables(c, "angles", pos_i, cst("inv"), cos, sin)
        with nc.Fori(0, layers) as l, ExitStack() as ctx:
            sb = lambda n, s: ctx.enter_context(nc.sbuf_tensor("b_" + n, s, F32))
            c.start_layer(B_WEIGHTS, d, "b_", l)
            cols_t, rows_t = sb("cols", [P, B_NCOLS]), sb("rows", [P, B_NROWS])
            cols = {n: cols_t[:, a:b] for n, (a, b) in B_COLS.items()}
            rows = {n: rows_t[:, a:b] for n, (a, b) in B_ROWS.items()}
            with c.stage("b_gains", "arrived") as (block, arrived):
                @block.sync
                def _(sp):
                    sp.dma_start(cols_t[:], d["b_cols"][bass.ds(l, 1)].rearrange("a p n -> p (a n)")
                                 ).then_inc(arrived, 16)
                    sp.dma_start(rows_t[:], d["b_rows"][bass.ds(l, 1), :].broadcast_to([P, B_NROWS])
                                 ).then_inc(arrived, 16)
                    c.load_up_to(sp, RING)
                    sp.wait_ge(arrived, 32)
            norm_transpose(c, "bmixnorm", x, [(0, DM)], cols["ln_mix"], half)
            with ExitStack() as ctx1:
                mix = ctx1.enter_context(nc.sbuf_tensor("b_mix", [P, TT, DM], F32))
                attentions(c, mix, cos, sin, cols, rows, half)
                gated_delta(c, mix, cols, rows, half)
                transpose_tiles(c, "bmixcat", [(lambda t, k=k: mix[:, t, k * P:(k + 1) * P], P, hT[:, k, :], 1.0)
                                               for k in range(8)])
            resid = lambda t, n, w: x[:, t, n:n + w]
            gemm_tokens(c, "bwout", hT, 8, 2, resid, add=resid)
            norm_transpose(c, "ffnnorm", x, [(0, DM)], cols["ln_ffn"], half)
            F = D_FF2 // P
            with nc.sbuf_tensor("b_act", [P, F, SEQ], F32) as actT, \
                    nc.sbuf_tensor("b_acc", [P, 4, SEQ], F32) as acc:
                conv_gemm(c, "up", 2 * F, FFN_CONV,
                          lambda f: cols["ffn_conv"][:, f * FFN_CONV:(f + 1) * FFN_CONV],
                          lambda f: ("silu", actT[:, f, :]) if f < F else ("times", actT[:, f - F, :]), acc)
                gemm_tokens(c, "down", actT, F, 2, resid, add=resid)
            norm_transpose(c, "plenorm", x, [(0, DM)], cols["ln_ple"], half)
            with ExitStack() as ctx1:
                sb1 = lambda n, s: ctx1.enter_context(nc.sbuf_tensor("b_" + n, s, F32))
                gate, ple, p_sb = sb1("gate", [P, TT, DM]), sb1("ple", [P, TT, DM]), sb1("p", [P, TT, D_PLE])
                pT = sb1("pT", [P, D_PLE // P, SEQ])
                with c.stage("p_load", "arrived") as (block, arrived):
                    @block.sync
                    def _(sp):
                        sp.dma_start(p_sb[:], d["p"][bass.ds(l, 1)].rearrange("a p t n -> p (a t) n")
                                     ).then_inc(arrived, 16)
                        sp.wait_ge(arrived, 16)
                gemm_tokens(c, "plegate", hT, 8, 2, lambda t, n, w: gate[:, t, n:n + w])
                transpose_tiles(c, "pleT", [(lambda t, k=k: p_sb[:, t, k * P:(k + 1) * P], P, pT[:, k, :], 1.0)
                                            for k in range(D_PLE // P)])
                gemm_tokens(c, "ple", pT, D_PLE // P, 2, lambda t, n, w: ple[:, t, n:n + w])
                with c.stage("sigmoid") as (block,):
                    @block.scalar
                    def _(act):
                        nc.scalar.activation(gate[:], gate[:], ACT.Sigmoid)
                rows_norm(c, "plerows", ple[:], rows["ple_norm"], half, x, gate=gate, add=x)
            c.end_layer()


def attentions(c, mix, cos, sin, cols, rows, half):
    nc, hT = c.nc, c.hT
    o_n = GDN_H * HD
    o_s = o_n + NSA_H * HD
    with ExitStack() as ctx:
        sb = lambda n, s: ctx.enter_context(nc.sbuf_tensor("b_" + n, s, F32))
        proj = sb("proj", [P, TT, B_ATT])
        gemm_tokens(c, "watt", hT, 8, 4, lambda t, n, w: proj[:, t, n:n + w])
        heads = lambda a, n: proj[:, :, a:a + n * HD].rearrange("p t (h d) -> p t h d", d=HD)
        gates = proj[:, :, B_GATE:B_GATE + 3 * NSA_H]
        with ExitStack() as ctx1:
            sb1 = lambda n, s: ctx1.enter_context(nc.sbuf_tensor("b_" + n, s, F32))
            qT, ksT, kwT = sb1("qT", [P, NSA_H // 2, SEQ]), sb1("ksT", [P, NSA_G, SEQ]), sb1("kwT", [P, NSA_G, SEQ])
            kv2T = sb1("kv2T", [P, 2, NSA_G, SEQ])
            with ExitStack() as ctx2:
                dup = ctx2.enter_context(nc.sbuf_tensor("b_dup", [P, 2, NSA_G, TT, 2, HD], F32))
                dupc = ctx2.enter_context(nc.sbuf_tensor("b_dupc", [P, 2, NSA_G, TT, 2, HD], F32))
                rt1 = ctx2.enter_context(nc.sbuf_tensor("b_rt1", [P, 2 * TT * NSA_H * HD // 2], F32))
                rt2 = ctx2.enter_context(nc.sbuf_tensor("b_rt2", [P, 2 * TT * NSA_G * HD // 2], F32))
                with c.stage("nsarope", "step", "pool_step") as (block, step_sem, pool_step):
                    @block.vector
                    def _(dve):
                        step = Steps(dve, step_sem)
                        rope(nc.vector, step, heads(B_NQ, NSA_H), cos, sin, rt1, NSA_H, HD // 2)

                    @block.gpsimd
                    def _(pool):
                        step = Steps(pool, pool_step)
                        for a in (B_KC, B_KS, B_KW):
                            rope(nc.gpsimd, step, heads(a, NSA_G), cos, sin, rt2, NSA_G, HD // 2)

                    @block.scalar
                    def _(act):
                        nc.scalar.activation(gates, gates, ACT.Sigmoid)
                        act.wait_ge(pool_step, 9)
                        for i, a in ((0, B_KS), (1, B_KW)):
                            for g in range(NSA_G):
                                for r in range(2):
                                    nc.scalar.copy(dup[:, i, g, :, r, :], proj[:, :, a + g * HD:a + (g + 1) * HD])
                        for i, a in ((0, B_KC), (1, B_VC)):
                            for g in range(NSA_G):
                                for r in range(2):
                                    nc.scalar.copy(dupc[:, i, g, :, r, :], proj[:, :, a + g * HD:a + (g + 1) * HD])
                both = lambda s: (lambda t: s[:, t].rearrange("p r d -> p (r d)"))
                jobs = [(lambda t, i=i: proj[:, t, B_NQ + i * P:B_NQ + (i + 1) * P], P, qT[:, i, :], HD ** -0.5)
                        for i in range(NSA_H // 2)]
                jobs += [(both(dup[:, 0, g]), P, ksT[:, g, :], 1.0) for g in range(NSA_G)]
                jobs += [(both(dup[:, 1, g]), P, kwT[:, g, :], 1.0) for g in range(NSA_G)]
                jobs += [(both(dupc[:, i, g]), P, kv2T[:, i, g, :], 1.0) for i in range(2) for g in range(NSA_G)]
                transpose_tiles(c, "nsaT", jobs)
            out4 = mix[:, :, o_n:o_n + NSA_H * HD].rearrange("p t (h d) -> p t h d", d=HD)
            with ExitStack() as ctx2:
                sb2 = lambda n, s: ctx2.enter_context(nc.sbuf_tensor("b_" + n, s, F32))
                kcT, vcmp = sb2("kcT", [P, NSA_G * N_CMP]), sb2("vcmp", [32, NSA_G, HD])
                blocks = sb2("blocks", [P, 2, CMP_LEN // 2, NSA_G * N_CMP])
                compressed_attention(c, "cmp", qT, blocks, cols["pe"], cols["w2"], gates, out4, kcT[:], vcmp, kv2T)
            units = []
            for i, (kT, v) in enumerate(((ksT, B_VS), (kwT, B_VW))):
                for h in range(NSA_H):
                    b, g = HD * (h % 2), h // NSA_R
                    for t in range(TT):
                        units.append((qT[b:b + HD, h // 2, t * P:(t + 1) * P], kT[b:b + HD, g, 0:(t + 1) * P],
                                      lambda j, v=v, g=g: proj[:, j, v + g * HD:v + (g + 1) * HD], c.causal,
                                      out4[:, t, h, :], gates[:, t, (i + 1) * NSA_H + h:(i + 1) * NSA_H + h + 1], True))
            softmax_attention(c, "nsa", units)
            head_norm(c, "nsanorm", out4, NSA_H, rows["nsa_norm"].unsqueeze(1), out4, half)
        with ExitStack() as ctx1:
            sb1 = lambda n, s: ctx1.enter_context(nc.sbuf_tensor("b_" + n, s, F32))
            sqT, skT = sb1("sqT", [P, SB_H // 2, SEQ]), sb1("skT", [P, SB_H // 2, SEQ])
            jobs = [(lambda t, a=a, i=i: proj[:, t, a + i * P:a + (i + 1) * P], P, dst[:, i, :], s)
                    for a, dst, s in ((B_SQ, sqT, HD ** -0.5), (B_SK, skT, 1.0)) for i in range(SB_H // 2)]
            transpose_tiles(c, "sbT", jobs)
            out4 = mix[:, :, o_s:o_s + SB_H * HD].rearrange("p t (h d) -> p t h d", d=HD)
            stick_breaking(c, "stick", sqT, skT, proj[:, :, B_SV:B_SV + SB_H * HD], out4)
            head_norm(c, "sbnorm", out4, SB_H, rows["sb_norm"].unsqueeze(1), out4, half)


def gated_delta(c, mix, cols, rows, half):
    nc, hT = c.nc, c.hT
    W = GDN_H * HD
    with ExitStack() as ctx:
        sb = lambda n, s: ctx.enter_context(nc.sbuf_tensor("b_" + n, s, F32))
        zab, qkv = sb("zab", [P, TT, B_ZAB]), sb("qkv", [P, TT, GDN_QKV])
        work = sb("work", [P, 24, SEQ])
        g = {n: sb("g_" + n, [P, TT, GDN_H])[:] for n in ("beta", "gcum", "minus_g", "eg", "el", "etot")}
        g["kbe"], g["kel"] = sb("kbe", [P, TT, W])[:], sb("kel", [P, TT, W])[:]
        qeT = sb("qeT", [P, GDN_H // 2, SEQ])
        sT = work[:, 0:9, :]
        conv_gemm(c, "conv", GDN_QKV // P, GDN_CONV,
                  lambda f: cols["gdn_conv"][:, f * GDN_CONV:(f + 1) * GDN_CONV], lambda f: ("silu", sT[:, f, :]),
                  work[:, 9:13, :])
        gemm_tokens(c, "zab", hT, 8, 1, lambda t, n, w: zab[:, t, n:n + w])
        transpose_tiles(c, "convT", [(lambda t, f=f: sT[:, f, t * P:(t + 1) * P], P, qkv[:, :, f * P:(f + 1) * P], 1.0)
                                     for f in range(GDN_QKV // P)])
        token_major = lambda i: work[:, i:i + 3, :].rearrange("p a s -> p (a s)").rearrange("p (t n) -> p t n", t=TT)
        g["kb"], g["qe"] = token_major(12), token_major(15)
        sq = work[:, 0:6, :].rearrange("p a s -> p (a s)").rearrange("p (t h d) -> p t h d", t=TT, d=HD)
        delta_inputs(c, "dinputs", qkv, zab, rows, half, g, sq)
        kT, kbT, dec, qT = hT[:, 0:3, :], hT[:, 3:6, :], hT[:, 6:8, :], work[:, 18:21, :]
        jobs = []
        for src, dst in ((qkv[:, :, W:2 * W], kT), (g["kb"], kbT), (qkv[:, :, 0:W], qT), (g["qe"], qeT)):
            jobs += [(lambda t, s=src, i=i: s[:, t, i * P:(i + 1) * P], P, dst[:, i, :], 1.0) for i in range(W // P)]
        transpose_tiles(c, "deltaT", jobs)
        LT, attnT, X, XT = (work[:, 6 * i:6 * i + 6, :] for i in range(4))
        delta_products(c, "dprod", g, kT, kbT, qT, LT, attnT, dec)
        unit_lower_inverse(c, "dinv", LT, X, XT, hT[:, 0:2, :], hT[:, 2:6, :].rearrange("p (a b) s -> p a b s", a=2))
        out4 = mix[:, :, 0:W].rearrange("p t (h d) -> p t h d", d=HD)
        S = hT[:, 5, 0:W // 2].rearrange("p (a d) -> p a d", d=HD)
        vn = hT[:, 3:5, :].rearrange("p a s -> p (a s)")[:, 0:2 * W].rearrange("p (a h d) -> p a h d", a=2, d=HD)
        delta_scan(c, "dscan", g, XT, attnT, qeT, qkv[:, :, 2 * W:3 * W], hT[:, 0:3, :], S, vn, out4)
        z4 = zab[:, :, 0:W].rearrange("p t (h d) -> p t h d", d=HD)
        view = lambda i: work[:, i:i + 3, :].rearrange("p a s -> p (a s)").rearrange("p (t h d) -> p t h d", t=TT, d=HD)
        head_norm(c, "gdnnorm", out4, GDN_H, rows["gdn_norm"].unsqueeze(1), out4, half, gate=z4,
                  scratch=(view(0), view(3)))


def program(nc, d, out):
    ctx = ExitStack()
    (_, where_a), (_, where_b) = shape_constants()
    width = lambda w: max(b for _, b in w.values())
    with ctx:
        c = Core(nc, ctx)
        pos = c.sb("pos_i", [P, TT], I32)
        for which, where in (("a", where_a), ("b", where_b)):
            with nc.sbuf_tensor("const_" + which, [P, width(where)], F32) as ct:
                cst = lambda n, ct=ct, where=where: ct[:, where[n][0]:where[n][1]]
                c.ident, c.causal, c.cst = cst("ident"), cst("causal"), cst
                with c.stage("load_" + which, "arrived") as (block, arrived):
                    @block.sync
                    def _(sp):
                        sp.dma_start(ct[:], d["const_" + which]).then_inc(arrived, 16)
                        if which == "a":
                            sp.dma_start(c.x[:], d["x"]).then_inc(arrived, 16)
                        else:
                            sp.dma_start(pos[:], d["positions"]).then_inc(arrived, 16)
                        sp.wait_ge(arrived, 32)
                if which == "a":
                    first_block(c, d, cst)
                else:
                    second_block(c, d, cst, pos[:])
                gain = c.hT[:, 0:2, :].rearrange("p a s -> p (a s)")
                with c.stage("final_" + which, "arrived") as (block, arrived):
                    @block.sync
                    def _(sp):
                        i = "ab".index(which)
                        sp.dma_start(gain, d["finals"][i:i + 1, :].broadcast_to([P, DM])).then_inc(arrived, 16)
                        sp.wait_ge(arrived, 16)
                rows_norm(c, "final" + which, c.x, gain, cst("half"), c.x)
        with c.stage("store", "stored") as (block, stored):
            @block.sync
            def _(sp):
                sp.dma_start(out.rearrange("(t p) n -> p t n", p=P), c.x[:]).then_inc(stored, 16)
                sp.wait_ge(stored, 16)


def laid_out(inputs):
    a = {k: np.asarray(v) for k, v in inputs.items()}
    tokens = lambda v: np.ascontiguousarray(v.reshape(TT, P, -1).transpose(1, 0, 2))

    def chunks(w, plan):
        w = w.reshape(w.shape[0], -1, P, w.shape[-1])
        return np.concatenate([w[:, k:k + kt, :, n:n + cols].transpose(0, 2, 1, 3).reshape(w.shape[0], P, -1)
                               for k, kt, n, cols in plan], axis=2)

    def column(v):
        return v.reshape(DEPTH, -1, P).transpose(0, 2, 1)

    def taps(v):
        return v.reshape(DEPTH, v.shape[1], -1, P).transpose(0, 3, 2, 1).reshape(DEPTH, P, -1)

    (const_a, _), (const_b, _) = shape_constants()
    d = {"const_a": const_a, "const_b": const_b, "x": tokens(a["x"][0])}
    for name, plan in A_WEIGHTS.items():
        d["a_" + name] = chunks(a[name], plan)
    d["a_gains"] = np.concatenate([column(a[n]) for n in ("g_mix", "g_q", "g_kv", "g_mlp")], axis=2)
    d["g_ret"] = a["g_ret"]
    w_in = a["w_in_2"]
    sizes = [GDN_H * HD] * 4 + [GDN_H] * 2
    z0 = 3 * GDN_H * HD
    att0 = sum(sizes)
    parts = {"w_in_conv": w_in[:, :, 0:z0], "w_in_zab": w_in[:, :, z0:att0], "w_in_att": w_in[:, :, att0:],
             "cmp_k_w1": a["nsa_cmp_k_w1_2"], "cmp_v_w1": a["nsa_cmp_v_w1_2"], "w_out": a["w_out_2"],
             "w_up": a["w_up_2"], "w_down": a["w_down_2"], "w_ple_gate": a["w_ple_gate_2"], "w_ple": a["w_ple_2"]}
    for name, plan in B_WEIGHTS.items():
        d["b_" + name] = chunks(parts[name], plan)
    pair = lambda v: v.reshape(DEPTH, CMP_LEN // 2, P).transpose(0, 2, 1)
    d["b_cols"] = np.concatenate(
        [column(a["ln_mix_2"]), column(a["ln_ffn_2"]), column(a["ln_ple_2"]), taps(a["gdn_conv_2"]),
         taps(a["ffn_conv_2"]), pair(a["nsa_pe_k_2"]), pair(a["nsa_pe_v_2"]), a["nsa_cmp_k_w2_2"],
         a["nsa_cmp_v_w2_2"]], axis=2)
    d["b_rows"] = np.concatenate([a[n] for n in ("gdn_a_log_2", "gdn_dt_bias_2", "gdn_norm_2", "nsa_norm_2",
                                                 "sb_norm_2", "ple_norm_2")], axis=1)
    d["p"] = a["p_2"][:, 0].reshape(DEPTH, TT, P, D_PLE).transpose(0, 2, 1, 3)
    d["positions"] = a["positions_2"][0].reshape(TT, P).T
    d["finals"] = np.stack([a["g_final"], a["ln_final_2"]])
    return {k: np.ascontiguousarray(v) for k, v in d.items()}


def kernel(**inputs):
    import concourse.bacc as bacc
    from concourse.bass_utils import run_bass_kernel_spmd

    nc = bacc.Bacc("TRN2", target_bir_lowering=False, num_devices=1)
    arrays = laid_out(inputs)
    d = {k: nc.dram_tensor(f"in_{k}", v.shape, mybir.dt.from_np(v.dtype), kind="ExternalInput").ap()
         for k, v in arrays.items()}
    out = nc.dram_tensor("out_h", [SEQ, DM], F32, kind="ExternalOutput").ap()
    program(nc, d, out)
    r = run_bass_kernel_spmd(nc, [{f"in_{k}": v for k, v in arrays.items()}], core_ids=[0])
    return r.results[0]["out_h"].reshape(1, SEQ, DM)
```

```python
import math
from contextlib import ExitStack, contextmanager

import numpy as np
import concourse.bass as bass
from concourse import mybir
from concourse.alu_op_type import AluOpType as ALU

F32 = mybir.dt.float32
F32R = mybir.dt.float32r
I32 = mybir.dt.int32
ACT = mybir.ActivationFunctionType
AX = mybir.AxisListType

P = 128
SEQ = 512
TT = SEQ // P
DM = 1024
DEPTH = 2
EPS = 1e-6
MASKED = -1e30
TAKEN = -3e38
BANK = 512

MLA_H, MLA_NOPE, MLA_ROPE, MLA_V = 8, 64, 32, 64
MLA_QK = MLA_NOPE + MLA_ROPE
Q_RANK, KV_RANK = 768, 256
DSA_H, DSA_D, IDX_H, IDX_D = 4, 64, 8, 32
TOPK = min(256, SEQ // 4)
RET_H, RET_D = 4, 64
D_FF = 4 * DM
A_CQ = 0
A_CKV = A_CQ + Q_RANK
A_KR = A_CKV + KV_RANK
A_AQ = A_KR + MLA_ROPE
A_AK = A_AQ + DSA_H * DSA_D
A_AV = A_AK + DSA_D
A_QI = A_AV + DSA_D
A_KI = A_QI + IDX_H * IDX_D
A_WI = A_KI + IDX_D
A_RQ = A_WI + IDX_H
A_RK = A_RQ + RET_H * RET_D
A_RV = A_RK + RET_H * RET_D
A_RG = A_RV + RET_H * RET_D
A_IN = A_RG + RET_H * RET_D

HD = 64
GDN_H, NSA_H, NSA_G, SB_H = 6, 6, 2, 4
NSA_R = NSA_H // NSA_G
GDN_QKV = 3 * GDN_H * HD
GDN_CONV = 4
CMP_LEN, CMP_STRIDE, CMP_HIDDEN = 32, 16, 128
N_CMP = (SEQ - CMP_LEN) // CMP_STRIDE + 1
D_FF2, FFN_CONV, D_PLE = 2816, 3, 256
B_NQ = 0
B_KC = B_NQ + NSA_H * HD
B_VC = B_KC + NSA_G * HD
B_KS = B_VC + NSA_G * HD
B_VS = B_KS + NSA_G * HD
B_KW = B_VS + NSA_G * HD
B_VW = B_KW + NSA_G * HD
B_GATE = B_VW + NSA_G * HD
B_SQ = B_GATE + 3 * NSA_H
B_SK = B_SQ + SB_H * HD
B_SV = B_SK + SB_H * HD
B_ATT = B_SV + SB_H * HD
B_Z = 0
B_A = B_Z + GDN_H * HD
B_B = B_A + GDN_H
B_ZAB = B_B + GDN_H

RING = 4
CHUNK = 4 * 512


def chunks_of(rows, cols, width=512, deep=4, row0=0, col0=0):
    tiles = rows // P
    return [(row0 + k, min(deep, tiles - k), col0 + n, min(width, cols - n))
            for n in range(0, cols, width) for k in range(0, tiles, deep)]


A_HALF, B_HALF = D_FF // 2, D_FF2 // 2
A_WEIGHTS = [
    ("w_in", chunks_of(DM, A_IN)), ("w_uq", chunks_of(Q_RANK, MLA_H * MLA_QK)),
    ("w_ukv", chunks_of(KV_RANK, MLA_H * (MLA_NOPE + MLA_V))), ("w_out", chunks_of(DM, DM)),
    ("w_ff1", chunks_of(DM, A_HALF)), ("w_ff2", chunks_of(A_HALF, DM)),
    ("w_ff1", chunks_of(DM, A_HALF, col0=A_HALF)), ("w_ff2", chunks_of(A_HALF, DM, row0=A_HALF // P)),
]
B_WEIGHTS = [
    ("w_in_att", chunks_of(DM, B_ATT)),
    ("cmp_k_w1", chunks_of(CMP_LEN * HD, CMP_HIDDEN, deep=16)),
    ("cmp_v_w1", chunks_of(CMP_LEN * HD, CMP_HIDDEN, deep=16)),
    ("w_in_conv", chunks_of(DM, GDN_QKV)), ("w_in_zab", chunks_of(DM, B_ZAB)),
    ("w_out", chunks_of(DM, DM)),
    ("w_up", chunks_of(DM, B_HALF)), ("w_up", chunks_of(DM, B_HALF, col0=D_FF2)),
    ("w_down", chunks_of(B_HALF, DM)),
    ("w_up", chunks_of(DM, B_HALF, col0=B_HALF)), ("w_up", chunks_of(DM, B_HALF, col0=D_FF2 + B_HALF)),
    ("w_down", chunks_of(B_HALF, DM, row0=B_HALF // P)),
    ("w_ple_gate", chunks_of(DM, DM)), ("w_ple", chunks_of(D_PLE, DM)),
]


def plan_of(weights, name):
    return [c for n, cs in weights if n == name for c in cs]


class Steps:

    def __init__(self, engine, sem):
        self.engine, self.sem, self.count = engine, sem, 0

    def __call__(self, instruction):
        self.count += 1
        instruction.then_inc(self.sem, 1)
        self.engine.wait_ge(self.sem, self.count)


class Core:

    def __init__(self, nc, ctx):
        self.nc, self.ctx, self.old = nc, ctx, []
        self.n_stage = 0
        self.ps = ctx.enter_context(nc.psum_tensor("ps", [P, 8, BANK], F32))
        self.x = self.sb("x", [P, TT, DM])
        self.ring = self.sb("ring", [P, RING, CHUNK])
        self.slot_full = [ctx.enter_context(nc.semaphore(f"slot{i}_full")) for i in range(RING)]
        self.chunk_used = ctx.enter_context(nc.semaphore("chunk_used"))

    def sb(self, name, shape, dt=F32):
        return self.ctx.enter_context(self.nc.sbuf_tensor(name, shape, dt))

    @contextmanager
    def stage(self, name, *signals):
        nc = self.nc
        self.n_stage += 1
        sems = [nc.alloc_semaphore(name=f"{name}{self.n_stage}_{s}") for s in signals]
        with nc.Block() as block:
            yield (block, *sems)
        for s in sems:
            nc.sync.sem_clear(s)
        for s in self.old:
            nc.release_semaphore(s)
        self.old = sems

    def banks(self, t):
        return self.ps[:, t, :]

    def start_layer(self, weights, drams, prefix, l):
        self.queue, self.offsets, at = [], [], {}
        for name, chunks in weights:
            for k, kt, n, w in chunks:
                self.queue.append((drams[prefix + name], (k, kt, n, w)))
                self.offsets.append(at.get(name, 0))
                at[name] = at.get(name, 0) + kt * w
        self.loaded = self.used = 0
        self.l = l

    def load_up_to(self, sp, end, first=0, slot_read=None):
        for i in range(self.loaded, min(end, len(self.queue))):
            if slot_read is not None and i - RING >= first:
                slot_read(sp, i - RING)
            d, (_, kt, _, w) = self.queue[i]
            o = self.offsets[i]
            src = d[bass.ds(self.l, 1), :, o:o + kt * w].rearrange("a p n -> p (a n)")
            sp.dma_start(self.ring[:, i % RING, 0:kt * w], src).then_inc(self.slot_full[i % RING], 16)
        self.loaded = max(self.loaded, min(end, len(self.queue)))

    def chunk(self, i):
        _, (_, kt, _, w) = self.queue[i]
        return self.ring[:, i % RING, 0:kt * w].rearrange("p (k n) -> p k n", n=w)

    def wait_chunk(self, engine, i):
        engine.wait_ge(self.slot_full[i % RING], 16 * (i // RING + 1))

    def end_layer(self):
        nc = self.nc
        assert self.used == self.loaded == len(self.queue)
        nc.all_engine_barrier()
        for s in self.slot_full + [self.chunk_used]:
            nc.sync.sem_clear(s)
        nc.all_engine_barrier()


class SplitWeights:

    def __init__(self, core, ctx, name, n_chunks, hi_made, lo_made):
        self.c, self.hi_made, self.lo_made = core, hi_made, lo_made
        self.first, self.n = core.used, n_chunks
        self.plan = [q[1] for q in core.queue[self.first:self.first + n_chunks]]
        self.tiles = [0]
        for k, kt, n, w in self.plan:
            self.tiles.append(self.tiles[-1] + kt)
        self.buf = ctx.enter_context(core.nc.sbuf_tensor(name + "whl", [P, 2, 2, CHUNK], F32R, side="right"))
        core.used += n_chunks

    def part(self, j, half, k):
        w = self.plan[j][3]
        return self.buf[:, j % 2, half, k * w:(k + 1) * w]

    def make_hi(self, act, j):
        if not j < self.n:
            return
        self.c.wait_chunk(act, self.first + j)
        if j >= 2:
            act.wait_ge(self.c.chunk_used, self.first + j - 1)
        src = self.c.chunk(self.first + j)
        for k in range(self.plan[j][1]):
            self.c.nc.scalar.copy(self.part(j, 0, k), src[:, k, :]).then_inc(self.hi_made, 1)

    def make_lo(self, dve, j):
        if not j < self.n:
            return
        src = self.c.chunk(self.first + j)
        for k in range(self.plan[j][1]):
            dve.wait_ge(self.hi_made, self.tiles[j] + k + 1)
            self.c.nc.vector.tensor_tensor(self.part(j, 1, k), src[:, k, :], self.part(j, 0, k).bitcast(F32),
                                           ALU.subtract).then_inc(self.lo_made, 1)

    def slot_read(self, sp, i):
        sp.wait_ge(self.lo_made, self.tiles[i - self.first + 1])

    def load(self, sp):
        self.c.load_up_to(sp, self.first + self.n + RING, self.first, self.slot_read)

    def wait_tile(self, pe, j, k):
        pe.wait_ge(self.lo_made, self.tiles[j] + k + 1)


def product(nc, bank, stationary, moving, start, stop):
    (sh, sl), (mh, ml) = stationary, moving
    nc.tensor.matmul(bank, sh, mh, start=start, stop=False)
    nc.tensor.matmul(bank, sh, ml, start=False, stop=False)
    return nc.tensor.matmul(bank, sl, mh, start=False, stop=stop)


def norm_transpose(c, name, src, groups, gain, half, hl, load=None):
    nc = c.nc
    G = len(groups)
    with ExitStack() as ctx:
        sb = lambda n, s: ctx.enter_context(nc.sbuf_tensor(name + n, s, F32))
        xn, junk = sb("xn", [P, TT, DM]), sb("junk", [P, DM])
        ssq, rstd = sb("ssq", [P, TT, G]), sb("rstd", [P, TT, G])
        with c.stage(name, "squares", "mean", "rstd", "rows", "turned", "kept", "arrived") as (
                block, squares, mean, rstd_ready, rows, turned, kept, arrived):
            if load is not None:
                @block.sync
                def _(sp):
                    sp.dma_start(*load).then_inc(arrived, 16)
                    sp.wait_ge(arrived, 16)

            @block.scalar
            def _(act):
                n = 0
                for t in range(TT):
                    for g, (a, w) in enumerate(groups):
                        if n:
                            act.wait_ge(squares, n)
                        nc.scalar.activation(junk[:, a:a + w], src[:, t, a:a + w], ACT.Square,
                                             accum_out=ssq[:, t, g:g + 1]).then_inc(squares, 1)
                        n += 1
                for k in range(8):
                    act.wait_ge(turned, k + 1)
                    nc.scalar.activation(hl[:, 0, k, :], c.banks(k), ACT.Copy,
                                         scale=gain[:, k:k + 1]).then_inc(kept, 1)

            @block.gpsimd
            def _(pool):
                for t in range(TT):
                    pool.wait_ge(squares, G * (t + 1))
                    for g, (a, w) in enumerate(groups):
                        nc.gpsimd.tensor_scalar(ssq[:, t, g:g + 1], ssq[:, t, g:g + 1], 1.0 / w, EPS,
                                                ALU.mult, ALU.add).then_inc(mean, 1)
                    pool.wait_ge(mean, G * (t + 1))
                    nc.gpsimd.tensor_tensor(rstd[:, t, :], ssq[:, t, :], half[:, 0:G],
                                            ALU.pow).then_inc(rstd_ready, 1)

            @block.vector
            def _(dve):
                for t in range(TT):
                    dve.wait_ge(rstd_ready, t + 1)
                    for g, (a, w) in enumerate(groups):
                        nc.vector.tensor_scalar(xn[:, t, a:a + w], src[:, t, a:a + w],
                                                rstd[:, t, g:g + 1], None, ALU.mult).then_inc(rows, 1)
                for k in range(8):
                    dve.wait_ge(kept, k + 1)
                    nc.vector.scalar_tensor_tensor(out=hl[:, 1, k, :], in0=c.banks(k), scalar=gain[:, k:k + 1],
                                                   in1=hl[:, 0, k, :].bitcast(F32), op0=ALU.mult,
                                                   op1=ALU.subtract)

            @block.tensor
            def _(pe):
                for t in range(TT):
                    pe.wait_ge(rows, G * (t + 1))
                    for k in range(8):
                        ins = nc.tensor.transpose(c.ps[:, k, t * P:(t + 1) * P],
                                                  xn[:, t, k * P:(k + 1) * P], c.ident)
                        if t == TT - 1:
                            ins.then_inc(turned, 1)


def gemm_tokens(c, name, aT, k_tiles, n_chunks, out, add=None, k0=0):
    nc = c.nc
    deep = [q[1][1] for q in c.queue[c.used:]]
    cols, at = [], 0
    for n in range(n_chunks):
        parts, done = [], 0
        while done < k_tiles:
            parts.append(at)
            done += deep[at]
            at += 1
        cols.append(parts)
    by_act = lambda t: add is None and t % 2 == 0
    n_act, n_dve = (TT // 2, TT // 2) if add is None else (0, TT)
    with ExitStack() as ctx, c.stage(name, "hi", "lo", "filled", "act_kept", "dve_kept") as (
            block, hi_made, lo_made, filled, act_kept, dve_kept):
        w = SplitWeights(c, ctx, name, at, hi_made, lo_made)

        @block.sync
        def _(sp):
            w.load(sp)

        @block.tensor
        def _(pe):
            for n, parts in enumerate(cols):
                if n >= 2:
                    if n_act:
                        pe.wait_ge(act_kept, n_act * (n - 1))
                    pe.wait_ge(dve_kept, n_dve * (n - 1))
                for j in parts:
                    row, kt, _, width = w.plan[j]
                    row -= k0
                    for t in range(TT):
                        for k in range(kt):
                            if t == 0:
                                w.wait_tile(pe, j, k)
                            s = slice(t * P, (t + 1) * P)
                            ins = product(nc, c.ps[:, (n % 2) * TT + t, 0:width],
                                          (aT(0, row + k)[:, s], aT(1, row + k)[:, s]),
                                          (w.part(j, 0, k), w.part(j, 1, k)),
                                          start=(row + k == 0), stop=(row + k == k_tiles - 1))
                        if t == TT - 1:
                            ins.then_inc(c.chunk_used, 1)
                        elif row + kt == k_tiles:
                            ins.then_inc(filled, 1)

        def keep(engine, n, scalar):
            _, _, n0, width = w.plan[cols[n][0]]
            for t in range(TT):
                if by_act(t) != scalar:
                    continue
                if t == TT - 1:
                    engine.wait_ge(c.chunk_used, w.first + cols[n][-1] + 1)
                else:
                    engine.wait_ge(filled, (TT - 1) * n + t + 1)
                bank = c.ps[:, (n % 2) * TT + t, 0:width]
                if scalar:
                    nc.scalar.copy(out(t, n0, width), bank).then_inc(act_kept, 1)
                elif add is None:
                    nc.vector.tensor_copy(out(t, n0, width), bank).then_inc(dve_kept, 1)
                else:
                    nc.vector.tensor_tensor(out(t, n0, width), bank, add(t, n0, width),
                                            ALU.add).then_inc(dve_kept, 1)

        @block.scalar
        def _(act):
            made = 0
            for n, parts in enumerate(cols):
                while made < min(parts[-1] + 2, at):
                    w.make_hi(act, made)
                    made += 1
                keep(act, n, True)

        @block.vector
        def _(dve):
            made = 0
            for n, parts in enumerate(cols):
                while made < min(parts[-1] + 2, at):
                    w.make_lo(dve, made)
                    made += 1
                keep(dve, n, False)


def transpose_tiles(c, name, jobs):
    nc = c.nc

    def bank(i, dst):
        b = c.ps[0:dst.shape[0], i % 8, :]
        return b if len(dst.shape) == 2 else b.rearrange("p (t n) -> p t n", t=TT)

    with c.stage(name, "turned", "act_kept", "dve_kept") as (block, turned, act_kept, dve_kept):
        @block.tensor
        def _(pe):
            for i, (src, m, dst, scale) in enumerate(jobs):
                if i >= 8:
                    if i % 2:
                        pe.wait_ge(dve_kept, (i - 8) // 2 + 1)
                    else:
                        pe.wait_ge(act_kept, (i - 8) // 2 + 1)
                for t in range(TT):
                    ins = nc.tensor.transpose(c.ps[0:m, i % 8, t * P:(t + 1) * P], src(t), c.ident)
                ins.then_inc(turned, 1)

        @block.scalar
        def _(act):
            for i, (src, m, dst, scale) in enumerate(jobs):
                if i % 2 == 0:
                    act.wait_ge(turned, i + 1)
                    nc.scalar.activation(dst, bank(i, dst), ACT.Copy,
                                         scale=scale).then_inc(act_kept, 1)

        @block.vector
        def _(dve):
            for i, (src, m, dst, scale) in enumerate(jobs):
                if i % 2:
                    dve.wait_ge(turned, i + 1)
                    nc.vector.tensor_scalar(dst, bank(i, dst), scale, None,
                                            ALU.mult).then_inc(dve_kept, 1)


def transpose_split(c, name, src, hl, n):
    nc = c.nc
    with c.stage(name, "turned", "his") as (block, turned, his):
        @block.tensor
        def _(pe):
            for k in range(n):
                for t in range(TT):
                    ins = nc.tensor.transpose(c.ps[:, k, t * P:(t + 1) * P], src(t, k), c.ident)
                ins.then_inc(turned, 1)

        @block.scalar
        def _(act):
            for k in range(n):
                act.wait_ge(turned, k + 1)
                nc.scalar.copy(hl[:, 0, k, :], c.banks(k)).then_inc(his, 1)

        @block.vector
        def _(dve):
            for k in range(n):
                dve.wait_ge(his, k + 1)
                nc.vector.tensor_tensor(hl[:, 1, k, :], c.banks(k), hl[:, 0, k, :].bitcast(F32), ALU.subtract)


def relu_squared_gemm(c, name, hl, F, u):
    nc = c.nc
    per_chunk, deep = 4, DM // P // 4
    with ExitStack() as ctx:
        r = ctx.enter_context(nc.sbuf_tensor(name + "r", [P, 4, SEQ], F32))
        y = ctx.enter_context(nc.sbuf_tensor(name + "y", [P, 4, SEQ], F32))
        with c.stage(name, "hi", "lo", "filled", "relu_done", "squared", "his", "los") as (
                block, hi_made, lo_made, filled, relu_done, squared, his, los):
            w = SplitWeights(c, ctx, name, F // per_chunk * deep, hi_made, lo_made)

            @block.sync
            def _(sp):
                w.load(sp)

            @block.tensor
            def _(pe):
                for g in range(F // per_chunk):
                    if g >= 2:
                        pe.wait_ge(squared, per_chunk * (g - 1))
                    for j in range(g * deep, (g + 1) * deep):
                        row, kt = w.plan[j][0:2]
                        for b in range(per_chunk):
                            f = g * per_chunk + b
                            for k in range(kt):
                                if b == 0:
                                    w.wait_tile(pe, j, k)
                                s = slice(b * P, (b + 1) * P)
                                ins = product(nc, c.banks(f % 8), (w.part(j, 0, k)[:, s], w.part(j, 1, k)[:, s]),
                                              (hl[:, 0, row + k, :], hl[:, 1, row + k, :]),
                                              start=(row + k == 0), stop=(row + k == 7))
                            if b == per_chunk - 1:
                                ins.then_inc(c.chunk_used, 1)
                            elif row + kt == 8:
                                ins.then_inc(filled, 1)

            @block.scalar
            def _(act):
                made = 0
                for g in range(F // per_chunk):
                    while made < min((g + 1) * deep + 1, w.n):
                        w.make_hi(act, made)
                        made += 1
                    for b in range(per_chunk):
                        f = g * per_chunk + b
                        if b == per_chunk - 1:
                            act.wait_ge(c.chunk_used, w.first + (g + 1) * deep)
                        else:
                            act.wait_ge(filled, (per_chunk - 1) * g + b + 1)
                        if f >= 4:
                            act.wait_ge(squared, f - 3)
                        nc.scalar.activation(r[:, f % 4, :], c.banks(f % 8), ACT.Relu).then_inc(relu_done, 1)
                        if f:
                            act.wait_ge(squared, f)
                            nc.scalar.copy(u[:, 0, f - 1, :], y[:, (f - 1) % 4, :]).then_inc(his, 1)
                act.wait_ge(squared, F)
                nc.scalar.copy(u[:, 0, F - 1, :], y[:, (F - 1) % 4, :]).then_inc(his, 1)

            @block.vector
            def _(dve):
                def low(f):
                    dve.wait_ge(his, f + 1)
                    nc.vector.tensor_tensor(u[:, 1, f, :], y[:, f % 4, :], u[:, 0, f, :].bitcast(F32),
                                            ALU.subtract).then_inc(los, 1)
                made = 0
                for g in range(F // per_chunk):
                    while made < min((g + 1) * deep + 1, w.n):
                        w.make_lo(dve, made)
                        made += 1
                    for b in range(per_chunk):
                        f = g * per_chunk + b
                        dve.wait_ge(relu_done, f + 1)
                        if f >= 4:
                            dve.wait_ge(los, f - 3)
                        nc.vector.tensor_tensor(y[:, f % 4, :], c.banks(f % 8), r[:, f % 4, :],
                                                ALU.mult).then_inc(squared, 1)
                        if f >= 2:
                            low(f - 2)
                low(F - 2)
                low(F - 1)


def rope(eng, step, x, cos, sin, tmp, heads, half):
    shape = [P, TT, heads, half]
    x1, x2 = x[:, :, :, 0:half], x[:, :, :, half:2 * half]
    cb = cos.unsqueeze(2).broadcast_to(shape)
    sb = sin.unsqueeze(2).broadcast_to(shape)
    n = TT * heads * half
    t1 = tmp[:, 0:n].rearrange("p (t h d) -> p t h d", t=TT, h=heads)
    t2 = tmp[:, n:2 * n].rearrange("p (t h d) -> p t h d", t=TT, h=heads)
    eng.tensor_tensor(t1, x1, sb, ALU.mult)
    step(eng.tensor_tensor(t2, x2, sb, ALU.mult))
    eng.tensor_tensor(x1, x1, cb, ALU.mult)
    step(eng.tensor_tensor(x2, x2, cb, ALU.mult))
    eng.tensor_tensor(x1, x1, t2, ALU.subtract)
    step(eng.tensor_tensor(x2, x2, t1, ALU.add))


def softmax_attention(c, name, units, meanwhile=None):
    nc = c.nc
    U = len(units)
    with ExitStack() as ctx:
        sb = lambda n, s: ctx.enter_context(nc.sbuf_tensor(name + n, s, F32))
        p, pT = sb("p", [P, 3, SEQ]), sb("pT", [P, 2, SEQ])
        negmax, rsum, rinv = sb("negmax", [P, 8]), sb("rsum", [P, 8]), sb("rinv", [P, 8])
        tmp = sb("o", [P, 2, HD])
        with c.stage(name, "scores", "maxed", "probs", "turned", "probsT", "outs", "kept", "step", "pool_step") as (
                block, scores, maxed, probs, turned, probsT, outs, kept, step_sem, pool_step):
            if meanwhile is not None:
                @block.gpsimd
                def _(pool):
                    meanwhile(pool, Steps(pool, pool_step))

            @block.tensor
            def _(pe):
                for i in range(U + 4):
                    if i < U:
                        qT, kT = units[i][0], units[i][1]
                        if i >= 4:
                            pe.wait_ge(probs, i - 3)
                        nc.tensor.matmul(c.ps[:, i % 4, 0:kT.shape[1]], qT, kT,
                                         start=True, stop=True).then_inc(scores, 1)
                    u = i - 2
                    if 0 <= u < U:
                        nk = units[u][1].shape[1]
                        pe.wait_ge(probs, u + 1)
                        if u >= 2:
                            pe.wait_ge(probsT, u - 1)
                        for j in range(nk // P):
                            ins = nc.tensor.transpose(c.ps[:, 4 + u % 2, j * P:(j + 1) * P],
                                                      p[:, u % 3, j * P:(j + 1) * P], c.ident)
                        ins.then_inc(turned, 1)
                    u = i - 4
                    if 0 <= u < U:
                        nb = units[u][1].shape[1] // P
                        pe.wait_ge(probsT, u + 1)
                        if u >= 2:
                            pe.wait_ge(kept, u - 1)
                        for j in range(nb):
                            v = units[u][2](j)
                            ins = nc.tensor.matmul(c.ps[:, 6 + u % 2, 0:v.shape[1]],
                                                   pT[:, u % 2, j * P:(j + 1) * P], v,
                                                   start=(j == 0), stop=(j == nb - 1))
                        ins.then_inc(outs, 1)

            @block.vector
            def _(dve):
                step = Steps(dve, step_sem)
                for i in range(U + 5):
                    if i < U:
                        mask, nk = units[i][3], units[i][1].shape[1]
                        dve.wait_ge(scores, i + 1)
                        nm = mask.shape[1]
                        s = c.ps[:, i % 4, nk - nm:nk]
                        step(nc.vector.tensor_tensor(s, s, mask, ALU.add))
                        nc.vector.tensor_reduce(negmax[:, i % 8:i % 8 + 1], c.ps[:, i % 4, 0:nk],
                                                AX.X, ALU.max, negate=True).then_inc(maxed, 1)
                    u = i - 5
                    if 0 <= u < U:
                        out, gate, add = units[u][4:7]
                        ri = rinv[:, u % 8:u % 8 + 1]
                        dve.wait_ge(outs, u + 1)
                        step(nc.vector.reciprocal(ri, rsum[:, u % 8:u % 8 + 1]))
                        o = c.ps[:, 6 + u % 2, 0:out.shape[1]]
                        if gate is None:
                            nc.vector.tensor_scalar(out, o, ri, None, ALU.mult).then_inc(kept, 1)
                        elif add:
                            step(nc.vector.tensor_scalar(tmp[:, u % 2, :], o, ri, gate, ALU.mult, ALU.mult))
                            nc.vector.tensor_tensor(out, out, tmp[:, u % 2, :], ALU.add).then_inc(kept, 1)
                        else:
                            nc.vector.tensor_scalar(out, o, ri, gate, ALU.mult, ALU.mult).then_inc(kept, 1)

            @block.scalar
            def _(act):
                for i in range(U + 3):
                    if i < U:
                        nk = units[i][1].shape[1]
                        act.wait_ge(maxed, i + 1)
                        if i >= 3:
                            act.wait_ge(turned, i - 2)
                        nc.scalar.activation(p[:, i % 3, 0:nk], c.ps[:, i % 4, 0:nk], ACT.Exp,
                                             bias=negmax[:, i % 8:i % 8 + 1],
                                             accum_out=rsum[:, i % 8:i % 8 + 1]).then_inc(probs, 1)
                    u = i - 2
                    if 0 <= u < U:
                        nk = units[u][1].shape[1]
                        act.wait_ge(turned, u + 1)
                        if u >= 2:
                            act.wait_ge(outs, u - 1)
                        nc.scalar.copy(pT[:, u % 2, 0:nk], c.ps[:, 4 + u % 2, 0:nk]).then_inc(probsT, 1)


def index_scores(c, name, qiT, kiT, weights, score):
    nc = c.nc
    units = [(t, h) for t in range(1, TT) for h in range(IDX_H)]
    with ExitStack() as ctx:
        rel = ctx.enter_context(nc.sbuf_tensor(name + "rel", [P, 3, SEQ], F32))
        with c.stage(name, "dots", "rectified", "summed") as (block, dots, rectified, summed):
            @block.tensor
            def _(pe):
                for u, (t, h) in enumerate(units):
                    b = 32 * (h % 4)
                    if u >= 8:
                        pe.wait_ge(rectified, u - 7)
                    nc.tensor.matmul(c.ps[:, u % 8, 0:(t + 1) * P],
                                     qiT[b:b + 32, h // 4, t * P:(t + 1) * P],
                                     kiT[b:b + 32, 0:(t + 1) * P], start=True, stop=True,
                                     ).then_inc(dots, 1)

            @block.scalar
            def _(act):
                for u, (t, h) in enumerate(units):
                    act.wait_ge(dots, u + 1)
                    if u >= 3:
                        act.wait_ge(summed, u - 2)
                    nc.scalar.activation(rel[:, u % 3, 0:(t + 1) * P], c.ps[:, u % 8, 0:(t + 1) * P],
                                         ACT.Relu).then_inc(rectified, 1)

            @block.vector
            def _(dve):
                for u, (t, h) in enumerate(units):
                    nk = (t + 1) * P
                    w = weights[:, t, h:h + 1]
                    dve.wait_ge(rectified, u + 1)
                    if h == 0:
                        nc.vector.tensor_scalar(score[:, t - 1, 0:nk], rel[:, u % 3, 0:nk], w, None,
                                                ALU.mult).then_inc(summed, 1)
                    else:
                        dve.wait_ge(summed, u)
                        nc.vector.scalar_tensor_tensor(out=score[:, t - 1, 0:nk], in0=rel[:, u % 3, 0:nk],
                                                       scalar=w, in1=score[:, t - 1, 0:nk],
                                                       op0=ALU.mult, op1=ALU.add).then_inc(summed, 1)
                dve.wait_ge(summed, len(units))
                for t in range(1, TT):
                    d = score[:, t - 1, t * P:(t + 1) * P]
                    nc.vector.tensor_tensor(d, d, c.causal, ALU.add).then_inc(summed, 1)
                dve.wait_ge(summed, len(units) + TT - 1)


def top_k_mask(nc, dve, step, score, best):
    for r in range(TOPK // 8):
        for t in range(1, TT):
            ins = nc.vector.max(best[:, t - 1, :], score[:, t - 1, 0:(t + 1) * P])
            if t == TT - 1:
                step(ins)
        for t in range(1, TT):
            s = score[:, t - 1, 0:(t + 1) * P]
            ins = nc.vector.match_replace(s, best[:, t - 1, :], s, TAKEN)
            if t == TT - 1:
                step(ins)
    for t in range(1, TT):
        s = score[:, t - 1, 0:(t + 1) * P]
        ins = nc.vector.tensor_scalar(s, s, TAKEN, MASKED, ALU.not_equal, ALU.mult)
    step(ins)


def retention(c, name, qT, kT, v, decay, out, meanwhile):
    nc = c.nc
    with ExitStack() as ctx:
        inner = ctx.enter_context(nc.sbuf_tensor(name + "inner", [P, 2, TT, SEQ], F32))
        with c.stage(name, "dots", "copied", "inners", "outs", "kept", "step") as (
                block, dots, copied, inners, outs, kept, step_sem):
            @block.tensor
            def _(pe):
                for i in range(RET_H + 1):
                    if i < RET_H:
                        b, pair = HD * (i % 2), i // 2
                        for j in range(TT):
                            if i >= 1:
                                pe.wait_ge(copied, TT * (i - 1) + j + 1)
                            nc.tensor.matmul(c.ps[:, j, 0:SEQ - j * P],
                                             kT[b:b + HD, pair, j * P:(j + 1) * P],
                                             qT[b:b + HD, pair, j * P:SEQ],
                                             start=True, stop=True).then_inc(dots, 1)
                    h = i - 1
                    if h >= 0:
                        pe.wait_ge(inners, TT * (h + 1))
                        if h >= 2:
                            pe.wait_ge(kept, h - 1)
                        for t in range(TT):
                            for j in range(t + 1):
                                ins = nc.tensor.matmul(
                                    c.ps[:, 4 + h % 2, t * HD:(t + 1) * HD],
                                    inner[:, h % 2, j, (t - j) * P:(t - j + 1) * P],
                                    v[:, j, h * HD:(h + 1) * HD], start=(j == 0), stop=(j == t))
                        ins.then_inc(outs, 1)

            @block.vector
            def _(dve):
                meanwhile(dve, Steps(dve, step_sem))

            @block.gpsimd
            def _(pool):
                for h in range(RET_H):
                    for j in range(TT):
                        part = inner[:, h % 2, j, 0:SEQ - j * P]
                        pool.wait_ge(copied, TT * h + j + 1)
                        nc.gpsimd.tensor_tensor(part, part, decay[:, h, 0:SEQ - j * P], ALU.mult).then_inc(inners, 1)

            @block.scalar
            def _(act):
                def keep(h):
                    act.wait_ge(outs, h + 1)
                    nc.scalar.copy(out[:, :, h, :], c.ps[:, 4 + h % 2, 0:TT * HD].rearrange(
                        "p (t d) -> p t d", t=TT)).then_inc(kept, 1)
                for h in range(RET_H):
                    if h >= 2:
                        act.wait_ge(outs, h - 1)
                    for j in range(TT):
                        act.wait_ge(dots, TT * h + j + 1)
                        nc.scalar.copy(inner[:, h % 2, j, 0:SEQ - j * P], c.ps[:, j, 0:SEQ - j * P]).then_inc(copied, 1)
                    if h >= 1:
                        keep(h - 1)
                keep(RET_H - 1)


def head_norm(c, name, src, heads, gain, dst, half, center=False, gate=None, scratch=None):
    nc = c.nc
    shape = [P, TT, heads, HD]
    with ExitStack() as ctx:
        sb = lambda n, s: ctx.enter_context(nc.sbuf_tensor(name + n, s, F32))
        y, sq = scratch or (sb("y", shape)[:], sb("sq", shape)[:])
        mean, ssq = sb("mean", [P, TT, heads]), sb("ssq", [P, TT, heads])[:]
        with c.stage(name, "summed", "power", "rstd", "step", "gated") as (
                block, summed, power, rstd, step_sem, gated):
            @block.gpsimd
            def _(pool):
                pool.wait_ge(summed, 1)
                nc.gpsimd.tensor_scalar(ssq, ssq, 1.0 / HD, EPS, ALU.mult, ALU.add).then_inc(power, 1)
                pool.wait_ge(power, 1)
                nc.gpsimd.tensor_tensor(
                    ssq, ssq, half[:, 0:1].unsqueeze(2).broadcast_to([P, TT, heads]),
                    ALU.pow).then_inc(rstd, 1)

            if gate is not None:
                @block.scalar
                def _(act):
                    nc.scalar.activation(gate, gate, ACT.Silu).then_inc(gated, 1)

            @block.vector
            def _(dve):
                step = Steps(dve, step_sem)
                z = src
                if center:
                    step(nc.vector.tensor_reduce(mean[:], src, AX.X, ALU.add))
                    step(nc.vector.tensor_scalar(mean[:], mean[:], -1.0 / HD, None, ALU.mult))
                    step(nc.vector.tensor_tensor(y, src, mean[:].unsqueeze(3).broadcast_to(shape), ALU.add))
                    z = y
                step(nc.vector.tensor_tensor(sq, z, z, ALU.mult))
                nc.vector.tensor_reduce(ssq, sq, AX.X, ALU.add).then_inc(summed, 1)
                dve.wait_ge(summed, 1)
                for t in range(TT):
                    ins = nc.vector.tensor_tensor(sq[:, t], z[:, t], gain.broadcast_to([P, heads, HD]), ALU.mult)
                step(ins)
                if gate is not None:
                    dve.wait_ge(gated, 1)
                    step(nc.vector.tensor_tensor(sq, sq, gate, ALU.mult))
                dve.wait_ge(rstd, 1)
                nc.vector.tensor_tensor(dst, sq, ssq.unsqueeze(3).broadcast_to(shape), ALU.mult)


def rotation_tables(c, name, pos_i, inv, cos, sin):
    nc = c.nc
    two_pi = 2 * math.pi

    def short(v, bits):
        e = math.floor(math.log2(v)) + 1 - bits
        return math.floor(v / 2.0 ** e) * 2.0 ** e
    c1 = short(two_pi, 8)
    c2 = short(two_pi - c1, 8)
    c3 = short(two_pi - c1 - c2, 8)
    c4 = two_pi - c1 - c2 - c3
    MAGIC, LIM = 1.5 * 2 ** 23, 3.1415925
    with ExitStack() as ctx:
        sb = lambda m, s: ctx.enter_context(nc.sbuf_tensor(name + m, s, F32))
        pos, ang, k, wrap = sb("pos", [P, TT]), sb("ang", [P, TT, HD // 2]), sb("k", [P, TT, HD // 2]), sb("wrap", [P, TT, HD // 2])
        with c.stage(name, "step", "angles") as (block, step_sem, angles):
            @block.vector
            def _(dve):
                step = Steps(dve, step_sem)
                step(nc.vector.tensor_copy(pos[:], pos_i))
                shape = [P, TT, HD // 2]
                step(nc.vector.tensor_tensor(ang[:], pos[:].unsqueeze(2).broadcast_to(shape),
                                             inv.unsqueeze(1).broadcast_to(shape), ALU.mult))
                step(nc.vector.tensor_scalar(k[:], ang[:], 1 / two_pi, None, ALU.mult))
                step(nc.vector.tensor_scalar(k[:], k[:], MAGIC, None, ALU.add))
                step(nc.vector.tensor_scalar(k[:], k[:], MAGIC, None, ALU.subtract))
                for part in (c1, c2, c3, c4):
                    step(nc.vector.scalar_tensor_tensor(out=ang[:], in0=k[:], scalar=-part, in1=ang[:],
                                                        op0=ALU.mult, op1=ALU.add))
                step(nc.vector.tensor_scalar(sin, ang[:], LIM, -LIM, ALU.min, ALU.max))
                step(nc.vector.tensor_scalar(cos, ang[:], math.pi / 2, None, ALU.add))
                step(nc.vector.tensor_scalar(wrap[:], cos, math.pi, -two_pi, ALU.is_gt, ALU.mult))
                step(nc.vector.tensor_tensor(cos, cos, wrap[:], ALU.add))
                nc.vector.tensor_scalar(cos, cos, LIM, -LIM, ALU.min, ALU.max).then_inc(angles, 1)

            @block.scalar
            def _(act):
                act.wait_ge(angles, 1)
                nc.scalar.activation(sin, sin, ACT.Sin)
                nc.scalar.activation(cos, cos, ACT.Sin)


def conv_gemm(c, name, hl, widths, taps, weight, acc, silu_out, times=None):
    nc = c.nc
    deep = DM // P // 4
    sizes = [w // P for w in widths]
    starts = [sum(sizes[:g]) for g in range(len(sizes))]
    blocks = sum(sizes)
    F, u = times or (blocks, None)
    with ExitStack() as ctx, c.stage(name, "hi", "lo", "filled", "convolved", "silus", "step", "timed",
                                     "his") as (block, hi_made, lo_made, filled, convolved, silus, step_sem,
                                                timed, his):
        w = SplitWeights(c, ctx, name, len(sizes) * deep, hi_made, lo_made)

        @block.sync
        def _(sp):
            w.load(sp)

        @block.tensor
        def _(pe):
            for g, size in enumerate(sizes):
                if starts[g] + size > 8:
                    pe.wait_ge(convolved, starts[g] + size - 8)
                for j in range(g * deep, (g + 1) * deep):
                    row, kt = w.plan[j][0:2]
                    for b in range(size):
                        for k in range(kt):
                            if b == 0:
                                w.wait_tile(pe, j, k)
                            s = slice(b * P, (b + 1) * P)
                            ins = product(nc, c.banks((starts[g] + b) % 8),
                                          (w.part(j, 0, k)[:, s], w.part(j, 1, k)[:, s]),
                                          (hl[:, 0, row + k, :], hl[:, 1, row + k, :]),
                                          start=(row + k == 0), stop=(row + k == 7))
                        if b == size - 1:
                            ins.then_inc(c.chunk_used, 1)
                        elif row + kt == 8:
                            ins.then_inc(filled, 1)

        @block.vector
        def _(dve):
            step = Steps(dve, step_sem)

            def low(m):
                if m >= 0:
                    dve.wait_ge(his, m + 1)
                    nc.vector.tensor_tensor(u[:, 1, m, :], silu_out(m), u[:, 0, m, :].bitcast(F32), ALU.subtract)
            made = 0
            for g, size in enumerate(sizes):
                while made < min((g + 1) * deep + 1, w.n):
                    w.make_lo(dve, made)
                    made += 1
                for b in range(size):
                    f = starts[g] + b
                    if b == size - 1:
                        dve.wait_ge(c.chunk_used, w.first + (g + 1) * deep)
                    else:
                        dve.wait_ge(filled, f + 1 - g)
                    cw, a = weight(f), acc[:, f % 4, :]
                    if f >= 4:
                        dve.wait_ge(silus, min(f - 3, F))
                        if f - 4 >= F:
                            dve.wait_ge(timed, f - 3 - F)
                    step(nc.vector.tensor_scalar(a, c.banks(f % 8), cw[:, taps - 1:taps], None, ALU.mult))
                    for i in range(1, taps):
                        ins = nc.vector.scalar_tensor_tensor(
                            out=a[:, i:], in0=c.banks(f % 8)[:, 0:SEQ - i], scalar=cw[:, taps - 1 - i:taps - i],
                            in1=a[:, i:], op0=ALU.mult, op1=ALU.add)
                        if i < taps - 1:
                            step(ins)
                    ins.then_inc(convolved, 1)
                    low(f - F - 2)
            for m in range(max(0, blocks - F - 2), blocks - F):
                low(m)

        @block.scalar
        def _(act):
            def high(m):
                if m >= 0:
                    act.wait_ge(timed, m + 1)
                    nc.scalar.copy(u[:, 0, m, :], silu_out(m)).then_inc(his, 1)
            made = 0
            for g, size in enumerate(sizes):
                while made < min((g + 1) * deep + 1, w.n):
                    w.make_hi(act, made)
                    made += 1
                for f in range(starts[g], starts[g] + size):
                    if f < F:
                        act.wait_ge(convolved, f + 1)
                        nc.scalar.activation(silu_out(f), acc[:, f % 4, :], ACT.Silu).then_inc(silus, 1)
                    else:
                        high(f - F - 1)
            if F < blocks:
                high(blocks - F - 1)

        if F < blocks:
            @block.gpsimd
            def _(pool):
                pool.wait_ge(silus, F)
                for f in range(F, blocks):
                    m = f - F
                    pool.wait_ge(convolved, f + 1)
                    nc.gpsimd.tensor_tensor(silu_out(m), silu_out(m), acc[:, f % 4, :],
                                            ALU.mult).then_inc(timed, 1)


def rows_norm(c, name, src, gain, half, out, gate=None, add=None):
    nc = c.nc
    with ExitStack() as ctx:
        sb = lambda n, s: ctx.enter_context(nc.sbuf_tensor(name + n, s, F32))
        junk, y = sb("junk", [P, DM]), sb("y", [P, 2, DM])
        ssq, rstd = sb("ssq", [P, TT]), sb("rstd", [P, TT])
        with c.stage(name, "squares", "mean", "rstd", "step", "gates") as (
                block, squares, mean, rstd_ready, step_sem, gates):
            @block.scalar
            def _(act):
                for t in range(TT):
                    if t:
                        act.wait_ge(squares, t)
                    nc.scalar.activation(junk[:], src[:, t, :], ACT.Square,
                                         accum_out=ssq[:, t:t + 1]).then_inc(squares, 1)
                    if gate is not None:
                        nc.scalar.activation(gate[:, t, :], gate[:, t, :], ACT.Sigmoid).then_inc(gates, 1)

            @block.gpsimd
            def _(pool):
                for t in range(TT):
                    pool.wait_ge(squares, t + 1)
                    nc.gpsimd.tensor_scalar(ssq[:, t:t + 1], ssq[:, t:t + 1], 1.0 / DM, EPS,
                                            ALU.mult, ALU.add).then_inc(mean, 1)
                    pool.wait_ge(mean, t + 1)
                    nc.gpsimd.tensor_tensor(rstd[:, t:t + 1], ssq[:, t:t + 1], half[:, 0:1],
                                            ALU.pow).then_inc(rstd_ready, 1)

            @block.vector
            def _(dve):
                step = Steps(dve, step_sem)
                for t in range(TT):
                    dve.wait_ge(rstd_ready, t + 1)
                    dst = out[:, t, :] if gate is None and add is None else y[:, t % 2, :]
                    ins = nc.vector.scalar_tensor_tensor(out=dst, in0=src[:, t, :], scalar=rstd[:, t:t + 1],
                                                         in1=gain, op0=ALU.mult, op1=ALU.mult)
                    if gate is not None:
                        step(ins)
                        dve.wait_ge(gates, t + 1)
                        ins = nc.vector.tensor_tensor(dst, dst, gate[:, t, :], ALU.mult)
                    if add is not None:
                        step(ins)
                        step(nc.vector.tensor_tensor(out[:, t, :], dst, add[:, t, :], ALU.add))
                    elif gate is None:
                        step(ins)


def delta_inputs(c, name, qkv, proj, rows, half, g, sq):
    nc = c.nc
    H, W = GDN_H, GDN_H * HD
    shape = [P, TT, H, HD]
    wide = lambda s: s.unsqueeze(3).broadcast_to(shape)
    q4, k4, v4 = (qkv[:, :, i * W:(i + 1) * W].rearrange("p t (h d) -> p t h d", d=HD) for i in range(3))
    with ExitStack() as ctx:
        sb = lambda n, s: ctx.enter_context(nc.sbuf_tensor(name + n, s, F32))
        norm = sb("norm", [P, TT, 2 * H])
        a, e, ea = sb("a", [P, TT, H]), sb("e", [P, TT, H]), sb("ea", [P, H])
        with c.stage(name, "step", "squared", "summed", "power", "rstd", "logits", "gates", "softs", "logged",
                     "beta", "decays", "sums", "shifted", "exps", "act_step") as (
                block, step_sem, squared, summed, power, rstd, logits, gates, softs, logged, beta, decays,
                sums, shifted, exps, act_step):
            @block.scalar
            def _(act):
                nc.scalar.activation(sq, qkv[:, :, 0:2 * W].rearrange("p t (h d) -> p t h d", d=HD),
                                     ACT.Square).then_inc(squared, 1)
                nc.scalar.activation(ea[:], rows["a_log"], ACT.Exp).then_inc(gates, 1)
                act.wait_ge(logits, 1)
                nc.scalar.activation(e[:], a[:], ACT.Abs).then_inc(act_step, 1)
                act.wait_ge(act_step, 1)
                nc.scalar.activation(e[:], e[:], ACT.Exp, scale=-1.0).then_inc(act_step, 1)
                act.wait_ge(act_step, 2)
                nc.scalar.activation(e[:], e[:], ACT.Ln, bias=1.0).then_inc(softs, 1)
                nc.scalar.activation(g["beta"], proj[:, :, B_B:B_B + H], ACT.Exp, scale=-1.0).then_inc(beta, 1)
                act.wait_ge(shifted, 1)
                nc.scalar.activation(g["eg"], g["gcum"], ACT.Exp).then_inc(exps, 1)
                nc.scalar.activation(g["el"], g["el"], ACT.Exp).then_inc(exps, 1)
                nc.scalar.activation(g["etot"], g["etot"], ACT.Exp).then_inc(exps, 1)

            @block.gpsimd
            def _(pool):
                pool.wait_ge(summed, 1)
                nc.gpsimd.tensor_scalar(norm[:], norm[:], EPS, None, ALU.add).then_inc(power, 1)
                pool.wait_ge(power, 1)
                nc.gpsimd.tensor_tensor(norm[:], norm[:],
                                        half[:, 0:1].unsqueeze(2).broadcast_to([P, TT, 2 * H]),
                                        ALU.pow).then_inc(rstd, 1)

            @block.tensor
            def _(pe):
                pe.wait_ge(decays, 1)
                for t in range(TT):
                    nc.tensor.matmul(c.ps[:, 0, t * H:(t + 1) * H], c.cst("upto"), a[:, t, :], start=True, stop=True)
                for t in range(TT):
                    ins = nc.tensor.matmul(c.ps[:, 1, t * H:(t + 1) * H], c.cst("ones"), a[:, t, :],
                                           start=True, stop=True)
                ins.then_inc(sums, 1)

            @block.vector
            def _(dve):
                step = Steps(dve, step_sem)
                rowsH = lambda r: r.unsqueeze(1).broadcast_to([P, TT, H])
                nc.vector.tensor_tensor(a[:], proj[:, :, B_A:B_A + H], rowsH(rows["dt_bias"]),
                                        ALU.add).then_inc(logits, 1)
                dve.wait_ge(squared, 1)
                nc.vector.tensor_reduce(norm[:], sq, AX.X, ALU.add).then_inc(summed, 1)
                dve.wait_ge(softs, 1)
                step(nc.vector.scalar_tensor_tensor(out=a[:], in0=a[:], scalar=0.0, in1=e[:],
                                                    op0=ALU.max, op1=ALU.add))
                dve.wait_ge(gates, 1)
                step(nc.vector.tensor_tensor(a[:], a[:], rowsH(ea[:]), ALU.mult))
                nc.vector.tensor_scalar(a[:], a[:], -1.0, None, ALU.mult).then_inc(decays, 1)
                dve.wait_ge(beta, 1)
                step(nc.vector.tensor_scalar(g["beta"], g["beta"], 1.0, None, ALU.add))
                step(nc.vector.reciprocal(g["beta"], g["beta"]))
                dve.wait_ge(sums, 1)
                view = lambda b: c.ps[:, b, 0:TT * H].rearrange("p (t h) -> p t h", t=TT)
                step(nc.vector.tensor_copy(g["gcum"], view(0)))
                nc.vector.tensor_scalar(g["minus_g"], view(0), -1.0, None, ALU.mult)
                step(nc.vector.tensor_copy(g["etot"], view(1)))
                nc.vector.tensor_tensor(g["el"], view(1), g["gcum"], ALU.subtract).then_inc(shifted, 1)
                dve.wait_ge(rstd, 1)
                step(nc.vector.tensor_scalar(norm[:, :, 0:H], norm[:, :, 0:H], HD ** -0.5, None, ALU.mult))
                nc.vector.tensor_tensor(q4, q4, wide(norm[:, :, 0:H]), ALU.mult)
                step(nc.vector.tensor_tensor(k4, k4, wide(norm[:, :, H:]), ALU.mult))
                as4 = lambda n: g[n].rearrange("p t (h d) -> p t h d", d=HD)
                nc.vector.tensor_tensor(as4("kb"), k4, wide(g["beta"]), ALU.mult)
                step(nc.vector.tensor_tensor(v4, v4, wide(g["beta"]), ALU.mult))
                dve.wait_ge(exps, 3)
                nc.vector.tensor_tensor(as4("qe"), q4, wide(g["eg"]), ALU.mult)
                nc.vector.tensor_tensor(as4("kbe"), as4("kb"), wide(g["eg"]), ALU.mult)
                nc.vector.tensor_tensor(as4("kel"), k4, wide(g["el"]), ALU.mult)


def delta_products(c, name, g, kT, kbT, qT, LT, attnT, dec):
    nc = c.nc
    H = GDN_H
    with c.stage(name, "rows", "masked", "decays", "dots", "kept", "step") as (
            block, rows, masked, decays, dots, kept, step_sem):
        @block.tensor
        def _(pe):
            for h in range(H):
                b, pair = HD * (h % 2), h // 2
                if h >= 2:
                    pe.wait_ge(kept, h - 1)
                for t in range(TT):
                    ins = nc.tensor.matmul(c.ps[:, h % 2, t * P:(t + 1) * P],
                                           g["gcum"][:, t, h:h + 1].broadcast_to([P, P]), c.ident,
                                           start=True, stop=True)
                ins.then_inc(rows, 1)
                for bank, rhs in ((2, kbT), (4, qT)):
                    for t in range(TT):
                        s = slice(t * P, (t + 1) * P)
                        ins = nc.tensor.matmul(c.ps[:, bank + h % 2, s], kT[b:b + HD, pair, s],
                                               rhs[b:b + HD, pair, s], start=True, stop=True)
                ins.then_inc(dots, 1)

        @block.scalar
        def _(act):
            for h in range(H):
                act.wait_ge(masked, h + 1)
                if h >= 2:
                    act.wait_ge(kept, h - 1)
                for t in range(TT):
                    s = slice(t * P, (t + 1) * P)
                    ins = nc.scalar.activation(dec[:, h % 2, s], c.ps[:, h % 2, s], ACT.Exp,
                                               bias=g["minus_g"][:, t, h:h + 1])
                ins.then_inc(decays, 1)

        @block.vector
        def _(dve):
            step = Steps(dve, step_sem)
            four = lambda m: m.unsqueeze(1).broadcast_to([P, TT, P])
            by4 = lambda a: a.rearrange("p (t n) -> p t n", t=TT)
            for h in range(H):
                dve.wait_ge(rows, h + 1)
                r = by4(c.banks(h % 2))
                nc.vector.tensor_tensor(r, r, four(c.cst("inclT")), ALU.add).then_inc(masked, 1)
                dve.wait_ge(decays, h + 1)
                dve.wait_ge(dots, h + 1)
                d = dec[:, h % 2, :]
                step(nc.vector.tensor_tensor(attnT[:, h, :], c.banks(4 + h % 2), d, ALU.mult))
                step(nc.vector.tensor_tensor(LT[:, h, :], c.banks(2 + h % 2), d, ALU.mult))
                L = by4(LT[:, h, :])
                nc.vector.tensor_tensor(L, L, four(c.cst("strict01")), ALU.mult).then_inc(kept, 1)


def unit_lower_inverse(c, name, LT, X, XT, Y, M):
    nc = c.nc
    H = GDN_H
    sizes = [2, 4, 8, 16, 32, 64]
    units = [(s, h) for s in sizes for h in range(H)]
    sl = [slice(t * P, (t + 1) * P) for t in range(TT)]
    with c.stage(name, "cut", "started", "turned", "X_kept", "Ys", "Y_kept", "Zs", "masked", "grown") as (
            block, cut, started, turned, X_kept, Ys, Y_kept, Zs, masked, grown):
        @block.tensor
        def _(pe):
            for h in range(H):
                pe.wait_ge(started, h + 1)
                if h >= 2:
                    pe.wait_ge(X_kept, h - 1)
                for t in range(TT):
                    ins = nc.tensor.transpose(c.ps[:, 6 + h % 2, sl[t]], XT[:, h, sl[t]], c.ident)
                ins.then_inc(turned, 1)
            for i in range(len(units) + 1):
                if i < len(units):
                    s, h = units[i]
                    if i < H:
                        pe.wait_ge(X_kept, i + 1)
                    else:
                        pe.wait_ge(grown, i - H + 1)
                    if i >= 2:
                        pe.wait_ge(Y_kept, i - 1)
                    for t in range(TT):
                        ins = nc.tensor.matmul(c.ps[:, i % 2, sl[t]], LT[:, h, sl[t]], X[:, h, sl[t]],
                                               start=True, stop=True)
                    ins.then_inc(Ys, 1)
                u = i - 1
                if u >= 0:
                    s, h = units[u]
                    pe.wait_ge(Y_kept, u + 1)
                    if u >= 2:
                        pe.wait_ge(masked, u - 1)
                    for t in range(TT):
                        ins = nc.tensor.matmul(c.ps[:, 2 + u % 2, sl[t]], Y[:, u % 2, sl[t]],
                                               XT[:, h, sl[t]], start=True, stop=True)
                    if s != sizes[-1]:
                        for t in range(TT):
                            ins = nc.tensor.matmul(c.ps[:, 4 + u % 2, sl[t]], XT[:, h, sl[t]],
                                                   Y[:, u % 2, sl[t]], start=True, stop=True)
                    ins.then_inc(Zs, 1)

        @block.scalar
        def _(act):
            for h in range(H):
                act.wait_ge(turned, h + 1)
                nc.scalar.copy(X[:, h, :], c.banks(6 + h % 2)).then_inc(X_kept, 1)
            for i in range(len(units)):
                act.wait_ge(Ys, i + 1)
                if i >= 2:
                    act.wait_ge(Zs, i - 1)
                nc.scalar.copy(Y[:, i % 2, :], c.banks(i % 2)).then_inc(Y_kept, 1)

        @block.vector
        def _(dve):
            four = lambda m: m.unsqueeze(1).broadcast_to([P, TT, P])
            by4 = lambda a: a.rearrange("p (t n) -> p t n", t=TT)
            for h in range(H):
                xt = by4(XT[:, h, :])
                nc.vector.tensor_tensor(xt, by4(LT[:, h, :]), four(c.cst("high1")), ALU.mult).then_inc(cut, 1)
                dve.wait_ge(cut, h + 1)
                nc.vector.tensor_tensor(xt, xt, four(c.ident), ALU.add).then_inc(started, 1)
            for i, (s, h) in enumerate(units):
                dve.wait_ge(Zs, i + 1)
                if i >= 2:
                    dve.wait_ge(grown, i - 1)
                ins = nc.vector.tensor_tensor(by4(M[:, i % 2, 0, :]), by4(c.banks(2 + i % 2)),
                                              four(c.cst(f"high{s}")), ALU.mult)
                if s != sizes[-1]:
                    ins = nc.vector.tensor_tensor(by4(M[:, i % 2, 1, :]), by4(c.banks(4 + i % 2)),
                                                  four(c.cst(f"low{s}")), ALU.mult)
                ins.then_inc(masked, 1)

        @block.gpsimd
        def _(pool):
            for i, (s, h) in enumerate(units):
                pool.wait_ge(masked, i + 1)
                if i < H:
                    pool.wait_ge(X_kept, i + 1)
                ins = nc.gpsimd.tensor_tensor(XT[:, h, :], XT[:, h, :], M[:, i % 2, 0, :], ALU.add)
                if s != sizes[-1]:
                    ins = nc.gpsimd.tensor_tensor(X[:, h, :], X[:, h, :], M[:, i % 2, 1, :], ALU.add)
                ins.then_inc(grown, 1)


def delta_scan(c, name, g, XT, attnT, qeT, vb, minus_wT, S, vn, out):
    nc = c.nc
    H = GDN_H
    half_of = lambda h: (HD * (h % 2), h // 2)
    heads_of = lambda bank: c.ps[:, bank, 0:H // 2 * HD].rearrange("p (a d) -> p a d", d=HD)
    with ExitStack() as ctx:
        sb = lambda n, s: ctx.enter_context(nc.sbuf_tensor(name + n, s, F32))
        et = sb("et", [P, TT, H // 2])
        with c.stage(name, "ws", "ws_kept", "news", "news_kept", "outs", "outs_kept", "grown", "states", "step") as (
                block, ws, ws_kept, news, news_kept, outs, outs_kept, grown, states, step_sem):
            @block.tensor
            def _(pe):
                for pair in range(H // 2):
                    for h in (2 * pair, 2 * pair + 1):
                        b = HD * (h % 2)
                        for t in range(TT):
                            s = slice(t * P, (t + 1) * P)
                            ins = nc.tensor.matmul(c.ps[b:b + HD, pair, s], g["kbe"][:, t, h * HD:(h + 1) * HD],
                                                   XT[:, h, s], start=True, stop=True)
                    ins.then_inc(ws, 1)
                pe.wait_ge(ws_kept, H // 2)
                for t in range(TT):
                    s = slice(t * P, (t + 1) * P)
                    if t:
                        pe.wait_ge(states, t)
                    for h in range(H):
                        b, pair = half_of(h)
                        col, own = slice(h * HD, (h + 1) * HD), slice(pair * HD, (pair + 1) * HD)
                        new = c.ps[:, (3, 6)[h % 2], own]
                        ins = nc.tensor.matmul(new, XT[:, h, s], vb[:, t, col],
                                               start=True, stop=(t == 0))
                        if t:
                            ins = nc.tensor.matmul(new, minus_wT[b:b + HD, pair, s],
                                                   S[b:b + HD, pair, :], start=False, stop=True)
                    ins.then_inc(news, 1)
                    if t:
                        pe.wait_ge(outs_kept, t)
                    pe.wait_ge(news_kept, t + 1)
                    for h in range(H):
                        b, pair = half_of(h)
                        if t < TT - 1:
                            ins = nc.tensor.matmul(c.ps[b:b + HD, 5, pair * HD:(pair + 1) * HD],
                                                   g["kel"][:, t, h * HD:(h + 1) * HD], vn[:, t % 2, h, :],
                                                   start=True, stop=True)
                    if t < TT - 1:
                        ins.then_inc(grown, 1)
                    for h in range(H):
                        b, pair = half_of(h)
                        o = c.ps[:, (4, 7)[h % 2], pair * HD:(pair + 1) * HD]
                        ins = nc.tensor.matmul(o, attnT[:, h, s], vn[:, t % 2, h, :],
                                               start=True, stop=(t == 0))
                        if t:
                            ins = nc.tensor.matmul(o, qeT[b:b + HD, pair, s],
                                                   S[b:b + HD, pair, :], start=False, stop=True)
                    ins.then_inc(outs, 1)

            @block.scalar
            def _(act):
                for pair in range(H // 2):
                    act.wait_ge(ws, pair + 1)
                    nc.scalar.mul(minus_wT[:, pair, :], c.banks(pair), -1.0).then_inc(ws_kept, 1)
                for t in range(TT):
                    act.wait_ge(outs, t + 1)
                    for b in range(2):
                        ins = nc.scalar.copy(out[:, t, b:H:2, :], heads_of((4, 7)[b]))
                    ins.then_inc(outs_kept, 1)

            @block.vector
            def _(dve):
                step = Steps(dve, step_sem)
                by_pair = g["etot"].rearrange("p t (a b) -> p t a b", b=2)
                for b in range(2):
                    r = slice(b * HD, (b + 1) * HD)
                    ins = nc.vector.tensor_copy(et[r], by_pair[r, :, :, b])
                step(ins)
                for t in range(TT):
                    dve.wait_ge(news, t + 1)
                    for b in range(2):
                        ins = nc.vector.tensor_copy(vn[:, t % 2, b:H:2, :], heads_of((3, 6)[b]))
                    ins.then_inc(news_kept, 1)
                    if t < TT - 1:
                        dve.wait_ge(grown, t + 1)
                        if t:
                            dve.wait_ge(outs, t + 1)
                        for pair in range(H // 2):
                            new = c.ps[:, 5, pair * HD:(pair + 1) * HD]
                            if t == 0:
                                ins = nc.vector.tensor_copy(S[:, pair, :], new)
                            else:
                                ins = nc.vector.scalar_tensor_tensor(
                                    out=S[:, pair, :], in0=S[:, pair, :], scalar=et[:, t, pair:pair + 1],
                                    in1=new, op0=ALU.mult, op1=ALU.add)
                        ins.then_inc(states, 1)
                        dve.wait_ge(states, t + 1)


def compressed_attention(c, name, qT, blocks, pe_tiles, w2, gates, out, kcT, vcmp, kv2T):
    nc = c.nc
    H, G, N = NSA_H, NSA_G, N_CMP
    first = c.used
    c.used += 2
    seen, neg = c.cst("cmp_seen"), c.cst("cmp_neg")
    with ExitStack() as ctx:
        sb = lambda n, s: ctx.enter_context(nc.sbuf_tensor(name + n, s, F32))
        hid = sb("hid", [P, 2, G * N])
        s, st = sb("s", [P, H, TT, N]), sb("st", [P, H, TT])
        pT = sb("pT", [N, H, SEQ])
        with c.stage(name, "summed", "hidden", "silus", "small", "small_kept", "scores", "step", "centred", "exps",
                     "masked", "turned", "turned_kept", "outs") as (
                block, summed, hidden, silus, small, small_kept, scores, step_sem, centred, exps, masked,
                turned, turned_kept, outs):
            @block.sync
            def _(sp):
                c.load_up_to(sp, first + 2 + RING, first, lambda sp, i: sp.wait_ge(c.chunk_used, i + 1))

            @block.tensor
            def _(pe):
                for i in range(2):
                    c.wait_chunk(pe, first + i)
                    wt = c.chunk(first + i)
                    pe.wait_ge(summed, i + 1)
                    for m in range(CMP_LEN // 2):
                        ins = nc.tensor.matmul(c.ps[:, i, 0:G * N], wt[:, m, :], blocks[:, i, m, :],
                                               start=(m == 0), stop=(m == CMP_LEN // 2 - 1))
                    ins.then_inc(c.chunk_used, 1)
                pe.wait_ge(silus, 2)
                for b in (0, HD):
                    nc.tensor.matmul(c.ps[b:b + HD, 2, 0:G * N], w2[:, 0:HD], hid[:, 0, :], start=True, stop=True)
                for gr in range(G):
                    ins = nc.tensor.matmul(c.ps[0:N, 3, gr * HD:(gr + 1) * HD], hid[:, 1, gr * N:(gr + 1) * N],
                                           w2[:, HD:2 * HD], start=True, stop=True)
                ins.then_inc(small, 1)
                pe.wait_ge(small_kept, 1)
                for h in range(H):
                    b, gr = HD * (h % 2), h // NSA_R
                    for t in range(TT):
                        ins = nc.tensor.matmul(c.ps[:, h, t * N:(t + 1) * N],
                                               qT[b:b + HD, h // 2, t * P:(t + 1) * P],
                                               kcT[b:b + HD, gr * N:(gr + 1) * N], start=True, stop=True)
                ins.then_inc(scores, 1)
                pe.wait_ge(masked, 1)
                for h in range(H):
                    for t in range(TT):
                        ins = nc.tensor.transpose(c.ps[0:N, h, t * P:(t + 1) * P], s[:, h, t, :], c.ident)
                    ins.then_inc(turned, 1)
                for h in range(H):
                    pe.wait_ge(turned_kept, h + 1)
                    for t in range(TT):
                        ins = nc.tensor.matmul(c.ps[:, h, t * HD:(t + 1) * HD], pT[:, h, t * P:(t + 1) * P],
                                               vcmp[0:N, h // NSA_R, :], start=True, stop=True)
                    ins.then_inc(outs, 1)

            @block.scalar
            def _(act):
                for i in range(2):
                    act.wait_ge(c.chunk_used, first + i + 1)
                    nc.scalar.activation(hid[:, i, :], c.ps[:, i, 0:G * N], ACT.Silu).then_inc(silus, 1)
                act.wait_ge(centred, 1)
                nc.scalar.activation(s[:], s[:], ACT.Exp).then_inc(exps, 1)
                for h in range(H):
                    act.wait_ge(turned, h + 1)
                    nc.scalar.copy(pT[:, h, :], c.ps[0:N, h, :]).then_inc(turned_kept, 1)

            @block.vector
            def _(dve):
                step = Steps(dve, step_sem)
                for i in range(2):
                    for gr in range(G):
                        by16 = kv2T[:, i, gr, :].rearrange("p (i r) -> p r i", r=16)
                        for b in range(2):
                            r = slice(b * HD, (b + 1) * HD)
                            for o in range(2):
                                ins = nc.vector.tensor_tensor(
                                    blocks[r, i, 8 * o:8 * o + 8, gr * N:(gr + 1) * N],
                                    by16[r, b:16:2, o:o + N],
                                    pe_tiles[r, 16 * i + 8 * o:16 * i + 8 * o + 8].unsqueeze(2
                                             ).broadcast_to([HD, 8, N]), ALU.add)
                    ins.then_inc(summed, 1)
                dve.wait_ge(small, 1)
                nc.vector.tensor_copy(kcT, c.ps[:, 2, 0:G * N])
                nc.vector.tensor_copy(vcmp[0:N], c.ps[0:N, 3, 0:G * HD].rearrange("p (g d) -> p g d", g=G)
                                      ).then_inc(small_kept, 1)
                dve.wait_ge(scores, 1)
                flat = s[:].rearrange("p h t n -> p h (t n)")
                step(nc.vector.tensor_tensor(flat, c.ps[:, 0:H, 0:TT * N],
                                             neg.unsqueeze(1).broadcast_to([P, H, TT * N]), ALU.add))
                step(nc.vector.tensor_reduce(st[:], s[:], AX.X, ALU.max))
                nc.vector.tensor_tensor(s[:], s[:], st[:].unsqueeze(3).broadcast_to([P, H, TT, N]),
                                        ALU.subtract).then_inc(centred, 1)
                dve.wait_ge(exps, 1)
                nc.vector.tensor_tensor(flat, flat, seen.unsqueeze(1).broadcast_to([P, H, TT * N]),
                                        ALU.mult).then_inc(masked, 1)
                dve.wait_ge(masked, 1)
                step(nc.vector.tensor_reduce(st[:], s[:], AX.X, ALU.add))
                step(nc.vector.tensor_scalar(st[:], st[:], 1e-30, None, ALU.max))
                step(nc.vector.reciprocal(st[:], st[:]))
                step(nc.vector.tensor_tensor(st[:], st[:], gates[:, :, 0:H].rearrange("p t h -> p h t"), ALU.mult))
                for h in range(H):
                    dve.wait_ge(outs, h + 1)
                    nc.vector.tensor_tensor(out[:, :, h, :], c.ps[:, h, 0:TT * HD].rearrange("p (t d) -> p t d", t=TT),
                                            st[:, h, :].unsqueeze(2).broadcast_to([P, TT, HD]), ALU.mult)


def stick_breaking(c, name, qT, kT, v, out):
    nc = c.nc
    units = [(h, j) for h in range(SB_H) for j in reversed(range(TT))]
    U = len(units)
    with ExitStack() as ctx:
        sb = lambda n, s: ctx.enter_context(nc.sbuf_tensor(name + n, s, F32))
        e = sb("e", [P, 2, SEQ])
        sp_, A = sb("sp", [P, 2, TT, SEQ]), sb("A", [P, 2, 2, SEQ])
        aT = sb("aT", [P, 2, TT, SEQ])
        with c.stage(name, "dots", "masked", "act_step", "logs", "softs", "suffix", "sums", "hidden", "weights",
                     "outs", "kept") as (block, dots, masked, act_step, logs, softs, suffix, sums, hidden,
                                         weights, outs, kept):
            @block.tensor
            def _(pe):
                for i in range(U + 8):
                    if i < U:
                        h, j = units[i]
                        b, pair = HD * (h % 2), h // 2
                        if i >= 3:
                            pe.wait_ge(softs, i - 2)
                        nc.tensor.matmul(c.ps[:, i % 3, 0:SEQ - j * P], kT[b:b + HD, pair, j * P:(j + 1) * P],
                                         qT[b:b + HD, pair, j * P:], start=True, stop=True).then_inc(dots, 1)
                    u = i - 2
                    if 0 <= u < U:
                        h, j = units[u]
                        b, pair = HD * (h % 2), h // 2
                        bank = c.ps[:, 3 + u % 3, 0:SEQ - j * P]
                        if u >= 3:
                            pe.wait_ge(weights, u - 2)
                        pe.wait_ge(softs, u + 1)
                        nc.tensor.matmul(bank, kT[b:b + HD, pair, j * P:(j + 1) * P], qT[b:b + HD, pair, j * P:],
                                         start=True, stop=False)
                        ins = nc.tensor.matmul(bank, c.cst("minus_from"), sp_[:, h % 2, j, 0:SEQ - j * P],
                                               start=False, stop=(j == TT - 1))
                        if j < TT - 1:
                            if j == TT - 2:
                                later = sp_[:, h % 2, TT - 1, 0:P]
                            else:
                                pe.wait_ge(suffix, 2 * h + (TT - 2 - j))
                                later = A[:, h % 2, j, 0:SEQ - (j + 1) * P]
                            ins = nc.tensor.matmul(bank[:, P:], c.cst("minus_ones"), later, start=False, stop=True)
                        ins.then_inc(sums, 1)
                    u = i - 5
                    if 0 <= u < U and units[u][1] == 0:
                        h = units[u][0]
                        pe.wait_ge(weights, u + 1)
                        if h >= 2:
                            pe.wait_ge(kept, h - 1)
                        for t in range(TT):
                            for j in range(t + 1):
                                ins = nc.tensor.matmul(c.ps[:, 6 + h % 2, t * HD:(t + 1) * HD],
                                                       aT[:, h % 2, j, (t - j) * P:(t - j + 1) * P],
                                                       v[:, j, h * HD:(h + 1) * HD], start=(j == 0), stop=(j == t))
                        ins.then_inc(outs, 1)

            @block.scalar
            def _(act):
                for i in range(U + 3):
                    if i < U:
                        h, j = units[i]
                        w = SEQ - j * P
                        z, ei = c.ps[:, i % 3, 0:w], e[:, i % 2, 0:w]
                        act.wait_ge(masked, i + 1)
                        if i >= 2:
                            act.wait_ge(softs, i - 1)
                        nc.scalar.activation(ei, z, ACT.Abs).then_inc(act_step, 1)
                        act.wait_ge(act_step, 2 * i + 1)
                        nc.scalar.activation(ei, ei, ACT.Exp, scale=-1.0).then_inc(act_step, 1)
                        act.wait_ge(act_step, 2 * i + 2)
                        nc.scalar.activation(ei, ei, ACT.Ln, bias=1.0).then_inc(logs, 1)
                    u = i - 2
                    if 0 <= u < U:
                        h, j = units[u]
                        w = SEQ - j * P
                        act.wait_ge(hidden, u + 1)
                        if h >= 2:
                            act.wait_ge(outs, h - 1)
                        nc.scalar.activation(aT[:, h % 2, j, 0:w], c.ps[:, 3 + u % 3, 0:w], ACT.Exp).then_inc(weights, 1)

            @block.vector
            def _(dve):
                for i in range(U + 3):
                    if i < U:
                        dve.wait_ge(dots, i + 1)
                        d = c.ps[:, i % 3, 0:P]
                        nc.vector.tensor_tensor(d, d, c.cst("strictT"), ALU.add).then_inc(masked, 1)
                    u = i - 1
                    if 0 <= u < U:
                        h, j = units[u]
                        w = SEQ - j * P
                        dve.wait_ge(logs, u + 1)
                        if h >= 2:
                            dve.wait_ge(weights, TT * (h - 1))
                        nc.vector.scalar_tensor_tensor(out=sp_[:, h % 2, j, 0:w], in0=c.ps[:, u % 3, 0:w],
                                                       scalar=0.0, in1=e[:, u % 2, 0:w], op0=ALU.max,
                                                       op1=ALU.add).then_inc(softs, 1)
                    u = i - 2
                    if 0 <= u < U:
                        dve.wait_ge(sums, u + 1)
                        d = c.ps[:, 3 + u % 3, 0:P]
                        nc.vector.tensor_tensor(d, d, c.cst("strictT"), ALU.add).then_inc(hidden, 1)
                    if 0 <= i - 3 < U and units[i - 3][1] == 1 and units[i - 3][0] >= 1:
                        h = units[i - 3][0] - 1
                        dve.wait_ge(outs, h + 1)
                        nc.vector.tensor_copy(out[:, :, h, :], c.ps[:, 6 + h % 2, 0:TT * HD].rearrange(
                            "p (t d) -> p t d", t=TT)).then_inc(kept, 1)
                h = SB_H - 1
                dve.wait_ge(outs, h + 1)
                nc.vector.tensor_copy(out[:, :, h, :], c.ps[:, 6 + h % 2, 0:TT * HD].rearrange(
                    "p (t d) -> p t d", t=TT)).then_inc(kept, 1)

            @block.gpsimd
            def _(pool):
                for h in range(SB_H):
                    if h >= 2:
                        pool.wait_ge(sums, TT * (h - 1))
                    pool.wait_ge(softs, TT * h + 2)
                    nc.gpsimd.tensor_copy(A[:, h % 2, 1, 0:P], sp_[:, h % 2, 2, 0:P])
                    nc.gpsimd.tensor_tensor(A[:, h % 2, 1, P:2 * P], sp_[:, h % 2, 2, P:2 * P],
                                            sp_[:, h % 2, 3, 0:P], ALU.add).then_inc(suffix, 1)
                    pool.wait_ge(softs, TT * h + 3)
                    pool.wait_ge(suffix, 2 * h + 1)
                    nc.gpsimd.tensor_copy(A[:, h % 2, 0, 0:P], sp_[:, h % 2, 1, 0:P])
                    nc.gpsimd.tensor_tensor(A[:, h % 2, 0, P:3 * P], sp_[:, h % 2, 1, P:3 * P],
                                            A[:, h % 2, 1, 0:2 * P], ALU.add).then_inc(suffix, 1)


def shape_constants():
    lane = np.arange(P)
    cols = {"ident": np.eye(P), "causal": np.where(lane[None, :] <= lane[:, None], 0.0, MASKED),
            "half": np.full((P, 64), -0.5)}
    common = list(cols)
    pos = np.arange(SEQ, dtype=np.float32)
    for dim in (32, 64):
        inv = (np.float32(10000.0) ** (-np.arange(0, dim, 2, dtype=np.float32) / dim)).astype(np.float32)
        ang = (pos[:, None] * inv[None, :]).astype(np.float32).astype(np.float64)
        for f, fn in (("cos", np.cos), ("sin", np.sin)):
            cols[f"{f}{dim}"] = fn(ang).reshape(TT, P, dim // 2).transpose(1, 0, 2).reshape(P, -1)
    gamma = np.log1p(-np.exp2(-5.0 - np.arange(RET_H)))
    rel = np.arange(SEQ)[None, None, :] - lane[:, None, None]
    decay = np.where(rel >= 0, np.exp(np.maximum(rel, 0) * gamma[None, :, None]), 0.0)
    cols["decay"] = decay.reshape(P, -1)
    first = list(cols)
    cols["strictT"] = np.where(lane[:, None] < lane[None, :], 0.0, MASKED)
    cols["inclT"] = np.where(lane[:, None] <= lane[None, :], 0.0, MASKED)
    cols["strict01"] = (lane[:, None] < lane[None, :]) * 1.0
    cols["upto"] = (lane[:, None] <= lane[None, :]) * 1.0
    cols["minus_from"] = (lane[:, None] >= lane[None, :]) * -1.0
    cols["ones"] = np.ones((P, P))
    cols["minus_ones"] = -np.ones((P, P))
    for s in (1, 2, 4, 8, 16, 32, 64):
        same = (lane[:, None] // (2 * s)) == (lane[None, :] // (2 * s))
        low = same & ((lane[:, None] // s) % 2 == 1) & ((lane[None, :] // s) % 2 == 0)
        cols[f"low{s}"] = -1.0 * low
        cols[f"high{s}"] = -1.0 * low.T
    t = np.arange(SEQ).reshape(TT, P).T[:, :, None]
    seen = np.arange(N_CMP)[None, None, :] * CMP_STRIDE + CMP_LEN - 1 <= t
    cols["cmp_seen"] = (seen * 1.0).reshape(P, -1)
    cols["cmp_neg"] = np.where(seen, 0.0, MASKED).reshape(P, -1)
    inv = (np.float32(10000.0) ** (-np.arange(HD // 2, dtype=np.float32) / (HD // 2))).astype(np.float32)
    cols["inv"] = np.broadcast_to(inv, (P, HD // 2))
    second = common + [k for k in cols if k not in first]

    def pack(names):
        where, at = {}, 0
        for k in names:
            where[k] = (at, at + cols[k].shape[1])
            at += cols[k].shape[1]
        return np.concatenate([cols[k] for k in names], axis=1).astype(np.float32), where
    return pack(first), pack(second)


def first_block(c, d, cst, layers=DEPTH):
    nc = c.nc
    x = c.x
    split_tile = lambda ctx: ctx.enter_context(nc.sbuf_tensor(f"a_hl{c.n_stage}", [P, 2, 8, SEQ], F32R, side="right"))
    of = lambda hl: (lambda half, k: hl[:, half, k, :])
    cos32 = cst("cos32").rearrange("p (t d) -> p t d", t=TT)
    sin32 = cst("sin32").rearrange("p (t d) -> p t d", t=TT)
    cos64 = cst("cos64").rearrange("p (t d) -> p t d", t=TT)
    sin64 = cst("sin64").rearrange("p (t d) -> p t d", t=TT)
    decay = cst("decay").rearrange("p (h u) -> p h u", h=RET_H)
    half = cst("half")
    with nc.Fori(0, layers) as l, ExitStack() as ctx:
        sb = lambda n, s: ctx.enter_context(nc.sbuf_tensor("a_" + n, s, F32))
        c.start_layer(A_WEIGHTS, d, "a_", l)
        gains = sb("gains", [P, 24])
        g_ret = sb("g_ret", [P, RET_H * RET_D])
        with c.stage("a_gains", "arrived") as (block, arrived):
            @block.sync
            def _(sp):
                layer = lambda n: d[n][bass.ds(l, 1)].rearrange("a p n -> p (a n)")
                sp.dma_start(gains[:], layer("a_gains")).then_inc(arrived, 16)
                sp.dma_start(g_ret[:], d["g_ret"][bass.ds(l, 1), :].broadcast_to([P, RET_H * RET_D])
                             ).then_inc(arrived, 16)
                c.load_up_to(sp, RING)
                sp.wait_ge(arrived, 32)

        with ExitStack() as ctx2, ExitStack() as right:
            hl = split_tile(right)
            norm_transpose(c, "mixnorm", x, [(0, DM)], gains[:, 0:8], half, hl)
            sb2 = lambda n, s: ctx2.enter_context(nc.sbuf_tensor("a_" + n, s, F32))
            mix = sb2("mix", [P, TT, DM])
            proj = sb2("proj", [P, TT, A_IN])
            gemm_tokens(c, "win", of(hl), 8, 6, lambda t, n, w: proj[:, t, n:n + w])
            norm_transpose(c, "ranknorm", proj, [(A_CQ, Q_RANK), (A_CKV, KV_RANK)], gains[:, 8:16], half, hl)
            heads = lambda a, n, dim: proj[:, :, a:a + n * dim].rearrange("p t (h d) -> p t h d", d=dim)
            with ExitStack() as ctx3:
                sb3 = lambda n, s: ctx3.enter_context(nc.sbuf_tensor("a_" + n, s, F32))
                q = sb3("q", [P, TT, MLA_H * MLA_QK])
                gemm_tokens(c, "uq", of(hl), Q_RANK // P, 2, lambda t, n, w: q[:, t, n:n + w])
                kv = proj[:, :, 0:DM]
                gemm_tokens(c, "ukv", lambda half, k: hl[:, half, Q_RANK // P + k, :], KV_RANK // P, 2,
                            lambda t, n, w: kv[:, t, n:n + w])
                right.close()
                kcat = sb3("kcat", [P, TT, MLA_H, MLA_QK])
                kT, qT = sb3("kT", [P, MLA_H, SEQ]), sb3("qT", [P, MLA_H, SEQ])
                q4 = q[:].rearrange("p t (h d) -> p t h d", d=MLA_QK)
                kv4 = kv.rearrange("p t (h d) -> p t h d", d=MLA_NOPE + MLA_V)
                flat = kT[:].rearrange("p h s -> p (h s)")
                rt1 = flat[:, 0:4 * SEQ]
                with c.stage("mla_rope", "step") as (block, step_sem):
                    @block.vector
                    def _(dve):
                        step = Steps(dve, step_sem)
                        kr = heads(A_KR, 1, MLA_ROPE)
                        rope(nc.vector, step, kr, cos32, sin32, rt1, 1, 16)
                        for t in range(TT):
                            nc.vector.tensor_copy(kcat[:, t, :, MLA_NOPE:], kr[:, t].broadcast_to([P, MLA_H, MLA_ROPE]))
                        rope(nc.vector, step, q4[:, :, :, MLA_NOPE:], cos32, sin32, rt1, MLA_H, 16)

                    @block.scalar
                    def _(act):
                        for t in range(TT):
                            nc.scalar.copy(kcat[:, t, :, 0:MLA_NOPE], kv4[:, t, :, 0:MLA_NOPE])
                mla_scale = MLA_QK ** -0.5
                jobs = [(lambda t, h=h: kcat[:, t, h, :], MLA_QK, kT[0:MLA_QK, h, :], 1.0) for h in range(MLA_H)]
                jobs += [(lambda t, h=h: q4[:, t, h, :], MLA_QK, qT[0:MLA_QK, h, :], mla_scale) for h in range(MLA_H)]
                transpose_tiles(c, "mlaT", jobs)

                def other_ropes(pool, step):
                    tmp = kcat[:].rearrange("p t h d -> p (t h d)")
                    for a, n, dim, cs, sn in ((A_AQ, DSA_H + 1, DSA_D, cos64, sin64),
                                              (A_QI, IDX_H + 1, IDX_D, cos32, sin32),
                                              (A_RQ, RET_H, RET_D, cos64, sin64), (A_RK, RET_H, RET_D, cos64, sin64)):
                        rope(nc.gpsimd, step, heads(a, n, dim), cs, sn, tmp, n, dim // 2)
                softmax_attention(c, "mla", [
                    (qT[0:MLA_QK, h, t * P:(t + 1) * P], kT[0:MLA_QK, h, 0:(t + 1) * P],
                     lambda j, h=h: kv4[:, j, h, MLA_NOPE:], c.causal,
                     mix[:, t, h * MLA_V:(h + 1) * MLA_V], None, False)
                    for h in range(MLA_H) for t in range(TT)], other_ropes)
            with ExitStack() as ctx3:
                sb3 = lambda n, s: ctx3.enter_context(nc.sbuf_tensor("a_" + n, s, F32))
                kdup, kidup = sb3("kdup", [P, TT, 2 * DSA_D]), sb3("kidup", [P, TT, 4 * IDX_D])
                qbT, kbT = sb3("qbT", [P, 2, SEQ]), sb3("kbT", [P, SEQ])
                qiT, kiT = sb3("qiT", [P, 2, SEQ]), sb3("kiT", [P, SEQ])
                rqT, rkT = sb3("rqT", [P, 2, SEQ]), sb3("rkT", [P, 2, SEQ])
                score, best = sb3("score", [P, TT - 1, SEQ]), sb3("best", [P, TT - 1, 8])
                with c.stage("a_dup") as (block,):
                    @block.scalar
                    def _(act):
                        for i in range(2):
                            nc.scalar.copy(kdup[:, :, i * DSA_D:(i + 1) * DSA_D], proj[:, :, A_AK:A_AK + DSA_D])
                        for i in range(4):
                            nc.scalar.copy(kidup[:, :, i * IDX_D:(i + 1) * IDX_D], proj[:, :, A_KI:A_KI + IDX_D])
                        nc.scalar.mul(proj[:, :, A_WI:A_WI + IDX_H], proj[:, :, A_WI:A_WI + IDX_H],
                                      IDX_H ** -0.5 * IDX_D ** -0.5)
                tile_of = lambda a: (lambda t: proj[:, t, a:a + P])
                jobs = [(tile_of(A_AQ + i * P), P, qbT[:, i, :], DSA_D ** -0.5) for i in range(2)]
                jobs += [(tile_of(A_QI + i * P), P, qiT[:, i, :], 1.0) for i in range(2)]
                jobs += [(tile_of(A_RQ + i * P), P, rqT[:, i, :], RET_D ** -0.5) for i in range(2)]
                jobs += [(tile_of(A_RK + i * P), P, rkT[:, i, :], 1.0) for i in range(2)]
                jobs += [(lambda t: kdup[:, t, :], P, kbT[:], 1.0), (lambda t: kidup[:, t, :], P, kiT[:], 1.0)]
                transpose_tiles(c, "mixT", jobs)
                index_scores(c, "idx", qiT, kiT, proj[:, :, A_WI:A_WI + IDX_H], score)
                o_b = MLA_H * MLA_V
                o_c = o_b + DSA_H * DSA_D
                out4 = mix[:, :, o_c:o_c + RET_H * RET_D].rearrange("p t (h d) -> p t h d", d=RET_D)
                retention(c, "ret", rqT, rkT, proj[:, :, A_RV:A_RV + RET_H * RET_D], decay, out4,
                          lambda dve, step: top_k_mask(nc, dve, step, score, best))
                units = []
                for h in range(DSA_H):
                    b = DSA_D * (h % 2)
                    for t in range(TT):
                        mask = c.causal if t == 0 else score[:, t - 1, 0:(t + 1) * P]
                        units.append((qbT[b:b + DSA_D, h // 2, t * P:(t + 1) * P],
                                      kbT[b:b + DSA_D, 0:(t + 1) * P],
                                      lambda j: proj[:, j, A_AV:A_AV + DSA_D], mask,
                                      mix[:, t, o_b + h * DSA_D:o_b + (h + 1) * DSA_D], None, False))
                softmax_attention(c, "dsa", units)
                head_norm(c, "retnorm", out4, RET_H, g_ret[:].rearrange("p (h d) -> p h d", d=RET_D), out4,
                          half, center=True, gate=heads(A_RG, RET_H, RET_D))
            hl = split_tile(right)
            transpose_split(c, "mixcat", lambda t, k: mix[:, t, k * P:(k + 1) * P], hl, 8)
            resid = lambda t, n, w: x[:, t, n:n + w]
            gemm_tokens(c, "wout", of(hl), 8, 2, resid, add=resid)
        with ExitStack() as right:
            hl = split_tile(right)
            norm_transpose(c, "mlpnorm", x, [(0, DM)], gains[:, 16:24], half, hl)
            F = A_HALF // P
            with nc.sbuf_tensor("a_u", [P, 2, F, SEQ], F32R) as u:
                for i in range(2):
                    relu_squared_gemm(c, f"ff1_{i}_", hl, F, u)
                    gemm_tokens(c, f"ff2_{i}_", of(u), F, 2, resid, add=resid, k0=i * F)
        c.end_layer()


def spans(sizes):
    at, where = 0, {}
    for n, w in sizes:
        where[n] = (at, at + w)
        at += w
    return where, at


B_COLS, B_NCOLS = spans([("ln_mix", 8), ("ln_ffn", 8), ("ln_ple", 8), ("gdn_conv", 9 * GDN_CONV),
                         ("ffn_conv", 2 * D_FF2 // P * FFN_CONV), ("pe", 2 * CMP_LEN // 2), ("w2", 2 * HD)])
B_ROWS, B_NROWS = spans([("a_log", GDN_H), ("dt_bias", GDN_H), ("gdn_norm", HD), ("nsa_norm", HD),
                         ("sb_norm", HD), ("ple_norm", DM)])


def second_block(c, d, cst, pos_i, layers=DEPTH):
    nc = c.nc
    x = c.x
    split_tile = lambda ctx: ctx.enter_context(nc.sbuf_tensor(f"b_hl{c.n_stage}", [P, 2, 8, SEQ], F32R, side="right"))
    of = lambda hl: (lambda half, k: hl[:, half, k, :])
    c.cst = cst
    half = cst("half")
    with ExitStack() as ctx0:
        cosb = ctx0.enter_context(nc.sbuf_tensor("b_cos", [P, TT, HD // 2], F32))
        sinb = ctx0.enter_context(nc.sbuf_tensor("b_sin", [P, TT, HD // 2], F32))
        cos, sin = cosb[:], sinb[:]
        rotation_tables(c, "angles", pos_i, cst("inv"), cos, sin)
        with nc.Fori(0, layers) as l, ExitStack() as ctx:
            sb = lambda n, s: ctx.enter_context(nc.sbuf_tensor("b_" + n, s, F32))
            c.start_layer(B_WEIGHTS, d, "b_", l)
            cols_t, rows_t = sb("cols", [P, B_NCOLS]), sb("rows", [P, B_NROWS])
            cols = {n: cols_t[:, a:b] for n, (a, b) in B_COLS.items()}
            rows = {n: rows_t[:, a:b] for n, (a, b) in B_ROWS.items()}
            with c.stage("b_gains", "arrived") as (block, arrived):
                @block.sync
                def _(sp):
                    sp.dma_start(cols_t[:], d["b_cols"][bass.ds(l, 1)].rearrange("a p n -> p (a n)")
                                 ).then_inc(arrived, 16)
                    sp.dma_start(rows_t[:], d["b_rows"][bass.ds(l, 1), :].broadcast_to([P, B_NROWS])
                                 ).then_inc(arrived, 16)
                    c.load_up_to(sp, RING)
                    sp.wait_ge(arrived, 32)
            resid = lambda t, n, w: x[:, t, n:n + w]
            with ExitStack() as left, ExitStack() as right:
                mix = left.enter_context(nc.sbuf_tensor("b_mix", [P, TT, DM], F32))
                hl = split_tile(right)
                norm_transpose(c, "bmixnorm", x, [(0, DM)], cols["ln_mix"], half, hl)
                attentions(c, of(hl), mix, cos, sin, cols, rows, half)
                gated_delta(c, hl, right, mix, cols, rows, half)
                hl = split_tile(right)
                transpose_split(c, "bmixcat", lambda t, k: mix[:, t, k * P:(k + 1) * P], hl, 8)
                gemm_tokens(c, "bwout", of(hl), 8, 2, resid, add=resid)
            with ExitStack() as right:
                hl = split_tile(right)
                norm_transpose(c, "ffnnorm", x, [(0, DM)], cols["ln_ffn"], half, hl)
                F = B_HALF // P
                with ExitStack() as left:
                    sb1 = lambda n, s, dt=F32: left.enter_context(nc.sbuf_tensor("b_" + n, s, dt))
                    u = sb1("u", [P, 2, F, SEQ], F32R)
                    acc, silus = sb1("acc", [P, 4, SEQ]), sb1("silus", [P, F, SEQ])
                    widths = [ch[3] for ch in chunks_of(DM, B_HALF, deep=8)] * 2
                    for i in range(2):
                        def tap(f, i=i):
                            f = (f if f < F else f + F) + i * F
                            return cols["ffn_conv"][:, f * FFN_CONV:(f + 1) * FFN_CONV]
                        conv_gemm(c, f"up{i}_", hl, widths, FFN_CONV, tap, acc, lambda f: silus[:, f, :], (F, u))
                        gemm_tokens(c, f"down{i}_", of(u), F, 2, resid, add=resid, k0=i * F)
            with ExitStack() as ctx1, ExitStack() as right:
                sb1 = lambda n, s, dt=F32: ctx1.enter_context(nc.sbuf_tensor("b_" + n, s, dt))
                hl = split_tile(right)
                gate, ple, p_sb = sb1("gate", [P, TT, DM]), sb1("ple", [P, TT, DM]), sb1("p", [P, TT, D_PLE])
                norm_transpose(c, "plenorm", x, [(0, DM)], cols["ln_ple"], half, hl,
                               load=(p_sb[:], d["p"][bass.ds(l, 1)].rearrange("a p t n -> p (a t) n")))
                pT = sb1("pT", [P, 2, D_PLE // P, SEQ], F32R)
                gemm_tokens(c, "plegate", of(hl), 8, 2, lambda t, n, w: gate[:, t, n:n + w])
                transpose_split(c, "pleT", lambda t, k: p_sb[:, t, k * P:(k + 1) * P], pT, D_PLE // P)
                gemm_tokens(c, "ple", of(pT), D_PLE // P, 2, lambda t, n, w: ple[:, t, n:n + w])
                rows_norm(c, "plerows", ple[:], rows["ple_norm"], half, x, gate=gate, add=x)
            c.end_layer()


def attentions(c, h_of, mix, cos, sin, cols, rows, half):
    nc = c.nc
    o_n = GDN_H * HD
    o_s = o_n + NSA_H * HD
    with ExitStack() as ctx:
        sb = lambda n, s: ctx.enter_context(nc.sbuf_tensor("b_" + n, s, F32))
        proj = sb("proj", [P, TT, B_ATT])
        gemm_tokens(c, "watt", h_of, 8, 4, lambda t, n, w: proj[:, t, n:n + w])
        heads = lambda a, n: proj[:, :, a:a + n * HD].rearrange("p t (h d) -> p t h d", d=HD)
        gates = proj[:, :, B_GATE:B_GATE + 3 * NSA_H]
        with ExitStack() as ctx1:
            sb1 = lambda n, s: ctx1.enter_context(nc.sbuf_tensor("b_" + n, s, F32))
            qT, ksT, kwT = sb1("qT", [P, NSA_H // 2, SEQ]), sb1("ksT", [P, NSA_G, SEQ]), sb1("kwT", [P, NSA_G, SEQ])
            kv2T = sb1("kv2T", [P, 2, NSA_G, SEQ])
            with ExitStack() as ctx2:
                dup = ctx2.enter_context(nc.sbuf_tensor("b_dup", [P, 2, NSA_G, TT, 2, HD], F32))
                dupc = ctx2.enter_context(nc.sbuf_tensor("b_dupc", [P, 2, NSA_G, TT, 2, HD], F32))
                rt1 = ctx2.enter_context(nc.sbuf_tensor("b_rt1", [P, 2 * TT * NSA_H * HD // 2], F32))
                rt2 = ctx2.enter_context(nc.sbuf_tensor("b_rt2", [P, 2 * TT * NSA_G * HD // 2], F32))
                with c.stage("nsarope", "step", "pool_step") as (block, step_sem, pool_step):
                    @block.vector
                    def _(dve):
                        step = Steps(dve, step_sem)
                        rope(nc.vector, step, heads(B_NQ, NSA_H), cos, sin, rt1, NSA_H, HD // 2)

                    @block.gpsimd
                    def _(pool):
                        step = Steps(pool, pool_step)
                        for a in (B_KC, B_KS, B_KW):
                            rope(nc.gpsimd, step, heads(a, NSA_G), cos, sin, rt2, NSA_G, HD // 2)

                    @block.scalar
                    def _(act):
                        nc.scalar.activation(gates, gates, ACT.Sigmoid)
                        act.wait_ge(pool_step, 9)
                        for i, a in ((0, B_KS), (1, B_KW)):
                            for g in range(NSA_G):
                                for r in range(2):
                                    nc.scalar.copy(dup[:, i, g, :, r, :], proj[:, :, a + g * HD:a + (g + 1) * HD])
                        for i, a in ((0, B_KC), (1, B_VC)):
                            for g in range(NSA_G):
                                for r in range(2):
                                    nc.scalar.copy(dupc[:, i, g, :, r, :], proj[:, :, a + g * HD:a + (g + 1) * HD])
                both = lambda s: (lambda t: s[:, t].rearrange("p r d -> p (r d)"))
                jobs = [(lambda t, i=i: proj[:, t, B_NQ + i * P:B_NQ + (i + 1) * P], P, qT[:, i, :], HD ** -0.5)
                        for i in range(NSA_H // 2)]
                jobs += [(both(dup[:, 0, g]), P, ksT[:, g, :], 1.0) for g in range(NSA_G)]
                jobs += [(both(dup[:, 1, g]), P, kwT[:, g, :], 1.0) for g in range(NSA_G)]
                jobs += [(both(dupc[:, i, g]), P, kv2T[:, i, g, :], 1.0) for i in range(2) for g in range(NSA_G)]
                transpose_tiles(c, "nsaT", jobs)
            out4 = mix[:, :, o_n:o_n + NSA_H * HD].rearrange("p t (h d) -> p t h d", d=HD)
            with ExitStack() as ctx2:
                sb2 = lambda n, s: ctx2.enter_context(nc.sbuf_tensor("b_" + n, s, F32))
                kcT, vcmp = sb2("kcT", [P, NSA_G * N_CMP]), sb2("vcmp", [32, NSA_G, HD])
                blocks = sb2("blocks", [P, 2, CMP_LEN // 2, NSA_G * N_CMP])
                compressed_attention(c, "cmp", qT, blocks, cols["pe"], cols["w2"], gates, out4, kcT[:], vcmp, kv2T)
            units = []
            for i, (kT, v) in enumerate(((ksT, B_VS), (kwT, B_VW))):
                for h in range(NSA_H):
                    b, g = HD * (h % 2), h // NSA_R
                    for t in range(TT):
                        units.append((qT[b:b + HD, h // 2, t * P:(t + 1) * P], kT[b:b + HD, g, 0:(t + 1) * P],
                                      lambda j, v=v, g=g: proj[:, j, v + g * HD:v + (g + 1) * HD], c.causal,
                                      out4[:, t, h, :], gates[:, t, (i + 1) * NSA_H + h:(i + 1) * NSA_H + h + 1], True))
            softmax_attention(c, "nsa", units)
            head_norm(c, "nsanorm", out4, NSA_H, rows["nsa_norm"].unsqueeze(1), out4, half)
        with ExitStack() as ctx1:
            sb1 = lambda n, s: ctx1.enter_context(nc.sbuf_tensor("b_" + n, s, F32))
            sqT, skT = sb1("sqT", [P, SB_H // 2, SEQ]), sb1("skT", [P, SB_H // 2, SEQ])
            jobs = [(lambda t, a=a, i=i: proj[:, t, a + i * P:a + (i + 1) * P], P, dst[:, i, :], s)
                    for a, dst, s in ((B_SQ, sqT, HD ** -0.5), (B_SK, skT, 1.0)) for i in range(SB_H // 2)]
            transpose_tiles(c, "sbT", jobs)
            out4 = mix[:, :, o_s:o_s + SB_H * HD].rearrange("p t (h d) -> p t h d", d=HD)
            stick_breaking(c, "stick", sqT, skT, proj[:, :, B_SV:B_SV + SB_H * HD], out4)
            head_norm(c, "sbnorm", out4, SB_H, rows["sb_norm"].unsqueeze(1), out4, half)


def gated_delta(c, hl, right, mix, cols, rows, half):
    nc = c.nc
    W = GDN_H * HD
    with ExitStack() as ctx:
        sb = lambda n, s: ctx.enter_context(nc.sbuf_tensor("b_" + n, s, F32))
        zab, qkv = sb("zab", [P, TT, B_ZAB]), sb("qkv", [P, TT, GDN_QKV])
        n_conv = GDN_QKV // P
        with ExitStack() as ctx1:
            sT = ctx1.enter_context(nc.sbuf_tensor("b_sT", [P, n_conv, SEQ], F32))
            acc = ctx1.enter_context(nc.sbuf_tensor("b_acc0", [P, 4, SEQ], F32))
            conv_gemm(c, "conv", hl, [ch[3] for ch in chunks_of(DM, GDN_QKV, deep=8)], GDN_CONV,
                      lambda f: cols["gdn_conv"][:, f * GDN_CONV:(f + 1) * GDN_CONV], acc, lambda f: sT[:, f, :])
            gemm_tokens(c, "zab", lambda i, k: hl[:, i, k, :], 8, 1, lambda t, n, w: zab[:, t, n:n + w])
            right.close()
            transpose_tiles(c, "convT", [(lambda t, f=f: sT[:, f, t * P:(t + 1) * P], P,
                                          qkv[:, :, f * P:(f + 1) * P], 1.0) for f in range(n_conv)])
        work, hT = sb("work", [P, 24, SEQ]), sb("work2", [P, 8, SEQ])
        g = {n: sb("g_" + n, [P, TT, GDN_H])[:] for n in ("beta", "gcum", "minus_g", "eg", "el", "etot")}
        g["kbe"], g["kel"] = sb("kbe", [P, TT, W])[:], sb("kel", [P, TT, W])[:]
        qeT = sb("qeT", [P, GDN_H // 2, SEQ])
        token_major = lambda i: work[:, i:i + 3, :].rearrange("p a s -> p (a s)").rearrange("p (t n) -> p t n", t=TT)
        g["kb"], g["qe"] = token_major(12), token_major(15)
        sq = work[:, 0:6, :].rearrange("p a s -> p (a s)").rearrange("p (t h d) -> p t h d", t=TT, d=HD)
        delta_inputs(c, "dinputs", qkv, zab, rows, half, g, sq)
        kT, kbT, dec, qT = hT[:, 0:3, :], hT[:, 3:6, :], hT[:, 6:8, :], work[:, 18:21, :]
        jobs = []
        for src, dst in ((qkv[:, :, W:2 * W], kT), (g["kb"], kbT), (qkv[:, :, 0:W], qT), (g["qe"], qeT)):
            jobs += [(lambda t, s=src, i=i: s[:, t, i * P:(i + 1) * P], P, dst[:, i, :], 1.0) for i in range(W // P)]
        transpose_tiles(c, "deltaT", jobs)
        LT, attnT, X, XT = (work[:, 6 * i:6 * i + 6, :] for i in range(4))
        delta_products(c, "dprod", g, kT, kbT, qT, LT, attnT, dec)
        unit_lower_inverse(c, "dinv", LT, X, XT, hT[:, 0:2, :], hT[:, 2:6, :].rearrange("p (a b) s -> p a b s", a=2))
        out4 = mix[:, :, 0:W].rearrange("p t (h d) -> p t h d", d=HD)
        S = hT[:, 5, 0:W // 2].rearrange("p (a d) -> p a d", d=HD)
        vn = hT[:, 3:5, :].rearrange("p a s -> p (a s)")[:, 0:2 * W].rearrange("p (a h d) -> p a h d", a=2, d=HD)
        delta_scan(c, "dscan", g, XT, attnT, qeT, qkv[:, :, 2 * W:3 * W], hT[:, 0:3, :], S, vn, out4)
        z4 = zab[:, :, 0:W].rearrange("p t (h d) -> p t h d", d=HD)
        view = lambda i: work[:, i:i + 3, :].rearrange("p a s -> p (a s)").rearrange("p (t h d) -> p t h d", t=TT, d=HD)
        head_norm(c, "gdnnorm", out4, GDN_H, rows["gdn_norm"].unsqueeze(1), out4, half, gate=z4,
                  scratch=(view(0), view(3)))


def program(nc, d, out):
    ctx = ExitStack()
    (_, where_a), (_, where_b) = shape_constants()
    width = lambda w: max(b for _, b in w.values())
    with ctx:
        c = Core(nc, ctx)
        pos = c.sb("pos_i", [P, TT], I32)
        for which, where in (("a", where_a), ("b", where_b)):
            with nc.sbuf_tensor("const_" + which, [P, width(where)], F32) as ct:
                cst = lambda n, ct=ct, where=where: ct[:, where[n][0]:where[n][1]]
                c.ident, c.causal, c.cst = cst("ident"), cst("causal"), cst
                with c.stage("load_" + which, "arrived") as (block, arrived):
                    @block.sync
                    def _(sp):
                        sp.dma_start(ct[:], d["const_" + which]).then_inc(arrived, 16)
                        if which == "a":
                            sp.dma_start(c.x[:], d["x"]).then_inc(arrived, 16)
                        else:
                            sp.dma_start(pos[:], d["positions"]).then_inc(arrived, 16)
                        sp.wait_ge(arrived, 32)
                if which == "a":
                    first_block(c, d, cst)
                else:
                    second_block(c, d, cst, pos[:])
                gain = c.ring[:, 0, 0:DM]
                with c.stage("final_" + which, "arrived") as (block, arrived):
                    @block.sync
                    def _(sp):
                        i = "ab".index(which)
                        sp.dma_start(gain, d["finals"][i:i + 1, :].broadcast_to([P, DM])).then_inc(arrived, 16)
                        sp.wait_ge(arrived, 16)
                rows_norm(c, "final" + which, c.x, gain, cst("half"), c.x)
        with c.stage("store", "stored") as (block, stored):
            @block.sync
            def _(sp):
                sp.dma_start(out.rearrange("(t p) n -> p t n", p=P), c.x[:]).then_inc(stored, 16)
                sp.wait_ge(stored, 16)


def laid_out(inputs):
    a = {k: np.asarray(v) for k, v in inputs.items()}
    tokens = lambda v: np.ascontiguousarray(v.reshape(TT, P, -1).transpose(1, 0, 2))

    def chunks(w, plan):
        w = w.reshape(w.shape[0], -1, P, w.shape[-1])
        return np.concatenate([w[:, k:k + kt, :, n:n + cols].transpose(0, 2, 1, 3).reshape(w.shape[0], P, -1)
                               for k, kt, n, cols in plan], axis=2)

    def column(v):
        return v.reshape(DEPTH, -1, P).transpose(0, 2, 1)

    def taps(v):
        return v.reshape(DEPTH, v.shape[1], -1, P).transpose(0, 3, 2, 1).reshape(DEPTH, P, -1)

    (const_a, _), (const_b, _) = shape_constants()
    d = {"const_a": const_a, "const_b": const_b, "x": tokens(a["x"][0])}
    for name in dict.fromkeys(n for n, _ in A_WEIGHTS):
        d["a_" + name] = chunks(a[name], plan_of(A_WEIGHTS, name))
    d["a_gains"] = np.concatenate([column(a[n]) for n in ("g_mix", "g_q", "g_kv", "g_mlp")], axis=2)
    d["g_ret"] = a["g_ret"]
    w_in = a["w_in_2"]
    sizes = [GDN_H * HD] * 4 + [GDN_H] * 2
    z0 = 3 * GDN_H * HD
    att0 = sum(sizes)
    parts = {"w_in_conv": w_in[:, :, 0:z0], "w_in_zab": w_in[:, :, z0:att0], "w_in_att": w_in[:, :, att0:],
             "cmp_k_w1": a["nsa_cmp_k_w1_2"], "cmp_v_w1": a["nsa_cmp_v_w1_2"], "w_out": a["w_out_2"],
             "w_up": a["w_up_2"], "w_down": a["w_down_2"], "w_ple_gate": a["w_ple_gate_2"], "w_ple": a["w_ple_2"]}
    for name in dict.fromkeys(n for n, _ in B_WEIGHTS):
        d["b_" + name] = chunks(parts[name], plan_of(B_WEIGHTS, name))
    pair = lambda v: v.reshape(DEPTH, CMP_LEN // 2, P).transpose(0, 2, 1)
    d["b_cols"] = np.concatenate(
        [column(a["ln_mix_2"]), column(a["ln_ffn_2"]), column(a["ln_ple_2"]), taps(a["gdn_conv_2"]),
         taps(a["ffn_conv_2"]), pair(a["nsa_pe_k_2"]), pair(a["nsa_pe_v_2"]), a["nsa_cmp_k_w2_2"],
         a["nsa_cmp_v_w2_2"]], axis=2)
    d["b_rows"] = np.concatenate([a[n] for n in ("gdn_a_log_2", "gdn_dt_bias_2", "gdn_norm_2", "nsa_norm_2",
                                                 "sb_norm_2", "ple_norm_2")], axis=1)
    d["p"] = a["p_2"][:, 0].reshape(DEPTH, TT, P, D_PLE).transpose(0, 2, 1, 3)
    d["positions"] = a["positions_2"][0].reshape(TT, P).T
    d["finals"] = np.stack([a["g_final"], a["ln_final_2"]])
    return {k: np.ascontiguousarray(v) for k, v in d.items()}


def kernel(**inputs):
    import concourse.bacc as bacc
    from concourse.bass_utils import run_bass_kernel_spmd

    nc = bacc.Bacc("TRN2", target_bir_lowering=False, num_devices=1)
    arrays = laid_out(inputs)
    d = {k: nc.dram_tensor(f"in_{k}", v.shape, mybir.dt.from_np(v.dtype), kind="ExternalInput").ap()
         for k, v in arrays.items()}
    out = nc.dram_tensor("out_h", [SEQ, DM], F32, kind="ExternalOutput").ap()
    program(nc, d, out)
    r = run_bass_kernel_spmd(nc, [{f"in_{k}": v for k, v in arrays.items()}], core_ids=[0])
    return r.results[0]["out_h"].reshape(1, SEQ, DM)
```
